# Optimizing a Trainium2 kernel written in Bass

```python
import jax, jax.numpy as jnp
from jax import lax
import numpy as np

D_MODEL = 1024
BATCH = 1
SEQ = 512
DEPTH = 1

HEAD_DIM = 64
MIX_WIDTH = D_MODEL
NSA_WIDTH = MIX_WIDTH // 2
DSA_WIDTH = MIX_WIDTH - NSA_WIDTH
NSA_HEADS = NSA_WIDTH // HEAD_DIM
NSA_KV_HEADS = 2
NSA_KV_W = NSA_KV_HEADS * HEAD_DIM
DSA_HEADS = DSA_WIDTH // HEAD_DIM
DSA_KV_HEADS = 2
DSA_KV_W = DSA_KV_HEADS * HEAD_DIM
IDX_HEADS = 4
IDX_DIM = 64
CMP_BLOCK = 32
CMP_STRIDE = 16
CMP_HIDDEN = 256
SEL_BLOCK = 64
SEL_TOPN = 16
WINDOW = 512
DSA_TOPK_MAX = 256
ROPE_THETA = 10000.0
EPS = 1e-6
Q_BLOCK = 128
SEL_Q_BLOCK = 64
NEG = -1e30
FORCE = 1e6
ATTN_SCALE = HEAD_DIM ** -0.5

IN_WIDTHS = (NSA_WIDTH, NSA_KV_W, NSA_KV_W, NSA_KV_W, NSA_KV_W, NSA_KV_W, NSA_KV_W,
             3 * NSA_HEADS, NSA_WIDTH,
             DSA_WIDTH, DSA_KV_W, DSA_KV_W, IDX_HEADS * IDX_DIM, IDX_DIM, IDX_HEADS, DSA_WIDTH)
IN_COLS = sum(IN_WIDTHS)


def rms_norm(x, gain):
    xf = x.astype(jnp.float32)
    y = xf * lax.rsqrt(jnp.mean(xf * xf, axis=-1, keepdims=True) + EPS)
    return (y * gain.astype(jnp.float32)).astype(x.dtype)

def rope(x, pos):
    half = x.shape[-1] // 2
    inv_freq = ROPE_THETA ** (-jnp.arange(half, dtype=jnp.float32) / half)
    ang = pos[:, None] * inv_freq[None, :]
    cos = jnp.cos(ang)[:, None, :]
    sin = jnp.sin(ang)[:, None, :]
    xf = x.astype(jnp.float32)
    x1, x2 = xf[..., :half], xf[..., half:]
    return jnp.concatenate([x1 * cos - x2 * sin, x2 * cos + x1 * sin], axis=-1).astype(x.dtype)

def masked_softmax(s, mask):
    s = jnp.where(mask, s.astype(jnp.float32), NEG)
    p = jax.nn.softmax(s, axis=-1)
    return jnp.where(mask, p, 0.0)

def split_columns(proj, widths):
    offsets = np.cumsum(np.array(widths))[:-1]
    return jnp.split(proj, [int(o) for o in offsets], axis=-1)

def compress(k_raw, pe, w1, b1, w2):
    B, S, G, Dh = k_raw.shape
    n_cmp = (S - CMP_BLOCK) // CMP_STRIDE + 1
    idx = jnp.arange(n_cmp)[:, None] * CMP_STRIDE + jnp.arange(CMP_BLOCK)[None, :]
    blocks = k_raw[:, idx] + pe[None, None, :, None, :]
    flat = blocks.transpose(0, 1, 3, 2, 4).reshape(B, n_cmp, G, CMP_BLOCK * Dh)
    hid = jax.nn.silu(flat @ w1 + b1)
    return hid @ w2

def compressed_branch(q, kc, vc):
    S = q.shape[1]
    n_cmp = kc.shape[1]
    cmp_end = jnp.arange(n_cmp) * CMP_STRIDE + CMP_BLOCK - 1
    t = jnp.arange(S)
    s = jnp.einsum('bsgrd,bcgd->bgrsc', q, kc) * ATTN_SCALE
    p = masked_softmax(s, cmp_end[None, :] <= t[:, None])
    o = jnp.einsum('bgrsc,bcgd->bsgrd', p.astype(vc.dtype), vc)
    return o, p

def selection_indices(p_cmp):
    S, n_cmp = p_cmp.shape[-2], p_cmp.shape[-1]
    n_sel = S // SEL_BLOCK
    c_start = jnp.arange(n_cmp) * CMP_STRIDE
    j = jnp.arange(n_sel)
    j_start = j * SEL_BLOCK
    overlap = jnp.clip(jnp.minimum(c_start[:, None] + CMP_BLOCK, j_start[None, :] + SEL_BLOCK)
                       - jnp.maximum(c_start[:, None], j_start[None, :]), 0, None)
    overlap = overlap.astype(jnp.float32) / CMP_BLOCK
    imp = jnp.einsum('bgrsc,cj->bgsj', p_cmp, overlap)
    t = jnp.arange(S)
    cur = t // SEL_BLOCK
    forced = (j[None, :] == 0) | (j[None, :] == cur[:, None]) | (j[None, :] == cur[:, None] - 1)
    imp = jnp.where(forced, FORCE, imp)
    imp = jnp.where(j_start[None, :] <= t[:, None], imp, NEG)
    _, idx = lax.top_k(imp, min(SEL_TOPN, n_sel))
    return idx.transpose(0, 2, 1, 3)

def selected_branch(q, ks, vs, sel_idx):
    B, S, G, R, Dh = q.shape
    n_sel = S // SEL_BLOCK
    n = sel_idx.shape[-1]
    k_blocks = ks.reshape(B, n_sel, SEL_BLOCK, G, Dh).transpose(0, 3, 1, 2, 4)
    v_blocks = vs.reshape(B, n_sel, SEL_BLOCK, G, Dh).transpose(0, 3, 1, 2, 4)
    b_ix = jnp.arange(B)[:, None, None, None]
    g_ix = jnp.arange(G)[None, None, :, None]

    def one_block(i):
        t0 = i * SEL_Q_BLOCK
        q_b = lax.dynamic_slice_in_dim(q, t0, SEL_Q_BLOCK, axis=1)
        idx_b = lax.dynamic_slice_in_dim(sel_idx, t0, SEL_Q_BLOCK, axis=1)
        k_sel = k_blocks[b_ix, g_ix, idx_b].reshape(B, SEL_Q_BLOCK, G, n * SEL_BLOCK, Dh)
        v_sel = v_blocks[b_ix, g_ix, idx_b].reshape(B, SEL_Q_BLOCK, G, n * SEL_BLOCK, Dh)
        kpos = (idx_b[..., None] * SEL_BLOCK + jnp.arange(SEL_BLOCK)).reshape(B, SEL_Q_BLOCK, G, n * SEL_BLOCK)
        t = t0 + jnp.arange(SEL_Q_BLOCK)
        mask = (kpos <= t[None, :, None, None])[:, :, :, None, :]
        s = jnp.einsum('btgrd,btgkd->btgrk', q_b, k_sel) * ATTN_SCALE
        p = masked_softmax(s, mask)
        return jnp.einsum('btgrk,btgkd->btgrd', p.astype(v_sel.dtype), v_sel)

    out = lax.map(one_block, jnp.arange(S // SEL_Q_BLOCK))
    return out.transpose(1, 0, 2, 3, 4, 5).reshape(B, S, G, R, Dh)

def window_branch(q, kw, vw):
    B, S, G, R, Dh = q.shape
    pad = ((0, 0), (WINDOW, 0), (0, 0), (0, 0))
    kp = jnp.pad(kw, pad)
    vp = jnp.pad(vw, pad)
    span = Q_BLOCK + WINDOW

    def one_block(i):
        t0 = i * Q_BLOCK
        q_b = lax.dynamic_slice_in_dim(q, t0, Q_BLOCK, axis=1)
        k_b = lax.dynamic_slice_in_dim(kp, t0, span, axis=1)
        v_b = lax.dynamic_slice_in_dim(vp, t0, span, axis=1)
        kpos = t0 - WINDOW + jnp.arange(span)
        t = t0 + jnp.arange(Q_BLOCK)
        diff = t[:, None] - kpos[None, :]
        mask = (diff >= 0) & (diff < WINDOW) & (kpos[None, :] >= 0)
        s = jnp.einsum('btgrd,bkgd->bgrtk', q_b, k_b) * ATTN_SCALE
        p = masked_softmax(s, mask)
        return jnp.einsum('bgrtk,bkgd->btgrd', p.astype(v_b.dtype), v_b)

    out = lax.map(one_block, jnp.arange(S // Q_BLOCK))
    return out.transpose(1, 0, 2, 3, 4, 5).reshape(B, S, G, R, Dh)

def dsa_branch(q, k, v, qi, ki, wi):
    B, S, G, R, Dh = q.shape
    topk = min(DSA_TOPK_MAX, S // 4)
    b_ix = jnp.arange(B)[:, None, None]
    key_pos = jnp.arange(S)
    wi = wi * (IDX_HEADS ** -0.5)

    def one_block(i):
        t0 = i * Q_BLOCK
        q_b = lax.dynamic_slice_in_dim(q, t0, Q_BLOCK, axis=1)
        qi_b = lax.dynamic_slice_in_dim(qi, t0, Q_BLOCK, axis=1)
        wi_b = lax.dynamic_slice_in_dim(wi, t0, Q_BLOCK, axis=1)
        t = t0 + jnp.arange(Q_BLOCK)
        logits = jnp.einsum('bthd,bsd->bths', qi_b, ki) * (IDX_DIM ** -0.5)
        score = jnp.einsum('bths,bth->bts', jax.nn.relu(logits), wi_b).astype(jnp.float32)
        score = jnp.where(key_pos[None, None, :] <= t[None, :, None], score, NEG)
        _, idx = lax.top_k(score, topk)
        k_sel = k[b_ix, idx]
        v_sel = v[b_ix, idx]
        mask = (idx <= t[None, :, None])[:, :, None, None, :]
        s = jnp.einsum('btgrd,btkgd->btgrk', q_b, k_sel) * ATTN_SCALE
        p = masked_softmax(s, mask)
        return jnp.einsum('btgrk,btkgd->btgrd', p.astype(v_sel.dtype), v_sel)

    out = lax.map(one_block, jnp.arange(S // Q_BLOCK))
    return out.transpose(1, 0, 2, 3, 4, 5).reshape(B, S, G, R, Dh)

def hybrid_layer(x, norm_gain, w_in, nsa_q_gain, nsa_kc_gain, nsa_ks_gain, nsa_kw_gain,
                 cmp_pe_k, cmp_k_w1, cmp_k_b1, cmp_k_w2, cmp_pe_v, cmp_v_w1, cmp_v_b1, cmp_v_w2,
                 dsa_q_gain, dsa_k_gain, w_out):
    B, S, _ = x.shape
    pos = jnp.arange(S, dtype=jnp.float32)
    h = rms_norm(x, norm_gain)
    proj = jnp.einsum('bsd,dc->bsc', h, w_in)
    (q_n, kc, vc, ks, vs, kw, vw, gate_logits, z_n,
     q_d, k_d, v_d, qi, ki, wi, z_d) = split_columns(proj, IN_WIDTHS)

    def heads(a, n):
        return a.reshape(B, S, n, HEAD_DIM)

    G, R = NSA_KV_HEADS, NSA_HEADS // NSA_KV_HEADS
    qn = rope(rms_norm(heads(q_n, NSA_HEADS), nsa_q_gain), pos).reshape(B, S, G, R, HEAD_DIM)
    kc_cmp = compress(heads(kc, G), cmp_pe_k, cmp_k_w1, cmp_k_b1, cmp_k_w2)
    vc_cmp = compress(heads(vc, G), cmp_pe_v, cmp_v_w1, cmp_v_b1, cmp_v_w2)
    cmp_pos = (jnp.arange(kc_cmp.shape[1]) * CMP_STRIDE + CMP_BLOCK - 1).astype(jnp.float32)
    kc_cmp = rope(rms_norm(kc_cmp, nsa_kc_gain), cmp_pos)
    o_cmp, p_cmp = compressed_branch(qn, kc_cmp, vc_cmp)
    sel_idx = selection_indices(p_cmp)
    ks_r = rope(rms_norm(heads(ks, G), nsa_ks_gain), pos)
    o_sel = selected_branch(qn, ks_r, heads(vs, G), sel_idx)
    kw_r = rope(rms_norm(heads(kw, G), nsa_kw_gain), pos)
    o_win = window_branch(qn, kw_r, heads(vw, G))
    g = jax.nn.sigmoid(gate_logits.astype(jnp.float32)).reshape(B, S, G, R, 3).astype(o_cmp.dtype)
    o_nsa = g[..., 0:1] * o_cmp + g[..., 1:2] * o_sel + g[..., 2:3] * o_win
    o_nsa = o_nsa.reshape(B, S, NSA_WIDTH) * jax.nn.silu(z_n)

    Gd, Rd = DSA_KV_HEADS, DSA_HEADS // DSA_KV_HEADS
    qd = rope(rms_norm(heads(q_d, DSA_HEADS), dsa_q_gain), pos).reshape(B, S, Gd, Rd, HEAD_DIM)
    kd = rope(rms_norm(heads(k_d, Gd), dsa_k_gain), pos)
    qi_r = rope(qi.reshape(B, S, IDX_HEADS, IDX_DIM), pos)
    ki_r = rope(ki.reshape(B, S, 1, IDX_DIM), pos).reshape(B, S, IDX_DIM)
    o_dsa = dsa_branch(qd, kd, heads(v_d, Gd), qi_r, ki_r, wi)
    o_dsa = o_dsa.reshape(B, S, DSA_WIDTH) * jax.nn.silu(z_d)

    mixed = jnp.concatenate([o_nsa, o_dsa], axis=-1)
    return x + jnp.einsum('bsc,cd->bsd', mixed, w_out)

def first_inputs(seed: int = 0) -> dict:
    key = jax.random.key(seed)
    k = jax.random.split(key, 18)
    L = DEPTH
    Dh = HEAD_DIM

    def nrm(kk, shape, scale):
        return jax.random.normal(kk, shape, jnp.float32) * scale

    def gain(kk, n):
        return 1.0 + 0.01 * jax.random.normal(kk, (L, n), jnp.float32)

    return {
        "x": nrm(k[0], (BATCH, SEQ, D_MODEL), 1.0),
        "norm_gain": gain(k[1], D_MODEL),
        "w_in": nrm(k[2], (L, D_MODEL, IN_COLS), D_MODEL ** -0.5),
        "nsa_q_gain": gain(k[3], Dh),
        "nsa_kc_gain": gain(k[4], Dh),
        "nsa_ks_gain": gain(k[5], Dh),
        "nsa_kw_gain": gain(k[6], Dh),
        "cmp_pe_k": nrm(k[7], (L, CMP_BLOCK, Dh), 0.1),
        "cmp_k_w1": nrm(k[8], (L, CMP_BLOCK * Dh, CMP_HIDDEN), (CMP_BLOCK * Dh) ** -0.5),
        "cmp_k_b1": nrm(k[9], (L, CMP_HIDDEN), 0.01),
        "cmp_k_w2": nrm(k[10], (L, CMP_HIDDEN, Dh), CMP_HIDDEN ** -0.5),
        "cmp_pe_v": nrm(k[11], (L, CMP_BLOCK, Dh), 0.1),
        "cmp_v_w1": nrm(k[12], (L, CMP_BLOCK * Dh, CMP_HIDDEN), (CMP_BLOCK * Dh) ** -0.5),
        "cmp_v_b1": nrm(k[13], (L, CMP_HIDDEN), 0.01),
        "cmp_v_w2": nrm(k[14], (L, CMP_HIDDEN, Dh), CMP_HIDDEN ** -0.5),
        "dsa_q_gain": gain(k[15], Dh),
        "dsa_k_gain": gain(k[16], Dh),
        "w_out": nrm(k[17], (L, MIX_WIDTH, D_MODEL), MIX_WIDTH ** -0.5),
    }

def first_block(x, norm_gain, w_in, nsa_q_gain, nsa_kc_gain, nsa_ks_gain, nsa_kw_gain,
              cmp_pe_k, cmp_k_w1, cmp_k_b1, cmp_k_w2, cmp_pe_v, cmp_v_w1, cmp_v_b1, cmp_v_w2,
              dsa_q_gain, dsa_k_gain, w_out):
    for l in range(DEPTH):
        x = hybrid_layer(x, norm_gain[l], w_in[l], nsa_q_gain[l], nsa_kc_gain[l], nsa_ks_gain[l],
                         nsa_kw_gain[l], cmp_pe_k[l], cmp_k_w1[l], cmp_k_b1[l], cmp_k_w2[l],
                         cmp_pe_v[l], cmp_v_w1[l], cmp_v_b1[l], cmp_v_w2[l],
                         dsa_q_gain[l], dsa_k_gain[l], w_out[l])
    return x


DEPTH_2 = 2

LRU_WIDTH = D_MODEL
LRU_BLOCKS = 8
LRU_BLOCK_W = LRU_WIDTH // LRU_BLOCKS
CONV_W = 4
LRU_C = 8.0
MLA_HEADS = 8
QK_NOPE = 128
QK_ROPE = 64
QK_HEAD = QK_NOPE + QK_ROPE
V_HEAD = D_MODEL // MLA_HEADS
Q_RANK = 256
KV_RANK = 128
D_FF = -(-8 * D_MODEL // (3 * 256)) * 256
D_IN = LRU_WIDTH + Q_RANK + KV_RANK + QK_ROPE + 2 * D_MODEL
IN_SPLIT_POINTS = (LRU_WIDTH,
                   LRU_WIDTH + Q_RANK,
                   LRU_WIDTH + Q_RANK + KV_RANK,
                   LRU_WIDTH + Q_RANK + KV_RANK + QK_ROPE,
                   LRU_WIDTH + Q_RANK + KV_RANK + QK_ROPE + D_MODEL)


def rms_norm_2(x, gain=None):
    xf = x.astype(jnp.float32)
    y = xf * lax.rsqrt(jnp.mean(xf * xf, axis=-1, keepdims=True) + EPS)
    if gain is not None:
        y = y * gain.astype(jnp.float32)
    return y.astype(x.dtype)

def rope_tables(positions):
    inv_freq = ROPE_THETA ** (-jnp.arange(0, QK_ROPE, 2, dtype=jnp.float32) / QK_ROPE)
    ang = positions.astype(jnp.float32)[..., None] * inv_freq
    return jnp.cos(ang), jnp.sin(ang)

def apply_rope(x, cos, sin):
    half = QK_ROPE // 2
    xf = x.astype(jnp.float32)
    x1, x2 = xf[..., :half], xf[..., half:]
    return jnp.concatenate([x1 * cos - x2 * sin, x2 * cos + x1 * sin], axis=-1).astype(x.dtype)

def causal_depthwise_conv(x, w, b):
    y = lax.conv_general_dilated(x, w[:, None, :].astype(x.dtype), window_strides=(1,),
                                 padding=((CONV_W - 1, 0),),
                                 dimension_numbers=('NWC', 'WIO', 'NWC'),
                                 feature_group_count=x.shape[-1])
    return y + b

def rg_lru(x, positions, w_a, b_a, w_x, b_x, a_param):
    B, S, _ = x.shape
    xf = x.astype(jnp.float32)
    xb = xf.reshape(B, S, LRU_BLOCKS, LRU_BLOCK_W)
    r = jax.nn.sigmoid(jnp.einsum('bsni,nij->bsnj', xb, w_a.astype(jnp.float32))
                       + b_a.astype(jnp.float32)).reshape(B, S, LRU_WIDTH)
    i = jax.nn.sigmoid(jnp.einsum('bsni,nij->bsnj', xb, w_x.astype(jnp.float32))
                       + b_x.astype(jnp.float32)).reshape(B, S, LRU_WIDTH)
    log_a = -LRU_C * r * jax.nn.softplus(-a_param.astype(jnp.float32))
    reset = (positions == 0)[..., None]
    a = jnp.where(reset, 0.0, jnp.exp(log_a))
    mult = jnp.where(reset, 1.0, jnp.sqrt(-jnp.expm1(2.0 * log_a)))
    b_in = xf * i * mult

    def combine(left, right):
        return (left[0] * right[0], right[0] * left[1] + right[1])

    _, h = lax.associative_scan(combine, (a, b_in), axis=1)
    return h.astype(x.dtype)

def causal_block_attention(q, k, v):
    B, S, H, Dk = q.shape
    nb = S // Q_BLOCK
    scale = QK_HEAD ** -0.5
    qb = q.reshape(B, nb, Q_BLOCK, H, Dk).transpose(1, 0, 2, 3, 4)
    k_idx = jnp.arange(S)

    def one_block(args):
        q_blk, blk = args
        s = jnp.einsum('bqhd,bkhd->bhqk', q_blk, k, preferred_element_type=jnp.float32) * scale
        q_idx = blk * Q_BLOCK + jnp.arange(Q_BLOCK)
        s = jnp.where(k_idx[None, :] <= q_idx[:, None], s, -jnp.inf)
        p = jax.nn.softmax(s, axis=-1)
        o = jnp.einsum('bhqk,bkhd->bqhd', p.astype(v.dtype), v, preferred_element_type=jnp.float32)
        return o.astype(v.dtype)

    o = lax.map(one_block, (qb, jnp.arange(nb)))
    return o.transpose(1, 0, 2, 3, 4).reshape(B, S, H, v.shape[-1])

def mla(q_down, kv_down, k_rope, cos, sin, q_norm_g, kv_norm_g, w_uq, w_ukv):
    B, S, _ = q_down.shape
    c_q = rms_norm_2(q_down, q_norm_g)
    q = jnp.einsum('bsr,rhd->bshd', c_q, w_uq)
    q = jnp.concatenate([q[..., :QK_NOPE],
                         apply_rope(q[..., QK_NOPE:], cos[:, :, None, :], sin[:, :, None, :])], axis=-1)
    c_kv = rms_norm_2(kv_down, kv_norm_g)
    kv = jnp.einsum('bsr,rhd->bshd', c_kv, w_ukv)
    k_pe = apply_rope(k_rope, cos, sin)
    k = jnp.concatenate([kv[..., :QK_NOPE],
                         jnp.broadcast_to(k_pe[:, :, None, :], (B, S, MLA_HEADS, QK_ROPE))], axis=-1)
    v = kv[..., QK_NOPE:]
    o = causal_block_attention(q, k, v)
    return o.reshape(B, S, MLA_HEADS * V_HEAD)

def hybrid_layer_2(x, c, positions, cos, sin, w_ada, b_ada, w_in, conv_w, conv_b,
                 lru_wa, lru_ba, lru_wx, lru_bx, lru_a_param, q_norm_g, kv_norm_g,
                 w_uq, w_ukv, w_out, w_ffn_in, w_ffn_out):
    mod = (c @ w_ada + b_ada)[:, None, :]
    sh_m, sc_m, g_m, sh_f, sc_f, g_f = jnp.split(mod, 6, axis=-1)
    h = rms_norm_2(x) * (1 + sc_m) + sh_m
    proj = h @ w_in
    x_lru, q_down, kv_down, k_rope, gate_a, gate_b = jnp.split(proj, IN_SPLIT_POINTS, axis=-1)
    y_a = rg_lru(causal_depthwise_conv(x_lru, conv_w, conv_b), positions,
                 lru_wa, lru_ba, lru_wx, lru_bx, lru_a_param)
    y_b = mla(q_down, kv_down, k_rope, cos, sin, q_norm_g, kv_norm_g, w_uq, w_ukv)
    y = jax.nn.sigmoid(gate_a) * y_a + jax.nn.sigmoid(gate_b) * y_b
    x = x + g_m * (y @ w_out)
    h = rms_norm_2(x) * (1 + sc_f) + sh_f
    gate, up = jnp.split(h @ w_ffn_in, 2, axis=-1)
    x = x + g_f * ((jax.nn.silu(gate) * up) @ w_ffn_out)
    return x

def second_inputs(seed: int = 0) -> dict:
    key = jax.random.key(seed)
    ks = jax.random.split(key, 24)
    f32 = jnp.float32
    x = jax.random.normal(ks[0], (BATCH, SEQ, D_MODEL), f32)
    c = jax.random.normal(ks[1], (BATCH, D_MODEL), f32)
    positions = jnp.broadcast_to(jnp.arange(SEQ, dtype=jnp.int32)[None, :], (BATCH, SEQ))
    w_ada = jax.random.normal(ks[2], (DEPTH_2, D_MODEL, 6 * D_MODEL), f32) * (0.3 * D_MODEL ** -0.5)
    b_ada = jax.random.normal(ks[3], (DEPTH_2, 6 * D_MODEL), f32) * 0.02
    w_in = jax.random.normal(ks[4], (DEPTH_2, D_MODEL, D_IN), f32) * D_MODEL ** -0.5
    conv_w = jax.random.normal(ks[5], (DEPTH_2, CONV_W, LRU_WIDTH), f32) * CONV_W ** -0.5
    conv_b = jax.random.normal(ks[6], (DEPTH_2, LRU_WIDTH), f32) * 0.01
    lru_wa = jax.random.normal(ks[7], (DEPTH_2, LRU_BLOCKS, LRU_BLOCK_W, LRU_BLOCK_W), f32) * LRU_BLOCK_W ** -0.5
    lru_ba = jax.random.normal(ks[8], (DEPTH_2, LRU_BLOCKS, LRU_BLOCK_W), f32) * 0.01
    lru_wx = jax.random.normal(ks[9], (DEPTH_2, LRU_BLOCKS, LRU_BLOCK_W, LRU_BLOCK_W), f32) * LRU_BLOCK_W ** -0.5
    lru_bx = jax.random.normal(ks[10], (DEPTH_2, LRU_BLOCKS, LRU_BLOCK_W), f32) * 0.01
    rad = jax.random.uniform(ks[11], (DEPTH_2, LRU_WIDTH), f32, minval=0.9, maxval=0.999)
    a0 = rad ** (1.0 / LRU_C)
    lru_a_param = jnp.log(a0) - jnp.log1p(-a0)
    q_norm_g = 1.0 + 0.01 * jax.random.normal(ks[12], (DEPTH_2, Q_RANK), f32)
    kv_norm_g = 1.0 + 0.01 * jax.random.normal(ks[13], (DEPTH_2, KV_RANK), f32)
    w_uq = jax.random.normal(ks[14], (DEPTH_2, Q_RANK, MLA_HEADS, QK_HEAD), f32) * Q_RANK ** -0.5
    w_ukv = jax.random.normal(ks[15], (DEPTH_2, KV_RANK, MLA_HEADS, QK_NOPE + V_HEAD), f32) * KV_RANK ** -0.5
    w_out = jax.random.normal(ks[16], (DEPTH_2, D_MODEL, D_MODEL), f32) * D_MODEL ** -0.5
    w_ffn_in = jax.random.normal(ks[17], (DEPTH_2, D_MODEL, 2 * D_FF), f32) * D_MODEL ** -0.5
    w_ffn_out = jax.random.normal(ks[18], (DEPTH_2, D_FF, D_MODEL), f32) * D_FF ** -0.5
    final_norm_g = 1.0 + 0.01 * jax.random.normal(ks[19], (D_MODEL,), f32)
    return {'x': x, 'c': c, 'positions': positions, 'w_ada': w_ada, 'b_ada': b_ada,
            'w_in': w_in, 'conv_w': conv_w, 'conv_b': conv_b, 'lru_wa': lru_wa,
            'lru_ba': lru_ba, 'lru_wx': lru_wx, 'lru_bx': lru_bx, 'lru_a_param': lru_a_param,
            'q_norm_g': q_norm_g, 'kv_norm_g': kv_norm_g, 'w_uq': w_uq, 'w_ukv': w_ukv,
            'w_out': w_out, 'w_ffn_in': w_ffn_in, 'w_ffn_out': w_ffn_out,
            'final_norm_g': final_norm_g}

def second_block(x, c, positions, w_ada, b_ada, w_in, conv_w, conv_b, lru_wa, lru_ba, lru_wx,
              lru_bx, lru_a_param, q_norm_g, kv_norm_g, w_uq, w_ukv, w_out, w_ffn_in,
              w_ffn_out, final_norm_g):
    cos, sin = rope_tables(positions)
    for l in range(DEPTH_2):
        x = hybrid_layer_2(x, c, positions, cos, sin, w_ada[l], b_ada[l], w_in[l], conv_w[l],
                         conv_b[l], lru_wa[l], lru_ba[l], lru_wx[l], lru_bx[l], lru_a_param[l],
                         q_norm_g[l], kv_norm_g[l], w_uq[l], w_ukv[l], w_out[l],
                         w_ffn_in[l], w_ffn_out[l])
    return rms_norm_2(x, final_norm_g)


def setup_inputs(seed=0):
    out = dict(first_inputs(seed))
    for name, value in second_inputs(seed + 1).items():
        if name != "x":
            out[name + "_2"] = value
    return out


def reference(
    x, norm_gain, w_in, nsa_q_gain, nsa_kc_gain, nsa_ks_gain, nsa_kw_gain, cmp_pe_k, cmp_k_w1,
    cmp_k_b1, cmp_k_w2, cmp_pe_v, cmp_v_w1, cmp_v_b1, cmp_v_w2, dsa_q_gain, dsa_k_gain, w_out,
    c_2, positions_2, w_ada_2, b_ada_2, w_in_2, conv_w_2, conv_b_2, lru_wa_2, lru_ba_2,
    lru_wx_2, lru_bx_2, lru_a_param_2, q_norm_g_2, kv_norm_g_2, w_uq_2, w_ukv_2, w_out_2,
    w_ffn_in_2, w_ffn_out_2, final_norm_g_2,
):
    x = first_block(
        x, norm_gain, w_in, nsa_q_gain, nsa_kc_gain, nsa_ks_gain, nsa_kw_gain, cmp_pe_k,
        cmp_k_w1, cmp_k_b1, cmp_k_w2, cmp_pe_v, cmp_v_w1, cmp_v_b1, cmp_v_w2, dsa_q_gain,
        dsa_k_gain, w_out,
    )
    return second_block(
        x, c_2, positions_2, w_ada_2, b_ada_2, w_in_2, conv_w_2, conv_b_2, lru_wa_2, lru_ba_2,
        lru_wx_2, lru_bx_2, lru_a_param_2, q_norm_g_2, kv_norm_g_2, w_uq_2, w_ukv_2, w_out_2,
        w_ffn_in_2, w_ffn_out_2, final_norm_g_2,
    )


_drawn_inputs = setup_inputs


def setup_inputs(seed=0):
    import zlib

    import numpy as np

    out = dict(_drawn_inputs(seed))
    spreads = {}
    factors = {'norm_gain': 8.0,
     'nsa_q_gain': 8.0,
     'nsa_kc_gain': 31.504,
     'nsa_ks_gain': 8.0,
     'nsa_kw_gain': 8.0,
     'cmp_pe_k': 8.0,
     'cmp_k_b1': 29.639,
     'cmp_pe_v': 12.041,
     'cmp_v_b1': 64.0,
     'dsa_q_gain': 8.0,
     'dsa_k_gain': 8.0,
     'conv_b_2': 200.0,
     'lru_ba_2': 200.0,
     'lru_bx_2': 200.0,
     'q_norm_g_2': 64.0,
     'kv_norm_g_2': 64.0,
     'final_norm_g_2': 143.72,
     'b_ada_2': 7.228,
     'conv_w_2': 7.153,
     'lru_wa_2': 64.0,
     'lru_wx_2': 22.332,
     'lru_a_param_2': 64.0,
     'w_ffn_in_2': 8.0,
     'w_ffn_out_2': 8.0}
    for name, (base, spread) in spreads.items():
        noise = np.random.default_rng([zlib.crc32(name.encode()), seed]).standard_normal(out[name].shape)
        drawn = base * np.exp(spread * noise) if base else spread * noise
        out[name] = __import__('jax').numpy.asarray(drawn.astype(out[name].dtype))
    for name, factor in factors.items():
        out[name] = (out[name] * factor).astype(out[name].dtype)
    return out
```

```python
import math
from contextlib import ExitStack

import numpy as np

import concourse.bass as bass
from concourse import mybir

ALU = mybir.AluOpType
ACT = mybir.ActivationFunctionType
F32 = mybir.dt.float32
F32R = mybir.dt.float32r
BF16 = mybir.dt.bfloat16
I32 = mybir.dt.int32
AX_X = mybir.AxisListType.X

P = 128
D = 1024
KD = D // P
S = 512
NT = S // P
HEADS = 8
DH = 64
HALF = DH // 2
NCMP = 32
CMP_STRIDE, CMP_BLOCK, CMP_HID = 16, 32, 256
TOPK = 128
QK = 192
Q_RANK, KV_RANK = 256, 128
DFF = 2816
FT = DFF // P
FH = FT // 2
LAYERS = 2
LRU_C = 8.0
NEG = -1e30
TAKEN = -3.0e38
EPS = 1e-6
THETA = 10000.0
RAW_RING = 7
SPLIT_RING = 4
ADA = 48


def stream_order():
    order = []
    ada = [("ada", 0, i) for i in range(ADA)]
    for g in P1_ORDER:
        for s in range(4):
            order.append(("p1", g, s))
            if g:
                order.append(ada.pop(0))
        if g in (2, 3):
            order += [("cw", g - 2, s) for s in range(4)]
    for n in range(KD):
        order.append(("o1", n))
        order += [ada.pop(0) for _ in range(3)]
    for layer in range(LAYERS):
        ada = [("ada", layer + 1, i) for i in range(ADA)] if layer + 1 < LAYERS else []
        for q in range(4):
            order += [("xl", layer, 2 * q), ("xl", layer, 2 * q + 1), ("ga", layer, q), ("lg", layer, q)]
        order += [("ga", layer, n) for n in range(4, KD)]
        order += [("gb", layer, n) for n in range(KD)]
        order += [("kvq", layer, s) for s in range(4)]
        order += [("uv", layer), ("uqr", layer)]
        order += [("hd", layer, n) for n in range(4)]
        order += [("o2", layer, n) for n in range(KD)]
        for half in range(2):
            for f in range(half * FH, half * FH + FH):
                for kind in ("fg", "fu"):
                    order.append((kind, layer, f))
                    if ada:
                        order.append(ada.pop(0))
            for s in range(FH):
                order.append(("fo", layer, half, s))
                if ada:
                    order.append(ada.pop(0))
        assert not ada
    return order


P1_ORDER = (0, 1, 4, 2, 3, 5, 6)
STREAM = stream_order()
SLOT = {key: n for n, key in enumerate(STREAM)}
WEIGHTS = [key for key in STREAM if key[0] not in ("ada", "cw")]
WSLOT = {key: n for n, key in enumerate(WEIGHTS)}
assert len(STREAM) % RAW_RING == 0


def fo_slot(layer, half, n):
    return ("fo", layer, half, (n * FH + FH - 1) // 8)


def next_norm(layer):
    return f"m{layer + 1}" if layer + 1 < LAYERS else "fin"


def mod_points():
    anchors = [("p1", g, 3) for g in P1_ORDER] + [("o1", n) for n in range(KD)]
    for half in range(2):
        anchors += [("fu", 0, f) for f in range(half * FH, half * FH + FH)]
        anchors += [fo_slot(0, half, n) for n in range(KD)]
    anchors = list(dict.fromkeys(anchors))
    out = {}
    for layer in range(LAYERS):
        for cb in range(ADA // 8):
            last = SLOT[("ada", layer, 8 * cb + 7)]
            key = next((k for k in anchors if SLOT[k] > last + 1), None)
            if layer == 0 and key[0] not in ("p1", "o1"):
                key = None
            out.setdefault(key or ("o1", KD - 1), []).append((layer, cb))
    return out


MODS = mod_points()

PB_ADA, PCONV_W, PCONV_B, PBA, PBX, PA, PQG, PKVG, PCOLS = 0, 48, 80, 88, 96, 104, 112, 114, 115
G_Q, G_KC, G_KS, G_KW, G_QD, G_KD, G_ONE, G_ROWS = 0, 1, 2, 3, 4, 5, 6, 7

SEMAPHORES = (
    "step", "consts", "x_in", "passed", "normed", "stored", "ada", "w_hi", "square", "sq_added", "pool_set",
    "read_act", "full", "ca", "read_dve", "gmix", "h_hi", "lru_par", "lru_w", "topk", "iscore", "cos_sin",
    "cmp_shift", "cmp_exp", "nmax", "mix_hi", "x_new", "conv", "xc_hi", "tanh", "lru_a", "one_aa", "mult",
    "ya_gated", "c_hi", "y_full", "y_hi", "hid", "hid_hi", "x_half", "h_lo", "yb", "y_lo", "cmp_p", "xc_lo",
    "p_norm", "hid_lo", "w_used",
)

UNITS1 = [(b, j, g, qt) for b in (0, 1) for j in range(4) for qt in range(NT) for g in range(2)]
UNITS1 += [(2, j, g, qt) for qt in range(NT) for j in range(4) for g in range(2)]
O1_SPLITS = (16, 28, 40, 60)
O1_ADAS = (8, 15, 22, 29, 36, 43, 50)
UNITS2 = [(h, qt) for h in range(HEADS) for qt in range(NT)]


def program(nc, a, known):
    note = {}
    with ExitStack() as ctx:
        base = (nc.sbuf_base + 63) // 64 * 64
        KB = 1024

        def at(name, shape, dt, off):
            return nc.alloc_sbuf_tensor_at(name, shape, dt, offset=base + int(off))

        X = at("X", [P, KD, S], F32, 0)
        HH = at("HH", [P, KD, S], F32R, 16 * KB)
        HL = at("HL", [P, KD, S], F32R, 32 * KB)
        RAW = [at(f"RAW{i}", [P, 1024], F32, (48 + 4 * i) * KB) for i in range(RAW_RING)]
        split0 = 48 + 4 * RAW_RING
        WH = [at(f"WH{i}", [P, 1024], F32R, (split0 + 8 * i) * KB) for i in range(SPLIT_RING)]
        WL = [at(f"WL{i}", [P, 1024], F32R, (split0 + 4 + 8 * i) * KB) for i in range(SPLIT_RING)]
        cur = [(split0 + 8 * SPLIT_RING) * KB]

        def small(name, shape, dt, size=4):
            off = cur[0]
            cur[0] += (int(np.prod(shape[1:])) * size + 31) // 32 * 32
            return at(name, shape, dt, off)

        ident = small("ident", [P, P], F32)
        ones = small("ones", [P, P], F32)
        identb = small("identb", [P, P], BF16, 2)
        causal = small("causal", [P, P], BF16, 2)
        vec1 = small("vec1", [P, 3 * KD], F32)
        par = small("par", [P, LAYERS, PCOLS], F32)
        mod = small("mod", [P, LAYERS, ADA], F32)
        sc1 = small("sc1", [P, LAYERS, 2, KD], F32)
        csc = small("csc", [P, LAYERS, KD], F32)
        lt = small("lt", [P, 6, LAYERS, KD], F32)
        cs2 = small("cs2", [P, 2, NT, HALF], F32)
        freq = small("freq", [P, HALF], F32)
        posi = small("posi", [P, NT], I32)
        posf = small("posf", [P, NT], F32)
        keep = small("keep", [P, S], BF16, 2)
        reset = small("reset", [P, S], BF16, 2)
        stat = small("stat", [P, 3, NT], F32)
        nmax = small("nmax", [P, 8], F32)
        rsum = small("rsum", [P, 8], F32)
        coef = small("coef", [P, 8], F32)
        gate = small("gate", [P, NT, 28], F32)
        kst = small("kst", [P, 3, NT * 8], F32)
        W0 = (cur[0] + 63) // 64 * 64

        def w(name, shape, dt, kb):
            return at(name, shape, dt, W0 + kb * KB)

        G = {1: w("G1", [P, NT, 512], F32, 0), 2: w("G2", [P, NT, 512], F32, 8),
             3: w("G3", [P, NT, 512], F32, 16), 4: w("G4", [P, NT, 512], F32, 24)}
        MISC = w("MISC", [P, NT, 384], F32, 32)
        QIT = w("QIT", [P, 2, S], F32, 38)
        KIT = w("KIT", [P, S], F32, 42)
        RELU = w("RELU", [P, 3, S], F32, 44)
        SCORE = w("SCORE", [P, S], F32, 50)
        Z = w("Z", [P, NT, D], F32, 32)
        KC2 = w("KC2", [P, 2, 544], F32, 52)
        CA = w("CA", [P, 16, 2 * NCMP], F32, 56.25)
        HID = w("HID", [P, 2, CMP_HID], F32, 60.25)
        HIDT = w("HIDT", [P, 2, 2, 2 * NCMP], F32, 62.25)
        CK = w("CK", [P, 3, DH], F32, 63.25)
        KCT = w("KCT", [P, NCMP], F32, 64)
        VBLK = w("VBLK", [P, 2, 256], F32, 64.25)
        MASKB = w("MASKB", [P, 3, S], BF16, 66.25)
        TAB = w("TAB", [P, 2, NT, DH], F32, 69.25)
        CS1 = w("CS1", [P, 2, NT, HALF], F32, 71.25)
        TMP = w("TMP", [P, 2, S], F32, 72.25)
        SQS = w("SQS", [P, S], F32, 76.25)
        ACC = w("ACC", [P, 2, 1024], F32, 78.25)
        gains = w("gains", [P, G_ROWS, DH], F32, 86.25)
        cb1 = w("cb1", [P, 2, CMP_HID], F32, 88)
        cw2 = w("cw2", [P, 2, 2, DH], F32, 90)
        pe2 = w("pe2", [P, 2, 16], F32, 91)
        cscmp = w("cscmp", [P, 2, HALF], F32, 91.125)
        cmask = w("cmask", [P, NT, NCMP], F32, 91.375)
        cvalid = w("cvalid", [P, NT], F32, 91.875)
        TKM = w("TKM", [P, 8], F32, 91.9375)
        MIX = w("MIX", [P, NT, D], F32, 8)
        PT1 = w("PT1", [P, 3, S], F32, 52)
        QNT = at("QNT", [P, 4, S], F32, 16 * KB)
        QDT = at("QDT", [P, 4, S], F32, 24 * KB)
        KT = at("KT", [P, 3, S], F32, 32 * KB)
        PR = at("PR", [P, 3, S], F32, 38 * KB)
        PC = at("PC", [P, 2, 8, NCMP], F32, 44 * KB)
        CST = at("CST", [P, 4, 8], F32, 46 * KB)

        YA = w("YA", [P, KD, S], F32, 0)
        YH = w("YH", [P, KD, S], F32R, 0)
        SG = w("SG", [P, KD, S], F32, 16)
        YL = w("YL", [P, KD, S], F32R, 16)
        XC = w("XC", [P, KD, S], F32, 32)
        LR = w("LR", [P, KD, S], F32, 48)
        LI = w("LI", [P, KD, S], F32, 64)
        XCH = w("XCH", [P, 2, S], F32R, 80)
        XCL = w("XCL", [P, 2, S], F32R, 84)
        V2 = w("V2", [P, NT, D], F32, 32)
        QRT = w("QRT", [P, 4, S], F32, 48)
        KPE = w("KPE", [P, S], F32, 56)
        QN = w("QN", [P, 2, S], F32, 58)
        KN = w("KN", [P, 2, S], F32, 62)
        P2 = w("P2", [P, 3, S], F32, 66)
        PT2 = w("PT2", [P, 2, NT, S], F32, 72)
        YT = w("YT", [P, 2, S], F32, 88)
        KVR = at("KVR", [P, NT, 448], F32, 16 * KB)
        TAB2 = at("TAB2", [P, 2, NT, DH], F32, 23 * KB)
        CQH = at("CQH", [P, 2, S], F32R, 25 * KB)
        CKH = at("CKH", [P, S], F32R, 29 * KB)
        CQL = at("CQL", [P, 2, S], F32R, 31 * KB)
        CKL = at("CKL", [P, S], F32R, 35 * KB)
        QRR = at("QRR", [P, NT, 512], F32, 37 * KB)
        HDH = w("HDH", [P, FH, S], F32R, 0)
        HDL = w("HDL", [P, FH, S], F32R, 22)
        SILU = w("SILU", [P, 2, S], F32, 44)
        HF = w("HF", [P, 2, S], F32, 48)
        NTMP = w("NTMP", [P, 2, S], F32, 52)
        SQT = w("SQT", [P, 2, S], F32, 56)
        SQ2 = w("SQ2", [P, S], F32, 60)

        bank = [ctx.enter_context(nc.psum_tensor(f"bank{i}", [P, S], F32)) for i in range(8)]
        landed = [ctx.enter_context(nc.semaphore(f"slot_landed{i}")) for i in range(RAW_RING)]
        sem = {name: ctx.enter_context(nc.semaphore(name)) for name in SEMAPHORES}
        step = sem["step"]
        count = dict.fromkeys(SEMAPHORES, 0)

        def mark(name, *key, by=1):
            count[name] += by
            note[(name,) + key] = count[name]
            return by

        def value(*key):
            if known and key not in known:
                raise KeyError(key)
            return known.get(key, 1)

        def own():
            count["step"] += 1
            return count["step"]

        def ring(key):
            return SLOT[key] % RAW_RING

        def loads(key):
            return 16 * (SLOT[key] // RAW_RING + 1)

        def last_use(key):
            name, v = known.get(("used",) + key, ("full", 1))
            return sem[name], v

        def raw(key):
            return RAW[SLOT[key] % RAW_RING]

        def hi(key):
            return WH[WSLOT[key] % SPLIT_RING]

        def lo(key):
            return WL[WSLOT[key] % SPLIT_RING]

        def bank_of(*key):
            return bank[known.get(("bank",) + key, 0)]

        def spread(ap, dims, shape):
            return ap.rearrange(dims, o=1).broadcast_to(shape)

        block = ctx.enter_context(nc.Block())

        @block.sync
        def _(sp):
            def load(dst, src):
                sp.dma_start(dst, src).then_inc(sem["consts"], mark("consts", by=16))

            for k in range(0, KD, 4):
                sp.dma_start(X[:, k:k + 4, :], a["xt"][:, k:k + 4, :]).then_inc(
                    sem["x_in"], mark("x_in", by=16))
            note[("x_in", "all")] = count["x_in"]
            for s in range(4):
                sp.dma_start(RAW[s][:], a["stream"][s]).then_inc(landed[s], 16)
            load(ones[:], a["ones"])
            load(ident[:], a["ident"])
            load(ACC[:, 0, 0:P], a["causal"])
            load(vec1[:], a["vec1"])
            load(par[:], a["par"])
            load(freq[:], a["freq"].broadcast_to([P, HALF]))
            load(posi[:], a["pos_tok"])
            load(ACC[:, 1, 0:S].bitcast(I32), a["pos"].broadcast_to([P, S]))
            load(CS1[:], a["cs1"])
            load(gains[:], spread(a["gains"], "(o r) d -> o r d", [P, G_ROWS, DH]))
            load(pe2[:], a["pe2"])
            load(cw2[:], a["cw2"])
            load(cb1[0:1], a["cb1"])
            load(cscmp[0:2 * NCMP], a["cscmp"])
            load(cmask[:], a["cmask"])
            load(cvalid[:], a["cvalid"])
            note[("consts", "all")] = count["consts"]
            for s in range(4, RAW_RING):
                sp.dma_start(RAW[s][:], a["stream"][s]).then_inc(landed[s], 16)

            with sp.Fori(1, len(STREAM) // RAW_RING) as i:
                for s in range(RAW_RING):
                    sp.wait_ge(sem["passed"], i * RAW_RING + (s + 1 - RAW_RING))
                    sp.dma_start(RAW[s][:], a["stream"][bass.ds(i * RAW_RING + s, 1)].rearrange(
                        "o p c -> (o p) c")).then_inc(landed[s], 16)

            for k in range(KD):
                sp.wait_ge(sem["normed"], value("normed", "fin", k))
                sp.dma_start(a["out"][:, k, :], YA[:, k, :]).then_inc(sem["stored"], mark("stored", k, by=16))
            sp.wait_ge(sem["stored"], 16 * KD)

        @block.gpsimd
        def _(pool):
            at_slot = [0]

            def pass_through(key, ahead=SPLIT_RING - 1):
                last = SLOT[WEIGHTS[min(WSLOT[key] + ahead, len(WEIGHTS) - 1)]]
                while at_slot[0] <= last:
                    k = STREAM[at_slot[0]]
                    if k[0] == "ada":
                        pool.wait_ge(sem["ada"], value("ada", *k[1:]))
                    elif k[0] == "cw":
                        pool.wait_ge(*last_use(k))
                    else:
                        pool.wait_ge(sem["w_hi"], value("w_hi", *k))
                        nc.gpsimd.tensor_tensor(lo(k)[:], raw(k)[:], hi(k)[:].bitcast(F32),
                                                ALU.subtract).then_inc(sem["passed"], mark("passed", *k))
                        at_slot[0] += 1
                        continue
                    pool.wait_ge(sem["passed"], max(1, count["passed"]))
                    pool.sem_inc(sem["passed"], 1)
                    count["passed"] += 1
                    at_slot[0] += 1

            def add_squares(tag, sq, total, key_of=None):
                for k in range(1, KD):
                    if key_of:
                        pass_through(key_of(k))
                    pool.wait_ge(sem["square"], value("square", tag, k))
                    if k > 1:
                        pool.wait_ge(sem["sq_added"], value("sq_added", tag, k - 1))
                    nc.gpsimd.tensor_tensor(total[:], sq[:, 0, :] if k == 1 else total[:],
                                            sq[:, k % 2, :], ALU.add).then_inc(
                        sem["sq_added"], mark("sq_added", tag, k))

            nc.gpsimd.memset(VBLK[:], 0.0).then_inc(sem["pool_set"], mark("pool_set", 0))
            nc.gpsimd.memset(KC2[:], 0.0).then_inc(sem["pool_set"], mark("pool_set", 1))
            add_squares("n1", RELU, SQS)
            pool.wait_ge(sem["consts"], value("consts", "all"))
            for kv in range(2):
                pass_through(("p1", (4, 2)[kv], 3))
                pool.wait_ge(sem["read_act"], value("read_act", "tc", kv))
                if kv:
                    pool.wait_ge(sem["full"], value("full", "hid", 0))
                for i in range(16):
                    src = KC2[:, :, 2 * i:2 * i + 16 * NCMP].rearrange("p g (c t) -> p g c t", t=16)[:, :, :, 0]
                    nc.gpsimd.tensor_scalar(
                   CA[:, i, :].rearrange("p (g c) -> p g c", g=2), src, pe2[:, kv, i:i + 1], None,
                   ALU.add).then_inc(sem["ca"], mark("ca", kv, i))
            pass_through(("o1", 2), 0)
            for qt in range(NT):
                pool.wait_ge(sem["read_dve"], value("read_dve", "o", 1, UNITS1.index((2, 3, 1, qt))))
                pool.wait_ge(sem["read_act"], value("read_act", "p1", 6, qt))
                nc.gpsimd.tensor_tensor(MIX[:, qt, :], MIX[:, qt, :], Z[:, qt, :], ALU.mult).then_inc(
                    sem["gmix"], mark("gmix", qt))
            add_squares("m0", SQT, SQ2, lambda k: ("o1", k))
            for layer in range(LAYERS):
                pass_through(("hd", layer, 3))
                add_squares(f"f{layer}", SQT, SQ2, lambda k: ("o2", layer, k))
                add_squares(next_norm(layer), SQT, SQ2, lambda k: fo_slot(layer, 1, k))

        @block.scalar
        def _(act):
            split_next = [0]

            def split_through(key, ahead=SPLIT_RING - 1):
                last = min(WSLOT[key] + ahead, len(WEIGHTS) - 1)
                while split_next[0] <= last:
                    k = WEIGHTS[split_next[0]]
                    act.wait_ge(landed[ring(k)], loads(k))
                    if split_next[0] >= SPLIT_RING:
                        act.wait_ge(*last_use(WEIGHTS[split_next[0] - SPLIT_RING]))
                    nc.scalar.activation(hi(k)[:], raw(k)[:], ACT.Copy).then_inc(sem["w_hi"], mark("w_hi", *k))
                    split_next[0] += 1

            def evict(dst, *key, func=ACT.Copy, **kw):
                act.wait_ge(sem["full"], value("full", *key))
                b = bank_of(*key)
                n = int(np.prod(dst.shape[1:]))
                return nc.scalar.activation(dst, b[0:dst.shape[0], 0:n], func, **kw).then_inc(
                    sem["read_act"], mark("read_act", *key))

            def square(tag, k, sq):
                if k >= 2:
                    act.wait_ge(sem["sq_added"], value("sq_added", tag, max(1, k - 2)))
                nc.scalar.activation(sq[:, k % 2, :], X[:, k, :], ACT.Square).then_inc(
                    sem["square"], mark("square", tag, k))

            def norm_hi(tag, tmp, shift):
                for k in range(KD):
                    act.wait_ge(sem["normed"], value("normed", tag, k))
                    if shift is None:
                        ins = nc.scalar.activation(HH[:, k, :], tmp[:, k % 2, :], ACT.Copy)
                    else:
                        ins = nc.scalar.activation(HH[:, k, :], tmp[:, k % 2, :], ACT.Identity,
                                                   bias=shift[:, k:k + 1])
                    ins.then_inc(sem["h_hi"], mark("h_hi", tag, k))

            act.wait_ge(sem["x_in"], value("x_in", "all"))
            split_through(("p1", 0, 0))
            for k in range(KD):
                square("n1", k, RELU)
            act.wait_ge(sem["consts"], value("consts", "all"))
            nc.scalar.activation(lt[:, 0], par[:, :, PA:PA + KD], ACT.Abs).then_inc(
                sem["lru_par"], mark("lru_par", 0))
            act.wait_ge(sem["lru_par"], value("lru_par", 0))
            nc.scalar.activation(lt[:, 1], lt[:, 0], ACT.Exp, scale=-1.0).then_inc(
                sem["lru_par"], mark("lru_par", 1))
            norm_hi("n1", TMP, None)
            act.wait_ge(sem["lru_w"], value("lru_w"))
            nc.scalar.activation(lt[:, 3], lt[:, 2], ACT.Ln).then_inc(sem["lru_par"], mark("lru_par", 2))

            def evict_group(g):
                split_through(("p1", g, 3), 0 if g in (2, 3, 6) else SPLIT_RING - 1)
                for tt in range(NT):
                    act.wait_ge(sem["full"], value("full", "p1", g, tt))
                    b = bank_of("p1", g, tt)
                    if g == 0:
                        nc.scalar.activation(MISC[:, tt, :], b[:, 0:384], ACT.Copy)
                        nc.scalar.activation(gate[:, tt, 24:28], b[:, 408:412], ACT.Copy, scale=0.5)
                        nc.scalar.activation(gate[:, tt, 0:24], b[:, 384:408], ACT.Sigmoid).then_inc(
                            sem["read_act"], mark("read_act", "p1", g, tt))
                    elif g < 5:
                        evict(G[g][:, tt, :], "p1", g, tt)
                    else:
                        act.wait_ge(sem["topk"], value("topk", 3))
                        evict(Z[:, tt, (g - 5) * 512:(g - 4) * 512], "p1", g, tt, func=ACT.Silu)

            def relus(qt):
                n = (qt + 1) * P
                for h in range(1, 4):
                    if qt > 1:
                        act.wait_ge(sem["iscore"], value("iscore", qt - 1, h))
                    evict(RELU[:, h - 1, 0:n], "idx", qt, h, func=ACT.Relu)

            def shift_in(kv):
                act.wait_ge(sem["full"], value("full", "tc", kv))
                b = bank_of("tc", kv)
                act.wait_ge(sem["pool_set"], value("pool_set", 1))
                if kv:
                    act.wait_ge(sem["ca"], value("ca", 0, 15))
                for g in range(2):
                    nc.scalar.activation(KC2[0:DH, g, 0:S], b[g * DH:(g + 1) * DH, :], ACT.Copy)
                    last = nc.scalar.activation(KC2[DH:P, g, 0:S - 1], b[g * DH:(g + 1) * DH, 1:S], ACT.Copy)
                last.then_inc(sem["read_act"], mark("read_act", "tc", kv))

            evict_group(0)
            evict_group(1)
            for i in range(3):
                evict(QIT[:, i, :] if i < 2 else KIT[:], "ti", i)
            evict_group(4)
            relus(1)
            shift_in(0)
            evict_group(2)
            relus(2)
            split_through(("p1", 3, 0))
            evict(HID[0:2 * NCMP, 0, :], "hid", 0, func=ACT.Silu)
            shift_in(1)
            evict_group(3)
            evict(HID[0:2 * NCMP, 1, :], "hid", 1, func=ACT.Silu)
            relus(3)
            for kv in range(2):
                evict(HIDT[:, kv].rearrange("p c t -> p (c t)"), "ht", kv)
            evict(CK[0:2 * NCMP, 0, :], "co", 0)
            act.wait_ge(sem["full"], value("full", "co", 1))
            b = bank_of("co", 1)
            act.wait_ge(sem["pool_set"], value("pool_set", 0))
            for g in range(2):
                for r in range(4):
                    last = nc.scalar.activation(VBLK[32 * r:32 * r + 32, g, DH * r:DH * r + DH],
                                                b[32 * g:32 * g + 32, 0:DH], ACT.Copy)
            last.then_inc(sem["read_act"], mark("read_act", "co", 1))
            evict_group(5)
            evict_group(6)
            for i in range(3):
                evict(KT[:, i, :], "tk", i)
            for i in range(4):
                evict(QNT[:, i, :], "tqn", i)
            act.wait_ge(sem["full"], value("full", "tkc"))
            b = bank_of("tkc")
            nc.scalar.activation(KCT[0:DH, :], b[0:DH, 0:NCMP], ACT.Copy)
            nc.scalar.activation(KCT[DH:P, :], b[0:DH, NCMP:2 * NCMP], ACT.Copy).then_inc(
                sem["read_act"], mark("read_act", "tkc"))

            act.wait_ge(step, value("angles"))
            nc.scalar.activation(cs2[:], cs2[:], ACT.Sin).then_inc(sem["cos_sin"], mark("cos_sin"))

            for qt in range(NT):
                act.wait_ge(sem["cmp_shift"], value("cmp_shift", qt))
                nc.scalar.activation(PC[:, qt % 2], PC[:, qt % 2], ACT.Exp).then_inc(
                    sem["cmp_exp"], mark("cmp_exp", qt))
                if qt >= 1:
                    if qt >= 4:
                        act.wait_ge(sem["full"], value("full", "cpv", qt - 4))
                    evict(PT1[:, (qt - 1) % 3, 0:256], "ct", qt - 1)
            act.wait_ge(sem["full"], value("full", "cpv", 0))
            evict(PT1[:, 0, 0:256], "ct", 3)

            for u in range(len(UNITS1) + 2):
                if u in O1_SPLITS:
                    split_through(("o1", O1_SPLITS.index(u)), 0)
                if u < len(UNITS1):
                    n = (UNITS1[u][3] + 1) * P
                    act.wait_ge(sem["nmax"], value("nmax", 1, u))
                    if u >= 3:
                        act.wait_ge(sem["full"], value("full", "t", 1, u - 3))
                    act.wait_ge(sem["full"], value("full", "s", 1, u))
                    b = bank_of("s", 1, u)
                    nc.scalar.activation(PR[:, u % 3, 0:n], b[:, 0:n], ACT.Exp, bias=nmax[:, u % 8:u % 8 + 1],
                                         accum_out=rsum[:, u % 8:u % 8 + 1]).then_inc(
                        sem["read_act"], mark("read_act", "s", 1, u))
                v = u - 2
                if v >= 0 and v % 2 == 0:
                    act.wait_ge(sem["full"], value("full", *(("o", 1, v - 3) if v >= 3 else ("cpv", 3))))
                    evict(PT1[:, v % 3, 0:(UNITS1[v][3] + 1) * P], "t", 1, v)
            for i in range(KD):
                act.wait_ge(sem["full"], value("full", "tm", i))
                b = bank_of("tm", i)
                nc.scalar.activation(HH[:, i, :], b[:], ACT.Copy).then_inc(sem["mix_hi"], mark("mix_hi", i))
            for n in range(KD):
                split_through(("o1", n))
                act.wait_ge(sem["x_new"], value("x_new", "m0", n))
                square("m0", n, SQT)

            for layer in range(LAYERS):
                L = layer

                def vec(col):
                    return par[:, L, col:col + 1]

                split_through(("xl", L, 0), 0)
                norm_hi(f"m{L}", NTMP, mod[:, L, 0:KD])
                for q in range(4):
                    split_through(("xl", L, 2 * q))
                    for n in (2 * q, 2 * q + 1):
                        split_through(("xl", L, n))
                        act.wait_ge(sem["conv"], value("conv", L, n))
                        if n >= 2:
                            act.wait_ge(sem["full"], value("full", "li", L, n - 2))
                        nc.scalar.activation(XCH[:, n % 2, :], XC[:, n, :], ACT.Copy).then_inc(
                            sem["xc_hi"], mark("xc_hi", L, n))
                    split_through(("ga", L, q))
                    evict(SG[:, q, :], "ga", L, q, func=ACT.Sigmoid)
                    split_through(("lg", L, q))
                    for n in (2 * q, 2 * q + 1):
                        evict(LR[:, n, :], "lr", L, n, func=ACT.Sigmoid, bias=vec(PBA + n))
                        evict(LI[:, n, :], "li", L, n, func=ACT.Sigmoid, bias=vec(PBX + n))
                        act.wait_ge(sem["read_act"], value("read_act", "lr", L, n))
                        nc.scalar.activation(YA[:, n, :], LR[:, n, :], ACT.Tanh, scale=csc[:, L, n:n + 1]).then_inc(
                            sem["tanh"], mark("tanh", L, n))
                for n in range(KD):
                    act.wait_ge(sem["tanh"], value("tanh", L, n))
                    nc.scalar.activation(LR[:, n, :], LR[:, n, :], ACT.Exp, scale=csc[:, L, n:n + 1]).then_inc(
                        sem["lru_a"], mark("lru_a", L, n))
                for n in range(4, KD):
                    split_through(("ga", L, n))
                    evict(SG[:, n, :], "ga", L, n, func=ACT.Sigmoid)
                for n in range(KD):
                    act.wait_ge(sem["one_aa"], value("one_aa", L, n))
                    nc.scalar.activation(YA[:, n, :], YA[:, n, :], ACT.Sqrt, scale=-1.0).then_inc(
                        sem["mult"], mark("mult", L, n))
                for n in range(KD):
                    split_through(("gb", L, n))
                    act.wait_ge(sem["ya_gated"], value("ya_gated", L, n))
                    evict(SG[:, n, :], "gb", L, n, func=ACT.Sigmoid)
                split_through(("kvq", L, 3))
                act.wait_ge(sem["full"], value("full", "kvq", L, NT - 1))
                for tt in range(NT):
                    evict(KVR[:, tt, :], "kvq", L, tt)
                for i in range(3):
                    act.wait_ge(sem["full"], value("full", "tc2", L, i))
                    b = bank_of("tc2", L, i)
                    dst = CQH[:, i, :] if i < 2 else CKH[:]
                    nc.scalar.activation(dst, b[:], ACT.Identity, scale=vec(PQG + i)).then_inc(
                        sem["c_hi"], mark("c_hi", L, i))
                act.wait_ge(sem["full"], value("full", "tc2", L, 3))
                b = bank_of("tc2", L, 3)
                nc.scalar.activation(KPE[0:DH, :], b[0:DH, :], ACT.Copy)
                nc.scalar.activation(KPE[DH:P, :], b[0:DH, :], ACT.Copy).then_inc(
                    sem["read_act"], mark("read_act", "tc2", L, 3))
                split_through(("uv", L))
                for tt in range(NT):
                    for half in range(2):
                        evict(V2[:, tt, half * 512:(half + 1) * 512], "v", L, tt, half)
                for tt in range(NT):
                    evict(QRR[:, tt, :], "qr", L, tt, scale=float(QK) ** -0.5)
                split_through(("uqr", L))
                for h in range(2):
                    evict(QN[:, h, :], "qn", L, h, scale=float(QK) ** -0.5)
                for i in range(4):
                    evict(QRT[:, i, :], "tq", L, i)
                for u in range(len(UNITS2) + 4):
                    if u < len(UNITS2):
                        h, qt = UNITS2[u]
                        n = (qt + 1) * P
                        act.wait_ge(sem["nmax"], value("nmax", 2 + L, u))
                        if u >= 3:
                            act.wait_ge(sem["full"], value("full", "t", 2 + L, u - 3))
                        act.wait_ge(sem["full"], value("full", "s", 2 + L, u))
                        b = bank_of("s", 2 + L, u)
                        nc.scalar.activation(P2[:, u % 3, 0:n], b[:, 0:n], ACT.Exp,
                                             bias=nmax[:, u % 8:u % 8 + 1],
                                             accum_out=rsum[:, u % 8:u % 8 + 1]).then_inc(
                            sem["read_act"], mark("read_act", "s", 2 + L, u))
                    v = u - 2
                    if 0 <= v < len(UNITS2) and v % 2 == 0:
                        h, qt = UNITS2[v]
                        if h >= 2:
                            act.wait_ge(sem["full"], value("full", "o", 2 + L, h - 2))
                        act.wait_ge(sem["full"], value("full", "t", 2 + L, v))
                        b = bank_of("t", 2 + L, v)
                        n = (qt + 1) * P
                        nc.scalar.activation(
                       PT2[:, h % 2, 0:qt + 1, qt * P:(qt + 1) * P],
                       b[:, 0:n].rearrange("p (k q) -> p k q", k=qt + 1), ACT.Copy).then_inc(
                            sem["read_act"], mark("read_act", "t", 2 + L, v))
                    if u >= 6 and (u - 6) % 4 == 0 and (u - 6) // 4 < HEADS:
                        h = (u - 6) // 4
                        act.wait_ge(sem["y_full"], value("y_full", L, h))
                        nc.scalar.activation(YH[:, h, :], YT[:, h % 2, :], ACT.Copy).then_inc(
                            sem["y_hi"], mark("y_hi", L, h))
                    if u < len(UNITS2):
                        h, qt = UNITS2[u]
                        if qt == 1 and 1 <= h < HEADS - 1:
                            split_through(("hd", L, (h + 1) // 2))
                            act.wait_ge(sem["full"], value("full", "s", 2 + L, 4 * (h - 1) + 3))
                            evict(QN[:, (h + 1) % 2, :], "qn", L, h + 1, scale=float(QK) ** -0.5)
                for n in range(KD):
                    split_through(("o2", L, n))
                    act.wait_ge(sem["x_new"], value("x_new", f"f{L}", n))
                    square(f"f{L}", n, SQT)
                norm_hi(f"f{L}", NTMP, mod[:, L, 3 * KD:4 * KD])
                for half in range(2):
                    for f in range(half * FH, half * FH + FH):
                        split_through(("fg", L, f))
                        if f >= 2:
                            act.wait_ge(sem["hid"], value("hid", L, f - 2))
                        evict(SILU[:, f % 2, :], "fg", L, f, func=ACT.Silu)
                        split_through(("fu", L, f))
                        act.wait_ge(sem["hid"], value("hid", L, f))
                        nc.scalar.activation(HDH[:, f % FH, :], HF[:, f % 2, :], ACT.Copy).then_inc(
                            sem["hid_hi"], mark("hid_hi", L, f))
                    for n in range(KD):
                        split_through(fo_slot(L, half, n))
                        if half == 1:
                            tag = next_norm(L)
                            act.wait_ge(sem["x_new"], value("x_new", tag, n))
                            square(tag, n, SQT)
                        else:
                            act.wait_ge(sem["x_half"], value("x_half", L, n))

        @block.vector
        def _(dve):
            V = nc.vector
            ada_next = [0]
            ada_list = [k for k in STREAM if k[0] == "ada"]

            def ada_through(key):
                while ada_next[0] < len(ada_list) and SLOT[ada_list[ada_next[0]]] <= SLOT[key] + 1:
                    ada_one()

            def ada_one():
                k = ada_list[ada_next[0]]
                _, layer, i = k
                cb, r = divmod(i, 8)
                acc = ACC[:, cb % 2, :]
                c = vec1[:, 2 * KD + r:2 * KD + r + 1]
                dve.wait_ge(landed[ring(k)], loads(k))
                if r == 0:
                    if cb >= 2:
                        dve.wait_ge(sem["full"], value("full", "mod", layer, cb - 2))
                    elif layer:
                        dve.wait_ge(sem["full"], value("full", "mod", layer - 1, ADA // 8 - 2 + cb))
                    ins = V.tensor_scalar(acc, raw(k)[:], c, None, ALU.mult)
                else:
                    dve.wait_ge(sem["ada"], value("ada", layer, i - 1))
                    ins = V.scalar_tensor_tensor(out=acc, in0=raw(k)[:], scalar=c, in1=acc, op0=ALU.mult,
                                                 op1=ALU.add)
                ins.then_inc(sem["ada"], mark("ada", layer, i))
                ada_next[0] += 1

            def mods(key):
                for layer, cb in MODS.get(key, ()):
                    dve.wait_ge(sem["full"], value("full", "mod", layer, cb))
                    b = bank_of("mod", layer, cb)
                    V.tensor_tensor(mod[:, layer, 8 * cb:8 * cb + 8], b[:, 0:8],
                                    par[:, layer, PB_ADA + 8 * cb:PB_ADA + 8 * cb + 8], ALU.add).then_inc(
                        sem["read_dve"], mark("read_dve", "mod", layer, cb))
                    if cb == ADA // 8 - 1:
                        dve.wait_ge(sem["read_dve"], value("read_dve", "mod", layer, cb))
                        V.tensor_scalar(sc1[:, layer, 0, :], mod[:, layer, KD:2 * KD], 1.0, None, ALU.add)
                        V.tensor_scalar(sc1[:, layer, 1, :], mod[:, layer, 4 * KD:5 * KD], 1.0, None,
                                        ALU.add).then_inc(step, 1)
                        dve.wait_ge(step, own())

            def rsqrt(y, v, t):
                V.tensor_scalar(y.bitcast(I32), v.bitcast(I32), 1, None, ALU.arith_shift_right).then_inc(
                    step, 1)
                dve.wait_ge(step, own())
                V.tensor_scalar(y.bitcast(I32), y.bitcast(I32), -1.0, float(0x5F3759DF), ALU.mult, ALU.add).then_inc(
                    step, 1)
                dve.wait_ge(step, own())
                for _ in range(3):
                    V.tensor_tensor(t, y, y, ALU.mult).then_inc(step, 1)
                    dve.wait_ge(step, own())
                    V.scalar_tensor_tensor(out=t, in0=t, scalar=-0.5, in1=v, op0=ALU.mult, op1=ALU.mult).then_inc(
                        step, 1)
                    dve.wait_ge(step, own())
                    V.scalar_tensor_tensor(out=y, in0=t, scalar=1.5, in1=y, op0=ALU.add, op1=ALU.mult).then_inc(
                        step, 1)
                    dve.wait_ge(step, own())

            def norm(tag, tmp, gain, shift):
                dve.wait_ge(sem["full"], value("full", "ss", tag))
                b = bank_of("ss", tag)
                V.tensor_scalar(stat[:, 0, :], b[:, 0:NT], 1.0 / D, EPS, ALU.mult, ALU.add).then_inc(
                    sem["read_dve"], mark("read_dve", "ss", tag))
                dve.wait_ge(sem["read_dve"], value("read_dve", "ss", tag))
                rsqrt(stat[:, 1, :], stat[:, 0, :], stat[:, 2, :])
                note[("rstd", tag)] = count["step"]
                dve.wait_ge(sem["full"], value("full", "rb", tag))
                b = bank_of("rb", tag)
                for k in range(KD + 1):
                    if k < KD:
                        dst = tmp(k)
                        if k >= 2 and tag != "fin":
                            dve.wait_ge(sem["h_lo"], value("h_lo", tag, k - 2))
                        ins = V.scalar_tensor_tensor(out=dst, in0=X[:, k, :], scalar=gain[:, k:k + 1], in1=b[:],
                                                     op0=ALU.mult, op1=ALU.mult)
                        ins.then_inc(sem["normed"], mark("normed", tag, k))
                    if k and tag != "fin":
                        dve.wait_ge(sem["h_hi"], value("h_hi", tag, k - 1))
                        if shift is None:
                            ins = V.tensor_tensor(HL[:, k - 1, :], tmp(k - 1), HH[:, k - 1, :].bitcast(F32),
                                                  ALU.subtract)
                        else:
                            ins = V.scalar_tensor_tensor(out=HL[:, k - 1, :], in0=tmp(k - 1),
                                                         scalar=shift[:, k - 1:k],
                                                         in1=HH[:, k - 1, :].bitcast(F32), op0=ALU.add,
                                                         op1=ALU.subtract)
                        ins.then_inc(sem["h_lo"], mark("h_lo", tag, k - 1))

            def tables(tab, cs, row, scale, parts=P):
                nt = cs.shape[2]
                g = [spread(gains[0:parts, row, HALF * i:HALF * i + HALF], "p (o d) -> p o d", [parts, nt, HALF])
                     for i in range(2)]
                for out, src, s, gi in ((tab[:, 0, :, 0:HALF], 0, scale, 0), (tab[:, 0, :, HALF:DH], 0, scale, 1),
                                        (tab[:, 1, :, 0:HALF], 1, -scale, 1), (tab[:, 1, :, HALF:DH], 1, scale, 0)):
                    last = V.scalar_tensor_tensor(out=out, in0=cs[:, src], scalar=s, in1=g[gi], op0=ALU.mult,
                                                  op1=ALU.mult)
                last.then_inc(step, 1)
                dve.wait_ge(step, own())

            def rope(x, cos, sin, rstd, t0, t1, out=None):
                V.tensor_tensor(t0, x, cos, ALU.mult)
                V.tensor_tensor(t1[:, :, :, 0:HALF], x[:, :, :, HALF:DH], sin[:, :, :, 0:HALF], ALU.mult)
                V.tensor_tensor(t1[:, :, :, HALF:DH], x[:, :, :, 0:HALF], sin[:, :, :, HALF:DH], ALU.mult).then_inc(
                    step, 1)
                dve.wait_ge(step, own())
                out = x if out is None else out
                if rstd is None:
                    V.tensor_tensor(out, t0, t1, ALU.add).then_inc(step, 1)
                    dve.wait_ge(step, own())
                else:
                    V.tensor_tensor(t0, t0, t1, ALU.add).then_inc(step, 1)
                    dve.wait_ge(step, own())
                    V.tensor_tensor(out, t0, rstd, ALU.mult).then_inc(step, 1)
                    dve.wait_ge(step, own())

            def tmp4(i, x4, buf=None):
                _, A, B, _ = x4.shape
                return (TMP[:, i, :] if buf is None else buf)[0:x4.shape[0], 0:A * B * DH].rearrange(
                    "p (a b d) -> p a b d", a=A, b=B)

            def rope_tok(x4, tab, t0, A, B, rstd=None, bufs=(None, None)):
                shape = [P, A, B, DH]
                cos = spread(tab[:, 0, t0:t0 + A, :], "p a (o d) -> p a o d", shape)
                sin = spread(tab[:, 1, t0:t0 + A, :], "p a (o d) -> p a o d", shape)
                rope(x4, cos, sin, rstd, tmp4(0, x4, bufs[0]), tmp4(1, x4, bufs[1]))

            def head_rstd(x4, col, n):
                t0 = tmp4(0, x4)
                V.tensor_tensor(t0, x4, x4, ALU.mult).then_inc(step, 1)
                dve.wait_ge(step, own())
                _, A, B, _ = x4.shape
                V.tensor_reduce(kst[:, 0, col:col + n].rearrange("p (a b) -> p a b", a=A), t0, AX_X, ALU.add).then_inc(
                    step, 1)
                dve.wait_ge(step, own())

            def finish_rstd(n, width=DH):
                V.tensor_scalar(kst[:, 0, 0:n], kst[:, 0, 0:n], 1.0 / width, EPS, ALU.mult, ALU.add).then_inc(
                    step, 1)
                dve.wait_ge(step, own())
                rsqrt(kst[:, 1, 0:n], kst[:, 0, 0:n], kst[:, 2, 0:n])

            def out_head(L, h):
                dve.wait_ge(sem["full"], value("full", "o", 2 + L, h))
                b = bank_of("o", 2 + L, h)
                V.tensor_tensor(YT[:, h % 2, :], SG[:, h, :], b[:], ALU.mult).then_inc(
                    sem["yb"], mark("yb", L, h))
                dve.wait_ge(sem["yb"], value("yb", L, h))
                V.tensor_tensor(YT[:, h % 2, :], YT[:, h % 2, :], YA[:, h, :], ALU.add).then_inc(
                    sem["y_full"], mark("y_full", L, h))
                dve.wait_ge(sem["y_hi"], value("y_hi", L, h))
                V.tensor_tensor(YL[:, h, :], YT[:, h % 2, :], YH[:, h, :].bitcast(F32), ALU.subtract).then_inc(
                    sem["y_lo"], mark("y_lo", L, h))

            dve.wait_ge(sem["consts"], value("consts", "all"))
            V.tensor_copy(identb[:], ident[:])
            V.tensor_copy(causal[:], ACC[:, 0, 0:P])
            V.tensor_scalar(reset[:], ACC[:, 1, 0:S].bitcast(I32), 0.0, None, ALU.is_equal)
            V.tensor_scalar(keep[:], ACC[:, 1, 0:S].bitcast(I32), 0.0, None, ALU.not_equal).then_inc(step, 1)
            dve.wait_ge(step, own())
            note[("setup",)] = count["step"]
            norm("n1", lambda k: TMP[:, k % 2, :], vec1[:, 0:KD], None)

            dve.wait_ge(sem["lru_par"], value("lru_par", 1))
            V.tensor_scalar(lt[:, 2], lt[:, 1], 1.0, None, ALU.add).then_inc(sem["lru_w"], mark("lru_w"))
            dve.wait_ge(sem["lru_w"], value("lru_w"))
            V.tensor_scalar(lt[:, 4], lt[:, 2], -1.0, None, ALU.add).then_inc(step, 1)
            dve.wait_ge(step, own())
            V.tensor_scalar(lt[:, 5], lt[:, 4], 0.0, None, ALU.is_equal).then_inc(step, 1)
            dve.wait_ge(step, own())
            V.tensor_tensor(lt[:, 4], lt[:, 4], lt[:, 5], ALU.add).then_inc(step, 1)
            dve.wait_ge(step, own())
            V.reciprocal(lt[:, 4], lt[:, 4]).then_inc(step, 1)
            dve.wait_ge(step, own())
            dve.wait_ge(sem["lru_par"], value("lru_par", 2))
            V.tensor_tensor(lt[:, 3], lt[:, 3], lt[:, 5], ALU.add).then_inc(step, 1)
            dve.wait_ge(step, own())
            V.tensor_tensor(lt[:, 4], lt[:, 4], lt[:, 1], ALU.mult).then_inc(step, 1)
            dve.wait_ge(step, own())
            V.tensor_tensor(lt[:, 4], lt[:, 4], lt[:, 3], ALU.mult).then_inc(step, 1)
            dve.wait_ge(step, own())
            V.tensor_scalar(lt[:, 0], par[:, :, PA:PA + KD], -1.0, 0.0, ALU.mult, ALU.max).then_inc(step, 1)
            dve.wait_ge(step, own())
            V.tensor_tensor(lt[:, 4], lt[:, 4], lt[:, 0], ALU.add).then_inc(step, 1)
            dve.wait_ge(step, own())
            V.tensor_scalar(csc[:], lt[:, 4], -LRU_C, None, ALU.mult).then_inc(step, 1)
            dve.wait_ge(step, own())
            note[("csc",)] = count["step"]

            tables(TAB, CS1, G_ONE, DH ** -0.5)
            for t in range(0, NT, 2):
                dve.wait_ge(sem["read_act"], value("read_act", "p1", 0, t + 1))
                rope_tok(MISC[:, t:t + 2, 0:256].rearrange("p a (b d) -> p a b d", d=DH), TAB, t, 2, 4)
            tables(TAB, CS1, G_ONE, 1.0)
            rope_tok(MISC[:, :, 256:384].rearrange("p a (b d) -> p a b d", d=DH), TAB, 0, NT, 2)
            note[("roped", 0)] = count["step"]

            V.tensor_copy(posf[:], posi[:]).then_inc(step, 1)
            dve.wait_ge(step, own())
            ang = TMP[:, 0, 0:P].rearrange("p (t f) -> p t f", t=NT)
            turn = TMP[:, 0, P:2 * P].rearrange("p (t f) -> p t f", t=NT)
            red = TMP[:, 0, 2 * P:3 * P].rearrange("p (t f) -> p t f", t=NT)
            for t in range(NT):
                last = V.tensor_scalar(ang[:, t, :], freq[:], posf[:, t:t + 1], None, ALU.mult)
            last.then_inc(step, 1)
            dve.wait_ge(step, own())
            c1, c2, c3 = 6.28125, 0.00193500518798828125, 3.0176e-07
            c2 = float(np.float32(round((2 * math.pi - c1) * 2 ** 18) / 2 ** 18))
            c3 = float(np.float32(round((2 * math.pi - c1 - c2) * 2 ** 30) / 2 ** 30))
            c4 = 2 * math.pi - c1 - c2 - c3
            big = float(3 * 2 ** 22)
            for i, quarter in ((1, 0.0), (0, 0.25)):
                V.tensor_scalar(turn, ang, 1.0 / (2 * math.pi), quarter, ALU.mult, ALU.add).then_inc(step, 1)
                dve.wait_ge(step, own())
                V.tensor_scalar(turn, turn, big, None, ALU.add).then_inc(step, 1)
                dve.wait_ge(step, own())
                V.tensor_scalar(turn, turn, -big, None, ALU.add).then_inc(step, 1)
                dve.wait_ge(step, own())
                V.scalar_tensor_tensor(out=red, in0=turn, scalar=-c1, in1=ang, op0=ALU.mult, op1=ALU.add).then_inc(
                    step, 1)
                dve.wait_ge(step, own())
                for c in (c2, c3, c4):
                    V.scalar_tensor_tensor(out=red, in0=turn, scalar=-c, in1=red, op0=ALU.mult, op1=ALU.add).then_inc(
                        step, 1)
                    dve.wait_ge(step, own())
                if quarter:
                    V.tensor_scalar(red, red, math.pi / 2, None, ALU.add).then_inc(step, 1)
                    dve.wait_ge(step, own())
                V.tensor_scalar(cs2[:, i], red, 3.1415925, -3.1415925, ALU.min, ALU.max).then_inc(step, 1)
                dve.wait_ge(step, own())
            note[("angles",)] = count["step"]

            def rope_keys():
                for i, row in enumerate((G_KS, G_KW, G_KD)):
                    x4 = G[1][:, :, i * P:(i + 1) * P].rearrange("p a (b d) -> p a b d", d=DH)
                    if i == 0:
                        dve.wait_ge(sem["read_act"], value("read_act", "p1", 1, 3))
                    head_rstd(x4, 8 * i, 8)
                finish_rstd(24)
                for i, row in enumerate((G_KS, G_KW, G_KD)):
                    x4 = G[1][:, :, i * P:(i + 1) * P].rearrange("p a (b d) -> p a b d", d=DH)
                    tables(TAB, CS1, row, 1.0)
                    r = spread(kst[:, 1, 8 * i:8 * i + 8].rearrange("p (a b) -> p a b", a=NT),
                               "p a (b o) -> p a b o", [P, NT, 2, DH])
                    rope_tok(x4, TAB, 0, NT, 2, r)
                note[("roped", 1)] = count["step"]

            def rope_queries(g, row):
                tables(TAB, CS1, row, DH ** -0.5)
                x4 = [G[g][:, t:t + 1, :].rearrange("p a (b d) -> p a b d", d=DH) for t in range(NT)]
                for t in range(NT):
                    dve.wait_ge(sem["read_act"], value("read_act", "p1", g, t))
                    head_rstd(x4[t], 8 * t, 8)
                finish_rstd(32)
                for t in range(NT):
                    r = spread(kst[:, 1, 8 * t:8 * t + 8].rearrange("p (a b) -> p a b", a=1),
                               "p a (b o) -> p a b o", [P, 1, 8, DH])
                    rope_tok(x4[t], TAB, t, 1, 8, r)
                note[("roped", g)] = count["step"]

            def index_scores(qt):
                n = (qt + 1) * P
                dve.wait_ge(sem["full"], value("full", "idx", qt, 0))
                b = bank_of("idx", qt, 0)
                V.tensor_scalar(SCORE[:, 0:n], b[:, 0:n], 0.0, gate[:, qt, 24:25], ALU.max, ALU.mult).then_inc(
                    sem["read_dve"], mark("read_dve", "idx", qt, 0))
                dve.wait_ge(sem["read_dve"], value("read_dve", "idx", qt, 0))
                for h in range(1, 4):
                    dve.wait_ge(sem["read_act"], value("read_act", "idx", qt, h))
                    V.scalar_tensor_tensor(out=SCORE[:, 0:n], in0=RELU[:, h - 1, 0:n],
                                           scalar=gate[:, qt, 24 + h:25 + h], in1=SCORE[:, 0:n],
                                           op0=ALU.mult, op1=ALU.add).then_inc(
                        sem["iscore"], mark("iscore", qt, h))
                    dve.wait_ge(sem["iscore"], value("iscore", qt, h))
                V.tensor_tensor(SCORE[:, n - P:n], SCORE[:, n - P:n], causal[:], ALU.add).then_inc(step, 1)
                dve.wait_ge(step, own())
                V.tensor_scalar(SCORE[:, 0:n], SCORE[:, 0:n], 0.0, None, ALU.add).then_inc(step, 1)
                dve.wait_ge(step, own())

            def take_topk(qt, keys):
                n = (qt + 1) * P
                for r in range(TOPK // 8):
                    V.max(TKM[:], SCORE[:, 0:n]).then_inc(step, 1)
                    dve.wait_ge(step, own())
                    V.match_replace(SCORE[:, 0:n], TKM[:], SCORE[:, 0:n], TAKEN).then_inc(step, 1)
                    dve.wait_ge(step, own())
                    if r % 3 == 2 and keys:
                        ada_through(keys.pop(0))
                V.tensor_scalar(MASKB[:, qt - 1, 0:n], SCORE[:, 0:n], TAKEN, NEG, ALU.not_equal, ALU.mult).then_inc(
                    sem["topk"], mark("topk", qt))
                dve.wait_ge(sem["topk"], value("topk", qt))

            ada_through(("p1", 1, 3))
            mods(("p1", 1, 3))
            rope_keys()
            ada_through(("p1", 4, 3))
            mods(("p1", 4, 3))
            index_scores(1)
            take_topk(1, [("p1", 2, 1), ("p1", 2, 2), ("p1", 2, 3)])
            ada_through(("p1", 2, 3))
            mods(("p1", 2, 3))
            index_scores(2)
            rope_queries(2, G_Q)
            take_topk(2, [("p1", 3, 1), ("p1", 3, 2), ("p1", 3, 3)])
            ada_through(("p1", 3, 3))
            mods(("p1", 3, 3))
            index_scores(3)
            take_topk(3, [("p1", 5, 0), ("p1", 5, 1), ("p1", 5, 2), ("p1", 5, 3)])
            ada_through(("p1", 5, 3))
            rope_queries(3, G_QD)
            dve.wait_ge(sem["read_act"], value("read_act", "co", 0))
            C = 2 * NCMP
            c4 = CK[0:C, 0:1, :].rearrange("p a (b d) -> p a b d", b=1)
            V.tensor_tensor(CK[0:C, 1, :], CK[0:C, 0, :], CK[0:C, 0, :], ALU.mult).then_inc(step, 1)
            dve.wait_ge(step, own())
            V.tensor_reduce(kst[0:C, 0, 0:1], CK[0:C, 1, :], AX_X, ALU.add).then_inc(step, 1)
            dve.wait_ge(step, own())
            V.tensor_scalar(kst[0:C, 0, 0:1], kst[0:C, 0, 0:1], 1.0 / DH, EPS, ALU.mult, ALU.add).then_inc(
                step, 1)
            dve.wait_ge(step, own())
            rsqrt(kst[0:C, 1, 0:1], kst[0:C, 0, 0:1], kst[0:C, 2, 0:1])
            tables(TAB[0:C, :, 0:1], cscmp[0:C].rearrange("p c (o f) -> p c o f", o=1), G_KC, 1.0, parts=C)
            rope(c4, TAB[0:C, 0:1, 0:1, :], TAB[0:C, 1:2, 0:1, :], None,
                 CK[0:C, 1:2, :].rearrange("p a (b d) -> p a b d", b=1),
                 CK[0:C, 2:3, :].rearrange("p a (b d) -> p a b d", b=1))
            V.tensor_scalar(CK[0:C, 0, :], CK[0:C, 0, :], kst[0:C, 1, 0:1], None, ALU.mult).then_inc(step, 1)
            dve.wait_ge(step, own())
            note[("cmp_key",)] = count["step"]
            mods(("p1", 5, 3))
            ada_through(("p1", 6, 3))
            mods(("p1", 6, 3))
            for i in range(4):
                dve.wait_ge(sem["full"], value("full", "tqd", i))
                b = bank_of("tqd", i)
                V.tensor_copy(QDT[:, i, :], b[:]).then_inc(sem["read_dve"], mark("read_dve", "tqd", i))

            for qt in range(NT + 2):
                if qt < NT:
                    pc = PC[:, qt % 2]
                    if qt >= 2:
                        dve.wait_ge(sem["full"], value("full", "ct", qt - 2))
                    for g in range(2):
                        dve.wait_ge(sem["full"], value("full", "cs", qt, g))
                        b = bank_of("cs", qt, g)
                        V.tensor_tensor(pc[:, 4 * g:4 * g + 4], b[:, 0:P].rearrange("p (h c) -> p h c", c=NCMP),
                                        spread(cmask[:, qt, :], "p (o c) -> p o c", [P, 4, NCMP]), ALU.add).then_inc(
                            sem["read_dve"], mark("read_dve", "cs", qt, g))
                    dve.wait_ge(sem["read_dve"], value("read_dve", "cs", qt, 1))
                    V.tensor_reduce(CST[:, 0, :], pc, AX_X, ALU.max).then_inc(step, 1)
                    dve.wait_ge(step, own())
                    V.tensor_tensor(pc, pc, spread(CST[:, 0, :], "p (h o) -> p h o", [P, 8, NCMP]),
                                    ALU.subtract).then_inc(sem["cmp_shift"], mark("cmp_shift", qt))
                    dve.wait_ge(sem["cmp_exp"], value("cmp_exp", qt))
                    V.tensor_reduce(CST[:, 1, :], pc, AX_X, ALU.add).then_inc(step, 1)
                    dve.wait_ge(step, own())
                    V.reciprocal(CST[:, 2, :], CST[:, 1, :]).then_inc(step, 1)
                    dve.wait_ge(step, own())
                    V.scalar_tensor_tensor(
                    out=CST[:, 3, :], in0=CST[:, 2, :], scalar=cvalid[:, qt:qt + 1],
                    in1=gate[:, qt, 0:24].rearrange("p (h b) -> p h b", b=3)[:, :, 0], op0=ALU.mult,
                    op1=ALU.mult).then_inc(step, 1)
                    dve.wait_ge(step, own())
                    V.tensor_tensor(pc, pc, spread(CST[:, 3, :], "p (h o) -> p h o", [P, 8, NCMP]),
                                    ALU.mult).then_inc(sem["cmp_p"], mark("cmp_p", qt))
                v = qt - 2
                if v >= 0:
                    dve.wait_ge(sem["full"], value("full", "cpv", v))
                    b = bank_of("cpv", v)
                    V.tensor_copy(MIX[:, v, 0:512], b[:]).then_inc(sem["read_dve"], mark("read_dve", "cpv", v))

            nU = len(UNITS1)
            for u in range(nU + 3):
                if u in O1_ADAS:
                    ada_one()
                if u < nU:
                    n = (UNITS1[u][3] + 1) * P
                    dve.wait_ge(sem["full"], value("full", "s", 1, u))
                    b = bank_of("s", 1, u)
                    V.tensor_reduce(nmax[:, u % 8:u % 8 + 1], b[:, 0:n], AX_X, ALU.max, negate=True).then_inc(
                        sem["nmax"], mark("nmax", 1, u))
                v = u - 2
                if 0 <= v < nU and v % 2 == 1:
                    n = (UNITS1[v][3] + 1) * P
                    dve.wait_ge(sem["full"], value("full", "t", 1, v))
                    b = bank_of("t", 1, v)
                    dve.wait_ge(sem["full"], value("full", *(("o", 1, v - 3) if v >= 3 else ("cpv", 3))))
                    V.tensor_copy(PT1[:, v % 3, 0:n], b[:, 0:n]).then_inc(
                        sem["read_dve"], mark("read_dve", "t", 1, v))
                v = u - 3
                if v >= 0:
                    br, j, g, qt = UNITS1[v]
                    head = 4 * g + j
                    cc = coef[:, v % 8:v % 8 + 1]
                    dve.wait_ge(sem["read_act"], value("read_act", "s", 1, v))
                    V.reciprocal(cc, rsum[:, v % 8:v % 8 + 1]).then_inc(step, 1)
                    dve.wait_ge(step, own())
                    dve.wait_ge(sem["full"], value("full", "o", 1, v))
                    b = bank_of("o", 1, v)
                    if br < 2:
                        V.tensor_tensor(cc, cc, gate[:, qt, 3 * head + 1 + br:3 * head + 2 + br], ALU.mult).then_inc(
                            step, 1)
                        dve.wait_ge(step, own())
                        dst = MIX[:, qt, head * DH:(head + 1) * DH]
                        V.scalar_tensor_tensor(out=dst, in0=b[:, 0:DH], scalar=cc, in1=dst, op0=ALU.mult,
                                               op1=ALU.add).then_inc(
                            sem["read_dve"], mark("read_dve", "o", 1, v))
                    else:
                        dst = MIX[:, qt, (8 + head) * DH:(9 + head) * DH]
                        V.tensor_scalar(dst, b[:, 0:DH], cc, None, ALU.mult).then_inc(
                            sem["read_dve"], mark("read_dve", "o", 1, v))
            for i in range(KD):
                dve.wait_ge(sem["full"], value("full", "tm", i))
                b = bank_of("tm", i)
                dve.wait_ge(sem["mix_hi"], value("mix_hi", i))
                V.tensor_tensor(HL[:, i, :], b[:], HH[:, i, :].bitcast(F32), ALU.subtract).then_inc(
                    sem["read_dve"], mark("read_dve", "tm", i))
            for n in range(KD):
                ada_through(("o1", n))
                dve.wait_ge(sem["full"], value("full", "o1", n))
                b = bank_of("o1", n)
                V.tensor_tensor(X[:, n, :], X[:, n, :], b[:], ALU.add).then_inc(
                    sem["x_new"], mark("x_new", "m0", n))
                mods(("o1", n)) if n < KD - 1 else None
            ada_through(("xl", 0, 0))
            mods(("o1", KD - 1))

            for layer in range(LAYERS):
                L = layer

                def vec(col):
                    return par[:, L, col:col + 1]

                norm(f"m{L}", lambda k: NTMP[:, k % 2, :], sc1[:, L, 0, :], mod[:, L, 0:KD])
                for n in range(KD):
                    dve.wait_ge(sem["full"], value("full", "xl", L, n))
                    b = bank_of("xl", L, n)
                    xc = XC[:, n, :]
                    V.tensor_scalar(xc, b[:], vec(PCONV_W + 4 * n + 3), vec(PCONV_B + n), ALU.mult, ALU.add).then_inc(
                        step, 1)
                    dve.wait_ge(step, own())
                    for d in range(1, 4):
                        ins = V.scalar_tensor_tensor(out=xc[:, d:S], in0=b[:, 0:S - d],
                                                     scalar=vec(PCONV_W + 4 * n + 3 - d), in1=xc[:, d:S],
                                                     op0=ALU.mult, op1=ALU.add)
                        if d < 3:
                            ins.then_inc(step, 1)
                            dve.wait_ge(step, own())
                    ins.then_inc(sem["conv"], mark("conv", L, n))
                    note[("conv", L, n)] = count["conv"]
                    dve.wait_ge(sem["xc_hi"], value("xc_hi", L, n))
                    V.tensor_tensor(XCL[:, n % 2, :], xc, XCH[:, n % 2, :].bitcast(F32), ALU.subtract).then_inc(
                        sem["xc_lo"], mark("xc_lo", L, n))
                for n in range(KD):
                    dve.wait_ge(sem["lru_a"], value("lru_a", L, n))
                    V.tensor_tensor(YT[:, n % 2, :], LR[:, n, :], LR[:, n, :], ALU.mult).then_inc(step, 1)
                    dve.wait_ge(step, own())
                    V.scalar_tensor_tensor(out=YA[:, n, :], in0=YT[:, n % 2, :], scalar=1.0, in1=YA[:, n, :],
                                           op0=ALU.add, op1=ALU.mult).then_inc(
                        sem["one_aa"], mark("one_aa", L, n))
                for n in range(KD):
                    if n == 0:
                        dve.wait_ge(sem["read_act"], value("read_act", "li", L, KD - 1))
                    V.tensor_tensor(LR[:, n, :], LR[:, n, :], keep[:], ALU.mult)
                    V.tensor_tensor(XC[:, n, :], XC[:, n, :], LI[:, n, :], ALU.mult).then_inc(step, 1)
                    dve.wait_ge(step, own())
                    dve.wait_ge(sem["mult"], value("mult", L, n))
                    V.tensor_tensor(YA[:, n, :], YA[:, n, :], reset[:], ALU.max).then_inc(step, 1)
                    dve.wait_ge(step, own())
                    V.tensor_tensor(XC[:, n, :], XC[:, n, :], YA[:, n, :], ALU.mult).then_inc(step, 1)
                    dve.wait_ge(step, own())
                    V.tensor_tensor_scan(YA[:, n, :], LR[:, n, :], XC[:, n, :], 0.0, ALU.mult, ALU.add).then_inc(
                        step, 1)
                    dve.wait_ge(step, own())
                    if n >= 4:
                        dve.wait_ge(sem["read_act"], value("read_act", "ga", L, n))
                    V.tensor_tensor(YA[:, n, :], YA[:, n, :], SG[:, n, :], ALU.mult).then_inc(
                        sem["ya_gated"], mark("ya_gated", L, n))
                dve.wait_ge(sem["read_act"], value("read_act", "kvq", L, NT - 1))
                for t in range(NT):
                    sq = YT[:, 0, 0:384]
                    V.tensor_tensor(sq, KVR[:, t, 0:384], KVR[:, t, 0:384], ALU.mult).then_inc(step, 1)
                    dve.wait_ge(step, own())
                    V.tensor_reduce(kst[:, 0, t:t + 1], sq[:, 0:Q_RANK], AX_X, ALU.add)
                    V.tensor_reduce(kst[:, 0, NT + t:NT + t + 1], sq[:, Q_RANK:384], AX_X, ALU.add).then_inc(
                        step, 1)
                    dve.wait_ge(step, own())
                V.tensor_scalar(kst[:, 0, 0:NT], kst[:, 0, 0:NT], 1.0 / Q_RANK, EPS, ALU.mult, ALU.add)
                V.tensor_scalar(kst[:, 0, NT:2 * NT], kst[:, 0, NT:2 * NT], 1.0 / KV_RANK, EPS, ALU.mult,
                                ALU.add).then_inc(step, 1)
                dve.wait_ge(step, own())
                rsqrt(kst[:, 1, 0:2 * NT], kst[:, 0, 0:2 * NT], kst[:, 2, 0:2 * NT])
                for t in range(NT):
                    V.tensor_scalar(KVR[:, t, 0:Q_RANK], KVR[:, t, 0:Q_RANK], kst[:, 1, t:t + 1], None, ALU.mult)
                    ins = V.tensor_scalar(KVR[:, t, Q_RANK:384], KVR[:, t, Q_RANK:384],
                                          kst[:, 1, NT + t:NT + t + 1], None, ALU.mult)
                ins.then_inc(step, 1)
                dve.wait_ge(step, own())
                dve.wait_ge(sem["cos_sin"], value("cos_sin"))
                V.tensor_copy(TAB2[:, 0, :, 0:HALF], cs2[:, 0])
                V.tensor_copy(TAB2[:, 0, :, HALF:DH], cs2[:, 0])
                V.tensor_scalar(TAB2[:, 1, :, 0:HALF], cs2[:, 1], -1.0, None, ALU.mult)
                V.tensor_copy(TAB2[:, 1, :, HALF:DH], cs2[:, 1]).then_inc(step, 1)
                dve.wait_ge(step, own())
                rope_tok(KVR[:, :, 384:448].rearrange("p a (b d) -> p a b d", b=1), TAB2, 0, NT, 1,
                         bufs=(YT[:, 0, :], YT[:, 1, :]))
                note[("latents", L)] = count["step"]
                for i in range(3):
                    dve.wait_ge(sem["full"], value("full", "tc2", L, i))
                    b = bank_of("tc2", L, i)
                    dve.wait_ge(sem["c_hi"], value("c_hi", L, i))
                    h_, l_ = (CQH[:, i, :], CQL[:, i, :]) if i < 2 else (CKH[:], CKL[:])
                    V.scalar_tensor_tensor(out=l_, in0=b[:], scalar=vec(PQG + i), in1=h_.bitcast(F32),
                                           op0=ALU.mult, op1=ALU.subtract).then_inc(
                        sem["read_dve"], mark("read_dve", "tc2", L, i))
                for t in range(NT):
                    dve.wait_ge(sem["read_act"], value("read_act", "qr", L, t))
                    rope_tok(QRR[:, t:t + 1, :].rearrange("p a (b d) -> p a b d", d=DH), TAB2, t, 1, 8,
                             bufs=(YT[:, 0, :], YT[:, 1, :]))
                note[("q_roped", L)] = count["step"]
                for h in range(2):
                    dve.wait_ge(sem["full"], value("full", "kn", L, h))
                    b = bank_of("kn", L, h)
                    V.tensor_copy(KN[:, h, :], b[:]).then_inc(sem["read_dve"], mark("read_dve", "kn", L, h))
                nU = len(UNITS2)
                for u in range(nU + 4):
                    if u < nU:
                        n = (UNITS2[u][1] + 1) * P
                        dve.wait_ge(sem["full"], value("full", "s", 2 + L, u))
                        b = bank_of("s", 2 + L, u)
                        V.tensor_reduce(nmax[:, u % 8:u % 8 + 1], b[:, 0:n], AX_X, ALU.max, negate=True).then_inc(
                            sem["nmax"], mark("nmax", 2 + L, u))
                    v = u - 1
                    if 0 <= v < nU:
                        n = (UNITS2[v][1] + 1) * P
                        cc = coef[:, v % 8:v % 8 + 1]
                        dve.wait_ge(sem["read_act"], value("read_act", "s", 2 + L, v))
                        V.reciprocal(cc, rsum[:, v % 8:v % 8 + 1]).then_inc(step, 1)
                        dve.wait_ge(step, own())
                        V.tensor_scalar(P2[:, v % 3, 0:n], P2[:, v % 3, 0:n], cc, None, ALU.mult).then_inc(
                            sem["p_norm"], mark("p_norm", 2 + L, v))
                    v = u - 2
                    if 0 <= v < nU and v % 2 == 1:
                        h, qt = UNITS2[v]
                        n = (qt + 1) * P
                        if h >= 2:
                            dve.wait_ge(sem["full"], value("full", "o", 2 + L, h - 2))
                        dve.wait_ge(sem["full"], value("full", "t", 2 + L, v))
                        b = bank_of("t", 2 + L, v)
                        V.tensor_copy(PT2[:, h % 2, 0:qt + 1, qt * P:(qt + 1) * P],
                                      b[:, 0:n].rearrange("p (k q) -> p k q", k=qt + 1)).then_inc(
                            sem["read_dve"], mark("read_dve", "t", 2 + L, v))
                    if u >= 6 and (u - 6) % 4 == 0 and (u - 6) // 4 < HEADS:
                        out_head(L, (u - 6) // 4)
                    if u < nU:
                        h, qt = UNITS2[u]
                        if qt == 1 and 1 <= h < HEADS - 1:
                            dve.wait_ge(sem["full"], value("full", "s", 2 + L, 4 * (h - 1) + 3))
                            dve.wait_ge(sem["full"], value("full", "kn", L, h + 1))
                            b = bank_of("kn", L, h + 1)
                            V.tensor_copy(KN[:, (h + 1) % 2, :], b[:]).then_inc(
                                sem["read_dve"], mark("read_dve", "kn", L, h + 1))
                for n in range(KD):
                    if n == 6:
                        ada_through(("fu", L, 0))
                    dve.wait_ge(sem["full"], value("full", "o2", L, n))
                    b = bank_of("o2", L, n)
                    V.scalar_tensor_tensor(out=X[:, n, :], in0=b[:], scalar=mod[:, L, 2 * KD + n:2 * KD + n + 1],
                                           in1=X[:, n, :], op0=ALU.mult, op1=ALU.add).then_inc(
                        sem["x_new"], mark("x_new", f"f{L}", n))
                norm(f"f{L}", lambda k: NTMP[:, k % 2, :], sc1[:, L, 1, :], mod[:, L, 3 * KD:4 * KD])
                for half in range(2):
                    for f in range(half * FH, half * FH + FH):
                        ada_through(("fu", L, f))
                        dve.wait_ge(sem["read_act"], value("read_act", "fg", L, f))
                        dve.wait_ge(sem["full"], value("full", "fu", L, f))
                        b = bank_of("fu", L, f)
                        V.tensor_tensor(HF[:, f % 2, :], SILU[:, f % 2, :], b[:], ALU.mult).then_inc(
                            sem["hid"], mark("hid", L, f))
                        dve.wait_ge(sem["hid_hi"], value("hid_hi", L, f))
                        V.tensor_tensor(HDL[:, f % FH, :], HF[:, f % 2, :], HDH[:, f % FH, :].bitcast(F32),
                                        ALU.subtract).then_inc(sem["hid_lo"], mark("hid_lo", L, f))
                        if L == 0:
                            mods(("fu", L, f))
                    for n in range(KD):
                        ada_through(fo_slot(L, half, n))
                        dve.wait_ge(sem["full"], value("full", "fo", L, half, n))
                        b = bank_of("fo", L, half, n)
                        ins = V.scalar_tensor_tensor(out=X[:, n, :], in0=b[:],
                                                     scalar=mod[:, L, 5 * KD + n:5 * KD + n + 1],
                                                     in1=X[:, n, :], op0=ALU.mult, op1=ALU.add)
                        if half:
                            ins.then_inc(sem["x_new"], mark("x_new", next_norm(L), n))
                        else:
                            ins.then_inc(sem["x_half"], mark("x_half", L, n))
                        if L == 0 and (n == KD - 1 or fo_slot(L, half, n + 1) != fo_slot(L, half, n)):
                            mods(fo_slot(L, half, n))
            norm("fin", lambda k: YA[:, k, :], vec1[:, KD:2 * KD], None)

        @block.tensor
        def _(pe):
            jobs, used_before = [], set()

            def claim(*key):
                j = len(jobs)
                jobs.append(key)
                note[("bank",) + key] = j % 8
                if j >= 8:
                    reader = last_reader(jobs[j - 8])
                    pe.wait_ge(sem[reader[0]], value(*reader))
                return bank[j % 8]

            def last_reader(key):
                kind = key[0]
                if kind in ("xl",):
                    return ("conv",) + key[1:]
                if kind == "o1":
                    return ("x_new", "m0", key[1])
                if kind == "o2":
                    return ("x_new", f"f{key[1]}", key[2])
                if kind == "fo":
                    return ("x_new", next_norm(key[1]), key[3]) if key[2] else ("x_half", key[1], key[3])
                if kind == "fu":
                    return ("hid",) + key[1:]
                if kind == "rb":
                    return ("normed", key[1], KD - 1)
                if kind == "o" and key[1] >= 2:
                    return ("yb", key[1] - 2, key[2])
                return ("read_dve",) + key if ("read_dve",) + key in known else ("read_act",) + key

            def full(ins, *key):
                return ins.then_inc(sem["full"], mark("full", *key))

            def used(key, family="full"):
                note[("used",) + key] = (family, count[family])

            def mm3(out, A, B, first, last):
                nc.tensor.matmul(out, A[0], B[0], start=first, stop=False)
                nc.tensor.matmul(out, A[0], B[1], start=False, stop=False)
                return nc.tensor.matmul(out, A[1], B[0], start=False, stop=last)

            def wpair(key, c0, n):
                return hi(key)[:, c0:c0 + n], lo(key)[:, c0:c0 + n]

            def dense(key, chunks, x):
                b = claim(*key)
                for i, (slot, col) in enumerate(chunks):
                    if i == 0 or slot != chunks[i - 1][0]:
                        pe.wait_ge(sem["passed"], value("passed", *slot))
                    last = mm3(b[:], wpair(slot, col, P), x(i), i == 0, i == len(chunks) - 1)
                full(last, *key)
                for slot in dict.fromkeys(s for s, _ in chunks):
                    used(slot)

            def first_use(*key):
                fresh = key not in used_before
                used_before.add(key)
                return fresh

            def h_pair(tag):
                def x(k):
                    if first_use("h", tag, k):
                        pe.wait_ge(sem["h_lo"], value("h_lo", tag, k))
                    return HH[:, k, :], HL[:, k, :]
                return x

            def tokens(kind, slots, width, tag):
                b = [claim(*kind, tt) for tt in range(NT)]
                for s, slot in enumerate(slots):
                    pe.wait_ge(sem["passed"], value("passed", *slot))
                    for tt in range(NT):
                        for c in range(2):
                            k = 2 * s + c
                            if first_use("h", tag, k):
                                pe.wait_ge(sem["h_lo"], value("h_lo", tag, k))
                            last = mm3(b[tt][:, 0:width],
                                       (HH[:, k, tt * P:(tt + 1) * P], HL[:, k, tt * P:(tt + 1) * P]),
                                       wpair(slot, 512 * c, width), k == 0, k == KD - 1)
                        if s == 3:
                            full(last, *kind, tt)
                    if s < 3:
                        last.then_inc(sem["w_used"], mark("w_used", *slot))
                        used(slot, "w_used")
                    else:
                        used(slot)

            def turn(key, srcs, rows=P):
                b = claim(*key)
                for tt, src in enumerate(srcs):
                    k = src.shape[0]
                    last = nc.tensor.transpose(b[0:rows, tt * k:(tt + 1) * k], src, ident[0:k, 0:k])
                full(last, *key)

            def norm(tag, total):
                pe.wait_ge(sem["sq_added"], value("sq_added", tag, KD - 1))
                pe.wait_ge(sem["consts"], value("consts", "all"))
                b = claim("ss", tag)
                for tt in range(NT):
                    last = nc.tensor.matmul(b[:, tt:tt + 1], total[:, tt * P:(tt + 1) * P], ones[:, 0:1],
                                            start=True, stop=True)
                full(last, "ss", tag)
                b = claim("rb", tag)
                pe.wait_ge(step, value("rstd", tag))
                for tt in range(NT):
                    last = nc.tensor.matmul(b[:, tt * P:(tt + 1) * P],
                                            stat[:, 1, tt:tt + 1].broadcast_to([P, P]), ident[:], start=True,
                                            stop=True)
                full(last, "rb", tag)

            def mods(key):
                for layer, cb in MODS.get(key, ()):
                    pe.wait_ge(sem["ada"], value("ada", layer, 8 * cb + 7))
                    b = claim("mod", layer, cb)
                    for c in range(8):
                        last = nc.tensor.matmul(b[:, c:c + 1], ACC[:, cb % 2, c * P:(c + 1) * P], ones[:, 0:1],
                                                start=True, stop=True)
                    full(last, "mod", layer, cb)

            def project(g):
                tokens(("p1", g), [("p1", g, s) for s in range(4)], 412 if g == 0 else 512, "n1")
                mods(("p1", g, 3))

            def index(qt):
                n = (qt + 1) * P
                for h in range(4):
                    pe.wait_ge(sem["read_act"], value("read_act", "ti", 2))
                    b = claim("idx", qt, h)
                    r = slice(DH * (h % 2), DH * (h % 2) + DH)
                    full(nc.tensor.matmul(b[:, 0:n], QIT[r, h // 2, qt * P:(qt + 1) * P], KIT[r, 0:n],
                                          start=True, stop=True), "idx", qt, h)

            def hidden(kv):
                pe.wait_ge(sem["ca"], value("ca", kv, 15))
                b = claim("hid", kv)
                for i in range(16):
                    slot = ("cw", kv, i // 4)
                    pe.wait_ge(landed[ring(slot)], loads(slot))
                    last = nc.tensor.matmul(b[0:2 * NCMP, 0:CMP_HID], CA[:, i, :],
                                            raw(slot)[:, (i % 4) * CMP_HID:(i % 4 + 1) * CMP_HID],
                                            start=(i == 0), stop=False)
                    if i % 4 == 3:
                        last.then_inc(sem["w_used"], mark("w_used", *slot))
                        used(slot, "w_used")
                full(nc.tensor.matmul(b[0:2 * NCMP, 0:CMP_HID], ones[0:1, 0:2 * NCMP], cb1[0:1, kv, :],
                                      start=False, stop=True), "hid", kv)

            norm("n1", SQS)
            project(0)
            project(1)
            pe.wait_ge(step, value("roped", 0))
            for i in range(3):
                turn(("ti", i), [MISC[:, tt, i * P:(i + 1) * P] for tt in range(NT)])
            project(4)
            index(1)
            pe.wait_ge(sem["read_act"], value("read_act", "p1", 1, 3))
            turn(("tc", 0), [G[1][:, tt, 384:512] for tt in range(NT)])
            project(2)
            index(2)
            hidden(0)
            pe.wait_ge(sem["read_act"], value("read_act", "p1", 4, 3))
            turn(("tc", 1), [G[4][:, tt, 384:512] for tt in range(NT)])
            project(3)
            hidden(1)
            index(3)
            for kv in range(2):
                pe.wait_ge(sem["read_act"], value("read_act", "hid", kv))
                b = claim("ht", kv)
                for c in range(2):
                    last = nc.tensor.transpose(b[:, 64 * c:64 * c + 64], HID[0:64, kv, c * P:(c + 1) * P],
                                               ident[0:64, 0:64])
                full(last, "ht", kv)
            for kv in range(2):
                pe.wait_ge(sem["read_act"], value("read_act", "ht", kv))
                b = claim("co", kv)
                for c in range(2):
                    last = nc.tensor.matmul(b[0:64, 0:DH], HIDT[:, kv, c, :], cw2[:, kv, c, :], start=(c == 0),
                                            stop=(c == 1))
                full(last, "co", kv)
            project(5)
            project(6)
            pe.wait_ge(step, value("roped", 1))
            for i in range(3):
                turn(("tk", i), [G[1][:, tt, i * P:(i + 1) * P] for tt in range(NT)])
            pe.wait_ge(step, value("roped", 2))
            for i in range(4):
                turn(("tqn", i), [G[2][:, tt, i * P:(i + 1) * P] for tt in range(NT)])
            pe.wait_ge(step, value("cmp_key"))
            turn(("tkc",), [CK[0:2 * NCMP, 0, :]], rows=DH)
            pe.wait_ge(step, value("roped", 3))
            for i in range(4):
                turn(("tqd", i), [G[3][:, tt, i * P:(i + 1) * P] for tt in range(NT)])

            for qt in range(NT + 2):
                if qt < NT:
                    pe.wait_ge(sem["read_act"], value("read_act", "tkc"))
                    for g in range(2):
                        b = claim("cs", qt, g)
                        for j in range(4):
                            last = nc.tensor.matmul(b[:, j * NCMP:(j + 1) * NCMP],
                                                    QNT[DH * g:DH * g + DH, j, qt * P:(qt + 1) * P],
                                                    KCT[DH * g:DH * g + DH, :], start=True, stop=True)
                        full(last, "cs", qt, g)
                v = qt - 1
                if 0 <= v < NT:
                    pe.wait_ge(sem["cmp_p"], value("cmp_p", v))
                    b = claim("ct", v)
                    for g in range(2):
                        last = nc.tensor.transpose(
                            b[:, g * P:(g + 1) * P],
                            PC[:, v % 2, 4 * g:4 * g + 4, :].rearrange("p h c -> p (h c)"), ident[:])
                    full(last, "ct", v)
                v = qt - 2
                if v >= 0:
                    pe.wait_ge(sem["read_act"], value("read_act", "ct", v))
                    b = claim("cpv", v)
                    for g in range(2):
                        last = nc.tensor.matmul(b[:, g * 256:(g + 1) * 256],
                                                PT1[:, v % 3, g * P:(g + 1) * P], VBLK[:, g, :], start=True,
                                                stop=True)
                    full(last, "cpv", v)

            nU = len(UNITS1)
            pe.wait_ge(sem["read_dve"], value("read_dve", "tqd", 3))
            pe.wait_ge(step, value("setup"))
            pe.wait_ge(sem["topk"], value("topk", 3))
            for u in range(nU + 3):
                if u < nU:
                    br, j, g, qt = UNITS1[u]
                    n = (qt + 1) * P
                    r = slice(DH * g, DH * g + DH)
                    b = claim("s", 1, u)
                    nc.tensor.matmul(b[:, 0:n], (QNT if br < 2 else QDT)[r, j, qt * P:(qt + 1) * P],
                                     KT[r, br, 0:n], start=True, stop=False)
                    if br == 2 and qt:
                        last = nc.tensor.matmul(b[:, 0:n], identb[:], MASKB[:, qt - 1, 0:n], start=False,
                                                stop=True)
                    else:
                        last = nc.tensor.matmul(b[:, n - P:n], identb[:], causal[:], start=False, stop=True)
                    full(last, "s", 1, u)
                v = u - 2
                if 0 <= v < nU:
                    pe.wait_ge(sem["read_act"], value("read_act", "s", 1, v))
                    b = claim("t", 1, v)
                    for kb in range(UNITS1[v][3] + 1):
                        last = nc.tensor.transpose(b[:, kb * P:(kb + 1) * P], PR[:, v % 3, kb * P:(kb + 1) * P],
                                                   ident[:])
                    full(last, "t", 1, v)
                v = u - 3
                if v >= 0:
                    br, j, g, qt = UNITS1[v]
                    evictor = ("read_act", "read_dve")[v % 2]
                    pe.wait_ge(sem[evictor], value(evictor, "t", 1, v))
                    b = claim("o", 1, v)
                    for kb in range(qt + 1):
                        c = br * P + g * DH
                        last = nc.tensor.matmul(b[:, 0:DH], PT1[:, v % 3, kb * P:(kb + 1) * P],
                                                G[4][:, kb, c:c + DH], start=(kb == 0), stop=(kb == qt))
                    full(last, "o", 1, v)
            pe.wait_ge(sem["gmix"], value("gmix", NT - 1))
            for i in range(KD):
                turn(("tm", i), [MIX[:, tt, i * P:(i + 1) * P] for tt in range(NT)])

            def mix_pair(k):
                if first_use("mix", k):
                    pe.wait_ge(sem["read_dve"], value("read_dve", "tm", k))
                return HH[:, k, :], HL[:, k, :]

            for n in range(KD):
                dense(("o1", n), [(("o1", n), P * k) for k in range(KD)], mix_pair)
                mods(("o1", n))

            for layer in range(LAYERS):
                L = layer
                tag = f"m{L}"
                norm(tag, SQ2)
                h = h_pair(tag)

                def square_tile(kind, n):
                    dense((kind, L, n), [((kind, L, n), P * k) for k in range(KD)], h)

                for q in range(4):
                    square_tile("xl", 2 * q)
                    square_tile("xl", 2 * q + 1)
                    square_tile("ga", q)
                    slot = ("lg", L, q)
                    pe.wait_ge(sem["passed"], value("passed", *slot))
                    for i in range(4):
                        n, which = 2 * q + i // 2, ("lr", "li")[i % 2]
                        pe.wait_ge(sem["xc_lo"], value("xc_lo", L, n))
                        b = claim(which, L, n)
                        full(mm3(b[:], wpair(slot, P * i, P), (XCH[:, n % 2, :], XCL[:, n % 2, :]), True, True),
                             which, L, n)
                    used(slot)
                for n in range(4, KD):
                    square_tile("ga", n)
                for n in range(KD):
                    square_tile("gb", n)
                tokens(("kvq", L), [("kvq", L, s) for s in range(4)], 448, tag)
                pe.wait_ge(step, value("latents", L))
                for i in range(3):
                    turn(("tc2", L, i), [KVR[:, tt, i * P:(i + 1) * P] for tt in range(NT)])
                turn(("tc2", L, 3), [KVR[:, tt, 384:448] for tt in range(NT)], rows=DH)
                slot = ("uv", L)
                pe.wait_ge(sem["passed"], value("passed", *slot))
                pe.wait_ge(sem["read_dve"], value("read_dve", "tc2", L, 2))
                for tt in range(NT):
                    for half in range(2):
                        b = claim("v", L, tt, half)
                        t = slice(tt * P, (tt + 1) * P)
                        full(mm3(b[:], (CKH[:, t], CKL[:, t]), wpair(slot, 512 * half, 512), True, True),
                             "v", L, tt, half)
                used(slot)
                slot = ("uqr", L)
                pe.wait_ge(sem["passed"], value("passed", *slot))
                for tt in range(NT):
                    b = claim("qr", L, tt)
                    t = slice(tt * P, (tt + 1) * P)
                    for k in range(2):
                        last = mm3(b[:], (CQH[:, k, t], CQL[:, k, t]), wpair(slot, 512 * k, 512), k == 0, k == 1)
                    full(last, "qr", L, tt)
                used(slot)

                def head_qk(hd):
                    slot = ("hd", L, hd // 2)
                    c = 3 * P * (hd % 2)
                    pe.wait_ge(sem["passed"], value("passed", *slot))
                    b = claim("qn", L, hd)
                    for k in range(2):
                        last = mm3(b[:], wpair(slot, c + P * k, P), (CQH[:, k, :], CQL[:, k, :]), k == 0, k == 1)
                    full(last, "qn", L, hd)
                    b = claim("kn", L, hd)
                    full(mm3(b[:], wpair(slot, c + 2 * P, P), (CKH[:], CKL[:]), True, True), "kn", L, hd)
                    used(slot)

                head_qk(0)
                head_qk(1)
                pe.wait_ge(step, value("q_roped", L))
                for i in range(4):
                    turn(("tq", L, i), [QRR[:, tt, i * P:(i + 1) * P] for tt in range(NT)])
                nU = len(UNITS2)
                for u in range(nU + 4):
                    if u < nU:
                        hd, qt = UNITS2[u]
                        n = (qt + 1) * P
                        r = slice(DH * (hd % 2), DH * (hd % 2) + DH)
                        if u == 0:
                            pe.wait_ge(sem["read_act"], value("read_act", "tq", L, 3))
                            pe.wait_ge(sem["read_act"], value("read_act", "tc2", L, 3))
                        pe.wait_ge(sem["read_act"], value("read_act", "qn", L, hd))
                        pe.wait_ge(sem["read_dve"], value("read_dve", "kn", L, hd))
                        b = claim("s", 2 + L, u)
                        nc.tensor.matmul(b[:, 0:n], QN[:, hd % 2, qt * P:(qt + 1) * P], KN[:, hd % 2, 0:n],
                                         start=True, stop=False)
                        nc.tensor.matmul(b[:, 0:n], QRT[r, hd // 2, qt * P:(qt + 1) * P], KPE[r, 0:n],
                                         start=False, stop=False)
                        full(nc.tensor.matmul(b[:, n - P:n], identb[:], causal[:], start=False, stop=True),
                             "s", 2 + L, u)
                    v = u - 2
                    if 0 <= v < nU:
                        pe.wait_ge(sem["p_norm"], value("p_norm", 2 + L, v))
                        b = claim("t", 2 + L, v)
                        for kb in range(UNITS2[v][1] + 1):
                            last = nc.tensor.transpose(b[:, kb * P:(kb + 1) * P],
                                                       P2[:, v % 3, kb * P:(kb + 1) * P], ident[:])
                        full(last, "t", 2 + L, v)
                    if u >= 6 and (u - 6) % 4 == 0 and (u - 6) // 4 < HEADS:
                        hd = (u - 6) // 4
                        pe.wait_ge(sem["read_act"], value("read_act", "t", 2 + L, 4 * hd + 2))
                        pe.wait_ge(sem["read_dve"], value("read_dve", "t", 2 + L, 4 * hd + 3))
                        b = claim("o", 2 + L, hd)
                        for kb in range(NT):
                            last = nc.tensor.matmul(b[:, kb * P:S], V2[:, kb, hd * P:(hd + 1) * P],
                                                    PT2[:, hd % 2, kb, kb * P:S], start=(kb == 0),
                                                    stop=(kb == NT - 1))
                        full(last, "o", 2 + L, hd)
                    if u < nU:
                        hd, qt = UNITS2[u]
                        if qt == 1 and 1 <= hd < HEADS - 1:
                            head_qk(hd + 1)

                def y_pair(k):
                    if first_use("y", L, k):
                        pe.wait_ge(sem["y_lo"], value("y_lo", L, k))
                    return YH[:, k, :], YL[:, k, :]

                for n in range(KD):
                    dense(("o2", L, n), [(("o2", L, n), P * k) for k in range(KD)], y_pair)
                tag = f"f{L}"
                norm(tag, SQ2)
                h = h_pair(tag)
                for half in range(2):
                    for f in range(half * FH, half * FH + FH):
                        square_tile("fg", f)
                        square_tile("fu", f)
                        if L == 0:
                            mods(("fu", L, f))

                    def hid_pair(j):
                        if first_use("hid", L, half, j):
                            pe.wait_ge(sem["hid_lo"], value("hid_lo", L, half * FH + j))
                        return HDH[:, j, :], HDL[:, j, :]

                    for n in range(KD):
                        chunks = [(("fo", L, half, (n * FH + j) // 8), P * ((n * FH + j) % 8)) for j in range(FH)]
                        dense(("fo", L, half, n), chunks, hid_pair)
                        if L == 0 and (n == KD - 1 or fo_slot(L, half, n + 1) != fo_slot(L, half, n)):
                            mods(fo_slot(L, half, n))
            norm("fin", SQ2)

    return note


def lay_out(v):
    A = {k: np.asarray(x) for k, x in v.items()}
    f = np.float32

    def tiles(w):
        k, n = w.shape
        return w.reshape(k // P, P, n // P, P).transpose(2, 1, 0, 3)

    def rows(w):
        return w.reshape(4, 2, P, 512).transpose(0, 2, 1, 3)

    slots = {}
    w = A["w_in"][0]
    c = dict(qn=0, kc=512, vc=640, ks=768, vs=896, kw=1024, vw=1152, gl=1280, zn=1304, qd=1816, kd=2328,
             vd=2456, qi=2584, ki=2840, wi=2904, zd=2908)
    r = {k: np.arange(o, o + 128) for k, o in c.items()}
    span = lambda k, n: np.arange(c[k], c[k] + n)
    heads = np.concatenate([np.arange(DH) + DH * (4 * g + j) for j in range(4) for g in range(2)])
    groups = {
        0: np.concatenate([span("qi", 256), span("ki", 64), span("ki", 64), span("gl", 24), span("wi", 4),
                           span("qi", 100)]),
        1: np.concatenate([r["ks"], r["kw"], r["kd"], r["kc"]]),
        2: c["qn"] + heads,
        3: c["qd"] + heads,
        4: np.concatenate([r["vs"], r["vw"], r["vd"], r["vc"]]),
        5: span("zn", 512),
        6: span("zd", 512),
    }
    for g, cols in groups.items():
        for s, x in enumerate(rows(w[:, cols])):
            slots[("p1", g, s)] = x
    for kv, name in enumerate(("cmp_k_w1", "cmp_v_w1")):
        for s, x in enumerate(A[name][0].reshape(4, 4, P, CMP_HID).transpose(0, 2, 1, 3)):
            slots[("cw", kv, s)] = x
    for n, x in enumerate(tiles(A["w_out"][0])):
        slots[("o1", n)] = x
    for L in range(LAYERS):
        w = A["w_in_2"][L]
        for kind, o in (("xl", 0), ("ga", 1472), ("gb", 2496)):
            for n, x in enumerate(tiles(w[:, o:o + D])):
                slots[(kind, L, n)] = x
        for s, x in enumerate(rows(np.concatenate([w[:, 1024:1472], w[:, 1024:1088]], 1))):
            slots[("kvq", L, s)] = x
        lw = np.stack([A["lru_wa_2"][L], A["lru_wx_2"][L]], 1)
        for q in range(4):
            x = lw[2 * q:2 * q + 2].transpose(2, 0, 1, 3).reshape(P, 512)
            slots[("lg", L, q)] = np.concatenate([x, x], 1)
        uq, ukv = A["w_uq_2"][L], A["w_ukv_2"][L]
        slots[("uv", L)] = ukv[:, :, P:].reshape(P, D)
        slots[("uqr", L)] = uq[:, :, P:].reshape(2, P, 512).transpose(1, 0, 2)
        for n in range(4):
            parts = []
            for h in (2 * n, 2 * n + 1):
                parts += [uq[0:P, h, 0:P], uq[P:2 * P, h, 0:P], ukv[:, h, 0:P]]
            slots[("hd", L, n)] = np.concatenate(parts + parts[0:2], 1)
        for n, x in enumerate(tiles(A["w_out_2"][L])):
            slots[("o2", L, n)] = x
        ff = tiles(A["w_ffn_in_2"][L])
        for i in range(FT):
            slots[("fg", L, i)], slots[("fu", L, i)] = ff[i], ff[FT + i]
        fo = A["w_ffn_out_2"][L].reshape(2, FH, P, KD, P).transpose(0, 2, 3, 1, 4).reshape(2, P, FH, 1024)
        for half in range(2):
            for s in range(FH):
                slots[("fo", L, half, s)] = fo[half, :, s]
        ada = A["w_ada_2"][L].reshape(KD, P, 6, 1024)
        for cb in range(6):
            for k in range(KD):
                slots[("ada", L, 8 * cb + k)] = ada[k, :, cb]
    stream = np.stack([slots[k].reshape(P, 1024) for k in STREAM])

    def col(x):
        return x.reshape(-1, P).T

    par = np.stack([np.concatenate([
        col(A["b_ada_2"][L]), A["conv_w_2"][L].reshape(4, KD, P).transpose(2, 1, 0).reshape(P, 32),
        col(A["conv_b_2"][L]), col(A["lru_ba_2"][L].reshape(-1)), col(A["lru_bx_2"][L].reshape(-1)),
        col(A["lru_a_param_2"][L]), col(A["q_norm_g_2"][L]), col(A["kv_norm_g_2"][L])], 1)
        for L in range(LAYERS)], 1)
    vec1 = np.concatenate([col(A["norm_gain"][0]), col(A["final_norm_g_2"]), col(A["c_2"][0])], 1)
    gains = np.stack([A["nsa_q_gain"][0], A["nsa_kc_gain"][0], A["nsa_ks_gain"][0], A["nsa_kw_gain"][0],
                      A["dsa_q_gain"][0], A["dsa_k_gain"][0], np.ones(DH, f)])
    pe2 = np.stack([A[n][0].reshape(16, P).T for n in ("cmp_pe_k", "cmp_pe_v")], 1)
    cw2 = np.stack([A[n][0].reshape(2, P, DH).transpose(1, 0, 2) for n in ("cmp_k_w2", "cmp_v_w2")], 1)
    cb1 = np.stack([A["cmp_k_b1"][0], A["cmp_v_b1"][0]])[None]

    freq = (f(THETA) ** (-np.arange(HALF, dtype=f) / f(HALF))).astype(f)
    ang = np.arange(S, dtype=f)[:, None] * freq
    cs1 = np.stack([np.cos(ang), np.sin(ang)]).astype(f).reshape(2, NT, P, HALF).transpose(2, 0, 1, 3)
    cpos = (np.arange(NCMP) * CMP_STRIDE + CMP_BLOCK - 1).astype(f)
    cang = np.tile(cpos, 2)[:, None] * freq
    cscmp = np.stack([np.cos(cang), np.sin(cang)], 1).astype(f)
    tok = np.arange(S).reshape(NT, P)
    sees = cpos[None, None, :] <= tok[:, :, None]
    cmask = np.where(sees, 0.0, NEG).astype(f).transpose(1, 0, 2)
    i = np.arange(P)
    return {
        "xt": A["x"][0].T.reshape(KD, P, S).transpose(1, 0, 2), "stream": stream, "ones": np.ones((P, P), f),
        "ident": np.eye(P, dtype=f), "causal": np.where(i[None, :] <= i[:, None], 0.0, NEG).astype(f),
        "vec1": vec1, "par": par, "freq": freq[None], "pos": A["positions_2"],
        "pos_tok": A["positions_2"].reshape(NT, P).T, "cs1": cs1, "gains": gains, "pe2": pe2, "cw2": cw2,
        "cb1": cb1, "cscmp": cscmp, "cmask": cmask, "cvalid": sees.any(2).astype(f).T,
    }


def kernel(**inputs):
    import concourse.bacc as bacc
    from concourse.bass_utils import run_bass_kernel_spmd

    arrays = {k: np.ascontiguousarray(x) for k, x in lay_out(inputs).items()}
    known = {}
    for _ in range(2):
        nc = bacc.Bacc("TRN2", target_bir_lowering=False, num_devices=1)
        args = {k: nc.dram_tensor(f"in_{k}", x.shape, mybir.dt.from_np(x.dtype), kind="ExternalInput").ap()
                for k, x in arrays.items()}
        args["out"] = nc.dram_tensor("out_t", (P, KD, S), F32, kind="ExternalOutput").ap()
        known = program(nc, args, known)
    r = run_bass_kernel_spmd(nc, [{f"in_{k}": x for k, x in arrays.items()}], core_ids=[0])
    out = np.asarray(r.results[0]["out_t"])
    return np.ascontiguousarray(out.transpose(1, 0, 2).reshape(D, S).T)[None]
```

```python
import math
from contextlib import ExitStack

import numpy as np

import concourse.bass as bass
from concourse import mybir

ALU = mybir.AluOpType
ACT = mybir.ActivationFunctionType
F32 = mybir.dt.float32
F32R = mybir.dt.float32r
BF16 = mybir.dt.bfloat16
I32 = mybir.dt.int32
AX_X = mybir.AxisListType.X

P = 128
D = 1024
KD = D // P
S = 512
NT = S // P
HEADS = 8
DH = 64
HALF = DH // 2
NCMP = 32
CMP_STRIDE, CMP_BLOCK, CMP_HID = 16, 32, 256
TOPK = 128
QK = 192
Q_RANK, KV_RANK = 256, 128
DFF = 2816
FT = DFF // P
FH = FT // 2
LAYERS = 2
LRU_C = 8.0
NEG = -1e30
TAKEN = -3.0e38
EPS = 1e-6
THETA = 10000.0
RAW_RING = 7
SPLIT_RING = 4
ADA = 48


def stream_order():
    order = []
    ada = [("ada", 0, i) for i in range(ADA)]
    for g in P1_ORDER:
        for s in range(4):
            order.append(("p1", g, s))
            if g in (1, 4):
                order.append(ada.pop(0))
            if (g, s) in ((2, 3), (5, 1)):
                order += [("cw", g // 5, i) for i in range(4)]
    order += [ada.pop(0) for _ in ATT_ADA]
    for n in range(KD):
        order.append(("o1", n))
        order += [ada.pop(0) for _ in range((2, 3, 3, 3, 3, 2, 0, 0)[n])]
    for layer in range(LAYERS):
        ada = [("ada", layer + 1, i) for i in range(ADA)] if layer + 1 < LAYERS else []
        for q in range(4):
            order += [("xl", layer, 2 * q), ("xl", layer, 2 * q + 1), ("ga", layer, q), ("lg", layer, q)]
        order += [("ga", layer, n) for n in range(4, KD)]
        order += [("kvq", layer, s) for s in range(4)]
        order += [("gb", layer, n) for n in range(KD)]
        order += [("uv", layer), ("uqr", layer)]
        order += [("hd", layer, n) for n in range(4)]
        order += [("o2", layer, n) for n in range(KD)]
        for half in range(2):
            for f in range(half * FH, half * FH + FH):
                for kind in ("fg", "fu"):
                    order.append((kind, layer, f))
                    if ada:
                        order.append(ada.pop(0))
            for s in range(FH):
                order.append(("fo", layer, half, s))
                if ada:
                    order.append(ada.pop(0))
        assert not ada
    return order


ATT_ADA = tuple(range(2, 74, 3))
P1_ORDER = (0, 1, 4, 2, 3, 5, 6)
STREAM = stream_order()
SLOT = {key: n for n, key in enumerate(STREAM)}
WEIGHTS = [key for key in STREAM if key[0] not in ("ada", "cw")]
WSLOT = {key: n for n, key in enumerate(WEIGHTS)}
assert len(STREAM) % RAW_RING == 0


def fo_slot(layer, half, n):
    return ("fo", layer, half, (n * FH + FH - 1) // 8)


def in_attention(key):
    return key[:2] == ("ada", 0) and 8 <= key[2] < 8 + len(ATT_ADA)


def next_norm(layer):
    return f"m{layer + 1}" if layer + 1 < LAYERS else "fin"


def mod_points():
    anchors = [("p1", g, 3) for g in P1_ORDER] + [("o1", n) for n in range(KD)]
    for half in range(2):
        anchors += [("fu", 0, f) for f in range(half * FH, half * FH + FH)]
        anchors += [fo_slot(0, half, n) for n in range(KD)]
    anchors = list(dict.fromkeys(anchors))
    out = {}
    for layer in range(LAYERS):
        for cb in range(ADA // 8):
            last = 8 * cb + 7
            if layer == 0 and 8 <= last < 8 + len(ATT_ADA):
                key = ("att", ATT_ADA[last - 8] + 4)
            else:
                key = next(k for k in anchors if SLOT[k] > SLOT[("ada", layer, last)] + 1)
            out.setdefault(key, []).append((layer, cb))
    return out


MODS = mod_points()

PB_ADA, PCONV_W, PCONV_B, PBA, PBX, PA, PQG, PKVG, PCOLS = 0, 48, 80, 88, 96, 104, 112, 114, 115
G_Q, G_KC, G_KS, G_KW, G_QD, G_KD, G_ONE, G_ROWS = 0, 1, 2, 3, 4, 5, 6, 7

SEMAPHORES = (
    "step", "consts", "x_in", "passed", "normed", "stored", "ada", "w_hi", "square", "sq_added", "n1_added", "x_in_2", "norm_consts", "ada_scaled", "ada_sum", "pool_set",
    "read_act", "full", "ca", "read_dve", "gmix", "h_hi", "lru_par", "lru_w", "topk", "iscore", "cos_sin",
    "cmp_shift", "cmp_exp", "nmax", "mix_hi", "x_new", "conv", "xc_hi", "tanh", "lru_a", "one_aa", "mult",
    "ya_gated", "c_hi", "y_full", "y_hi", "hid", "hid_hi", "x_half", "h_lo", "yb", "y_lo", "cmp_p", "xc_lo",
    "p_norm", "hid_lo", "w_used",
)

UNITS1 = [(b, j, g, qt) for b in (0, 1) for j in range(4) for qt in range(NT) for g in range(2)]
UNITS1 += [(2, j, g, qt) for qt in range(NT) for j in range(4) for g in range(2)]
O1_SPLITS = (75, 80, 88)
CMP_START = (32, 40, 48, 56)
CMP_MASK, CMP_EXP, CMP_NORM, CMP_TURN, CMP_MOVE, CMP_PV, CMP_ADD = 0, 1, 2, 4, 4, 6, 6


TOPK_UNITS = tuple(range(2, 50, 3))
assert len(TOPK_UNITS) == TOPK // 8


def cmp_tile(u, step):
    return CMP_START.index(u - step) if u - step in CMP_START else None


T_LAG, O_LAG = 3, 4
RING = 4


def evictor(v):
    return "read_dve" if v % 4 == 3 else "read_act"


UNITS2 = [(h, qt) for h in range(HEADS) for qt in range(NT)]


def program(nc, a, known):
    note = {}
    with ExitStack() as ctx:
        base = (nc.sbuf_base + 63) // 64 * 64
        KB = 1024

        def at(name, shape, dt, off):
            return nc.alloc_sbuf_tensor_at(name, shape, dt, offset=base + int(off))

        X = at("X", [P, KD, S], F32, 0)
        HH = at("HH", [P, KD, S], F32R, 16 * KB)
        HL = at("HL", [P, KD, S], F32R, 32 * KB)
        RAW = [at(f"RAW{i}", [P, 1024], F32, (48 + 4 * i) * KB) for i in range(RAW_RING)]
        split0 = 48 + 4 * RAW_RING
        WH = [at(f"WH{i}", [P, 1024], F32R, (split0 + 8 * i) * KB) for i in range(SPLIT_RING)]
        WL = [at(f"WL{i}", [P, 1024], F32R, (split0 + 4 + 8 * i) * KB) for i in range(SPLIT_RING)]
        cur = [(split0 + 8 * SPLIT_RING) * KB]

        def small(name, shape, dt, size=4):
            off = cur[0]
            cur[0] += (int(np.prod(shape[1:])) * size + 31) // 32 * 32
            return at(name, shape, dt, off)

        ident = small("ident", [P, P], F32)
        ones = small("ones", [P, P], F32)
        identb = small("identb", [P, P], BF16, 2)
        causal = small("causal", [P, P], BF16, 2)
        vec1 = small("vec1", [P, 3 * KD], F32)
        par = small("par", [P, LAYERS, PCOLS], F32)
        mod = small("mod", [P, LAYERS, ADA], F32)
        sc1 = small("sc1", [P, LAYERS, 2, KD], F32)
        csc = small("csc", [P, LAYERS, KD], F32)
        lt = small("lt", [P, 6, LAYERS, KD], F32)
        cs2 = small("cs2", [P, 2, NT, HALF], F32)
        freq = small("freq", [P, HALF], F32)
        posi = small("posi", [P, NT], I32)
        posf = small("posf", [P, NT], F32)
        keep = small("keep", [P, S], BF16, 2)
        reset = small("reset", [P, S], BF16, 2)
        stat = small("stat", [P, 3, NT], F32)
        nmax = small("nmax", [P, 8], F32)
        rsum = small("rsum", [P, 8], F32)
        coef = small("coef", [P, 8], F32)
        gate = small("gate", [P, NT, 28], F32)
        kst = small("kst", [P, 3, NT * 8], F32)
        W0 = (cur[0] + 63) // 64 * 64

        def w(name, shape, dt, kb):
            return at(name, shape, dt, W0 + kb * KB)

        G = {1: w("G1", [P, NT, 512], F32, 0), 2: w("G2", [P, NT, 512], F32, 8),
             3: w("G3", [P, NT, 512], F32, 16), 4: w("G4", [P, NT, 512], F32, 24)}
        MISC = w("MISC", [P, NT, 384], F32, 32)
        QIT = w("QIT", [P, 2, S], F32, 38)
        KIT = w("KIT", [P, S], F32, 42)
        RELU = w("RELU", [P, 3, S], F32, 44)
        SCORE = w("SCORE", [P, S], F32, 50)
        Z = w("Z", [P, NT, D], F32, 32)
        KC2 = w("KC2", [P, 2, 544], F32, 52)
        CA = w("CA", [P, 16, 2 * NCMP], F32, 56.25)
        HID = w("HID", [P, 2, CMP_HID], F32, 60.25)
        HIDT = w("HIDT", [P, 2, 2, 2 * NCMP], F32, 62.25)
        CK = w("CK", [P, 3, DH], F32, 63.25)
        KCT = w("KCT", [P, NCMP], F32, 64)
        VBLK = w("VBLK", [P, 2, 256], F32, 64.25)
        MASKB = w("MASKB", [P, 3, S], BF16, 66.25)
        TAB = w("TAB", [P, 2, NT, DH], F32, 69.25)
        CS1 = w("CS1", [P, 2, NT, HALF], F32, 71.25)
        TMP = w("TMP", [P, 2, S], F32, 72.25)
        SQS = w("SQS", [P, S], F32, 76.25)
        ACC = w("ACC", [P, 2, 1024], F32, 78.25)
        ADA_T = w("ADA_T", [P, 1024], F32, 72.25)
        ADA_T2 = w("ADA_T2", [P, 1024], F32, 60)
        gains = w("gains", [P, G_ROWS, DH], F32, 86.25)
        cb1 = w("cb1", [P, 2, CMP_HID], F32, 88)
        cw2 = w("cw2", [P, 2, 2, DH], F32, 90)
        pe2 = w("pe2", [P, 2, 16], F32, 91)
        cscmp = w("cscmp", [P, 2, HALF], F32, 91.125)
        cmask = w("cmask", [P, NT, NCMP], F32, 91.375)
        cvalid = w("cvalid", [P, NT], F32, 91.875)
        TKM = w("TKM", [P, 8], F32, 91.9375)
        MIX = w("MIX", [P, NT, D], F32, 8)
        PTC = w("PTC", [P, 2, 256], F32, 48)
        PT1 = w("PT1", [P, RING, S], F32, 52)
        QNT = at("QNT", [P, 4, S], F32, 16 * KB)
        QDT = at("QDT", [P, 4, S], F32, 24 * KB)
        KT = at("KT", [P, 6, S], F32, 32 * KB)
        PR = w("PR", [P, RING, S], F32, 0)
        PC = at("PC", [P, 2, 8, NCMP], F32, 44 * KB)
        CST = at("CST", [P, 4, 8], F32, 46 * KB)

        YA = w("YA", [P, KD, S], F32, 0)
        YH = w("YH", [P, KD, S], F32R, 0)
        SG = w("SG", [P, KD, S], F32, 16)
        YL = w("YL", [P, KD, S], F32R, 16)
        XC = w("XC", [P, KD, S], F32, 32)
        LR = w("LR", [P, KD, S], F32, 48)
        LI = w("LI", [P, KD, S], F32, 64)
        XCH = w("XCH", [P, 2, S], F32R, 80)
        XCL = w("XCL", [P, 2, S], F32R, 84)
        V2 = w("V2", [P, NT, D], F32, 32)
        QRT = w("QRT", [P, 4, S], F32, 48)
        KPE = w("KPE", [P, 2, S], F32, 66)
        QN = w("QN", [P, 2, S], F32, 58)
        KN = w("KN", [P, 2, S], F32, 62)
        P2 = at("P2", [P, RING, S], F32, 16 * KB)
        PT2 = w("PT2", [P, 2, NT, S], F32, 72)
        YT = w("YT", [P, 2, S], F32, 88)
        TAB2 = at("TAB2", [P, 2, NT, DH], F32, 23 * KB)
        TAB2K = YT[:, :, 256:512].rearrange("p c (t d) -> p c t d", t=NT)
        KVR = w("KVR", [P, NT, 448], F32, 80)
        CQH = at("CQH", [P, 2, S], F32R, 25 * KB)
        CKH = at("CKH", [P, S], F32R, 29 * KB)
        CQL = at("CQL", [P, 2, S], F32R, 31 * KB)
        CKL = at("CKL", [P, S], F32R, 35 * KB)
        QRR = at("QRR", [P, NT, 512], F32, 37 * KB)
        HDH = w("HDH", [P, FH, S], F32R, 0)
        HDL = w("HDL", [P, FH, S], F32R, 22)
        SILU = w("SILU", [P, 2, S], F32, 44)
        HF = w("HF", [P, 2, S], F32, 48)
        NTMP = w("NTMP", [P, 2, S], F32, 52)
        SQT = w("SQT", [P, 2, S], F32, 56)
        SQ2 = w("SQ2", [P, S], F32, 60)

        bank = [ctx.enter_context(nc.psum_tensor(f"bank{i}", [P, S], F32)) for i in range(8)]
        landed = [ctx.enter_context(nc.semaphore(f"slot_landed{i}")) for i in range(RAW_RING)]
        sem = {name: ctx.enter_context(nc.semaphore(name)) for name in SEMAPHORES}
        step = sem["step"]
        count = dict.fromkeys(SEMAPHORES, 0)

        def mark(name, *key, by=1):
            count[name] += by
            note[(name,) + key] = count[name]
            return by

        def value(*key):
            if known and key not in known:
                raise KeyError(key)
            return known.get(key, 1)

        def own():
            count["step"] += 1
            return count["step"]

        def ring(key):
            return SLOT[key] % RAW_RING

        def loads(key):
            return 16 * (SLOT[key] // RAW_RING + 1)

        def last_use(key):
            name, v = known.get(("used",) + key, ("full", 1))
            return sem[name], v

        def raw(key):
            return RAW[SLOT[key] % RAW_RING]

        def hi(key):
            return WH[WSLOT[key] % SPLIT_RING]

        def lo(key):
            return WL[WSLOT[key] % SPLIT_RING]

        def bank_of(*key):
            return bank[known.get(("bank",) + key, 0)]

        def spread(ap, dims, shape):
            return ap.rearrange(dims, o=1).broadcast_to(shape)

        block = ctx.enter_context(nc.Block())

        @block.sync
        def _(sp):
            def load(dst, src):
                sp.dma_start(dst, src).then_inc(sem["consts"], mark("consts", by=16))

            for k in range(0, KD, 4):
                half = ("x_in", "x_in_2")[k // 4]
                sp.dma_start(X[:, k:k + 4, :], a["xt"][:, k:k + 4, :]).then_inc(sem[half], mark(half, by=16))
            for dst, name in ((ones, "ones"), (ident, "ident"), (vec1, "vec1")):
                sp.dma_start(dst[:], a[name]).then_inc(sem["norm_consts"], mark("norm_consts", by=16))
            for s in range(4):
                sp.dma_start(RAW[s][:], a["stream"][s]).then_inc(landed[s], 16)
            load(ACC[:, 0, 0:P], a["causal"])
            load(par[:], a["par"])
            load(freq[:], a["freq"].broadcast_to([P, HALF]))
            load(posi[:], a["pos_tok"])
            load(ACC[:, 1, 0:S].bitcast(I32), a["pos"].broadcast_to([P, S]))
            load(CS1[:], a["cs1"])
            load(gains[:], spread(a["gains"], "(o r) d -> o r d", [P, G_ROWS, DH]))
            load(pe2[:], a["pe2"])
            load(cw2[:], a["cw2"])
            load(cb1[0:1], a["cb1"])
            load(cscmp[0:2 * NCMP], a["cscmp"])
            load(cmask[:], a["cmask"])
            load(cvalid[:], a["cvalid"])
            note[("consts", "all")] = count["consts"]
            for s in range(4, RAW_RING):
                sp.dma_start(RAW[s][:], a["stream"][s]).then_inc(landed[s], 16)

            with sp.Fori(1, len(STREAM) // RAW_RING) as i:
                for s in range(RAW_RING):
                    sp.wait_ge(sem["passed"], i * RAW_RING + (s + 1 - RAW_RING))
                    sp.dma_start(RAW[s][:], a["stream"][bass.ds(i * RAW_RING + s, 1)].rearrange(
                        "o p c -> (o p) c")).then_inc(landed[s], 16)

            for k in range(KD):
                sp.wait_ge(sem["normed"], value("normed", "fin", k))
                sp.dma_start(a["out"][:, k, :], YA[:, k, :]).then_inc(sem["stored"], mark("stored", k, by=16))
            sp.wait_ge(sem["stored"], 16 * KD)

        @block.gpsimd
        def _(pool):
            at_slot = [0]

            def pass_through(key, ahead=SPLIT_RING - 1):
                pass_to(SLOT[WEIGHTS[min(WSLOT[key] + ahead, len(WEIGHTS) - 1)]] + 1)

            def pass_to(end):
                while at_slot[0] < end:
                    k = STREAM[at_slot[0]]
                    if in_attention(k):
                        pool.wait_ge(sem["ada_scaled"], value("ada_scaled", k[2]))
                    elif k[0] == "ada":
                        pool.wait_ge(sem["ada"], value("ada", *k[1:]))
                    elif k[0] == "cw":
                        pool.wait_ge(*last_use(k))
                    else:
                        pool.wait_ge(sem["w_hi"], value("w_hi", *k))
                        nc.gpsimd.tensor_tensor(lo(k)[:], raw(k)[:], hi(k)[:].bitcast(F32),
                                                ALU.subtract).then_inc(sem["passed"], mark("passed", *k))
                        at_slot[0] += 1
                        continue
                    pool.wait_ge(sem["passed"], max(1, count["passed"]))
                    pool.sem_inc(sem["passed"], 1)
                    count["passed"] += 1
                    at_slot[0] += 1
                    if in_attention(k) and k[2] % 8:
                        add_ada(k[2])

            def add_ada(i):
                acc = ACC[:, i // 8 % 2, :]
                if i % 8 > 1:
                    pool.wait_ge(sem["ada_sum"], value("ada_sum", i - 1))
                nc.gpsimd.tensor_tensor(acc, acc, (ADA_T, ADA_T2)[i % 2][:], ALU.add).then_inc(
                    sem["ada_sum"], mark("ada_sum", i))

            def add_squares(tag, sq, total, key_of=None):
                for k in range(1, KD):
                    if key_of:
                        pass_through(key_of(k))
                    pool.wait_ge(sem["square"], value("square", tag, k))
                    if k > 1:
                        pool.wait_ge(sem["sq_added"], value("sq_added", tag, k - 1))
                    nc.gpsimd.tensor_tensor(total[:], sq[:, 0, :] if k == 1 else total[:],
                                            sq[:, k % 2, :], ALU.add).then_inc(
                        sem["sq_added"], mark("sq_added", tag, k))

            nc.gpsimd.memset(VBLK[:], 0.0).then_inc(sem["pool_set"], mark("pool_set", 0))
            nc.gpsimd.memset(KC2[:], 0.0).then_inc(sem["pool_set"], mark("pool_set", 1))
            for kv in range(2):
                pass_through(("p1", (4, 2)[kv], 3))
                pool.wait_ge(sem["consts"], value("consts", "all"))
                pool.wait_ge(sem["read_act"], value("read_act", "tc", kv))
                if kv:
                    pool.wait_ge(sem["full"], value("full", "hid", 0))
                for i in range(16):
                    src = KC2[:, :, 2 * i:2 * i + 16 * NCMP].rearrange("p g (c t) -> p g c t", t=16)[:, :, :, 0]
                    nc.gpsimd.tensor_scalar(
                   CA[:, i, :].rearrange("p (g c) -> p g c", g=2), src, pe2[:, kv, i:i + 1], None,
                   ALU.add).then_inc(sem["ca"], mark("ca", kv, i))
            pass_through(("p1", 6, 3), 0)
            pool.wait_ge(sem["full"], value("full", "p1", 6, NT - 1))
            for i in range(3):
                nc.gpsimd.memset(KT[DH:P, 2 * i, :], 0.0)
                nc.gpsimd.memset(KT[0:DH, 2 * i + 1, :], 0.0).then_inc(sem["pool_set"], mark("pool_set", 2 + i))
            pass_through(("o1", 0), 0)
            for qt in range(NT):
                pool.wait_ge(sem["read_dve"], value("read_dve", "o", 1, UNITS1.index((2, 3, 1, qt))))
                pool.wait_ge(sem["read_act"], value("read_act", "p1", 6, qt))
                nc.gpsimd.tensor_tensor(MIX[:, qt, :], MIX[:, qt, :], Z[:, qt, :], ALU.mult).then_inc(
                    sem["gmix"], mark("gmix", qt))
            add_squares("m0", SQT, SQ2, lambda k: ("o1", k))
            for layer in range(LAYERS):
                pass_through(("gb", layer, KD - 1))
                pool.wait_ge(sem["ya_gated"], value("ya_gated", layer, KD - 1))
                pool.wait_ge(sem["passed"], max(1, count["passed"]))
                nc.gpsimd.memset(KPE[DH:P, 0, :], 0.0)
                nc.gpsimd.memset(KPE[0:DH, 1, :], 0.0).then_inc(sem["pool_set"], mark("pool_set", "kpe", layer))
                pool.wait_ge(sem["pool_set"], value("pool_set", "kpe", layer))
                pass_through(("hd", layer, 3))
                add_squares(f"f{layer}", SQT, SQ2, lambda k: ("o2", layer, k))
                add_squares(next_norm(layer), SQT, SQ2, lambda k: fo_slot(layer, 1, k))

        @block.scalar
        def _(act):
            split_next = [0]

            def split_through(key, ahead=SPLIT_RING - 1):
                last = min(WSLOT[key] + ahead, len(WEIGHTS) - 1)
                while split_next[0] <= last:
                    k = WEIGHTS[split_next[0]]
                    act.wait_ge(landed[ring(k)], loads(k))
                    if split_next[0] >= SPLIT_RING:
                        act.wait_ge(*last_use(WEIGHTS[split_next[0] - SPLIT_RING]))
                    nc.scalar.activation(hi(k)[:], raw(k)[:], ACT.Copy).then_inc(sem["w_hi"], mark("w_hi", *k))
                    split_next[0] += 1

            def evict(dst, *key, func=ACT.Copy, **kw):
                act.wait_ge(sem["full"], value("full", *key))
                b = bank_of(*key)
                n = int(np.prod(dst.shape[1:]))
                return nc.scalar.activation(dst, b[0:dst.shape[0], 0:n], func, **kw).then_inc(
                    sem["read_act"], mark("read_act", *key))

            def square(tag, k, sq):
                if k >= 2:
                    adder = "n1_added" if tag == "n1" else "sq_added"
                    act.wait_ge(sem[adder], value(adder, tag, max(1, k - 2)))
                nc.scalar.activation(sq[:, k % 2, :], X[:, k, :], ACT.Square).then_inc(
                    sem["square"], mark("square", tag, k))

            def norm_hi(tag, tmp, shift):
                for k in range(KD):
                    act.wait_ge(sem["normed"], value("normed", tag, k))
                    if shift is None:
                        ins = nc.scalar.activation(HH[:, k, :], tmp[:, k % 2, :], ACT.Copy)
                    else:
                        ins = nc.scalar.activation(HH[:, k, :], tmp[:, k % 2, :], ACT.Identity,
                                                   bias=shift[:, k:k + 1])
                    ins.then_inc(sem["h_hi"], mark("h_hi", tag, k))

            for k in range(KD):
                half = ("x_in", "x_in_2")[k // 4]
                act.wait_ge(sem[half], value(half))
                square("n1", k, RELU)
            split_through(("p1", 0, 0))
            norm_hi("n1", TMP, None)
            act.wait_ge(sem["consts"], value("consts", "all"))
            nc.scalar.activation(lt[:, 0], par[:, :, PA:PA + KD], ACT.Abs).then_inc(
                sem["lru_par"], mark("lru_par", 0))
            act.wait_ge(sem["lru_par"], value("lru_par", 0))
            nc.scalar.activation(lt[:, 1], lt[:, 0], ACT.Exp, scale=-1.0).then_inc(
                sem["lru_par"], mark("lru_par", 1))
            act.wait_ge(sem["lru_w"], value("lru_w"))
            nc.scalar.activation(lt[:, 3], lt[:, 2], ACT.Ln).then_inc(sem["lru_par"], mark("lru_par", 2))

            def evict_group(g):
                split_through(("p1", g, 3), 0 if g in (2, 3, 6) else SPLIT_RING - 1)
                for tt in range(NT):
                    act.wait_ge(sem["full"], value("full", "p1", g, tt))
                    b = bank_of("p1", g, tt)
                    if g == 0:
                        nc.scalar.activation(MISC[:, tt, :], b[:, 0:384], ACT.Copy)
                        nc.scalar.activation(gate[:, tt, 24:28], b[:, 408:412], ACT.Copy, scale=0.5)
                        nc.scalar.activation(gate[:, tt, 0:24], b[:, 384:408], ACT.Sigmoid).then_inc(
                            sem["read_act"], mark("read_act", "p1", g, tt))
                    elif g < 5:
                        evict(G[g][:, tt, :], "p1", g, tt)
                    else:
                        act.wait_ge(sem["iscore"], value("iscore", 3, 3))
                        evict(Z[:, tt, (g - 5) * 512:(g - 4) * 512], "p1", g, tt, func=ACT.Silu)

            def relus(qt):
                n = (qt + 1) * P
                for h in range(1, 4):
                    if qt > 1:
                        act.wait_ge(sem["iscore"], value("iscore", qt - 1, h))
                    evict(RELU[:, h - 1, 0:n], "idx", qt, h, func=ACT.Relu)

            def shift_in(kv):
                act.wait_ge(sem["full"], value("full", "tc", kv))
                b = bank_of("tc", kv)
                act.wait_ge(sem["pool_set"], value("pool_set", 1))
                if kv:
                    act.wait_ge(sem["ca"], value("ca", 0, 15))
                for g in range(2):
                    nc.scalar.activation(KC2[0:DH, g, 0:S], b[g * DH:(g + 1) * DH, :], ACT.Copy)
                    last = nc.scalar.activation(KC2[DH:P, g, 0:S - 1], b[g * DH:(g + 1) * DH, 1:S], ACT.Copy)
                last.then_inc(sem["read_act"], mark("read_act", "tc", kv))

            evict_group(0)
            evict_group(1)
            for i in range(3):
                evict(QIT[:, i, :] if i < 2 else KIT[:], "ti", i)
            evict_group(4)
            relus(1)
            shift_in(0)
            evict_group(2)
            relus(2)
            split_through(("p1", 3, 0))
            evict(HID[0:2 * NCMP, 0, :], "hid", 0, func=ACT.Silu)
            shift_in(1)
            evict_group(3)
            split_through(("p1", 5, 1), 0)
            evict(HID[0:2 * NCMP, 1, :], "hid", 1, func=ACT.Silu)
            relus(3)
            for kv in range(2):
                evict(HIDT[:, kv].rearrange("p c t -> p (c t)"), "ht", kv)
            evict(CK[0:2 * NCMP, 0, :], "co", 0)
            act.wait_ge(sem["full"], value("full", "co", 1))
            b = bank_of("co", 1)
            act.wait_ge(sem["pool_set"], value("pool_set", 0))
            for g in range(2):
                for r in range(4):
                    last = nc.scalar.activation(VBLK[32 * r:32 * r + 32, g, DH * r:DH * r + DH],
                                                b[32 * g:32 * g + 32, 0:DH], ACT.Copy)
            last.then_inc(sem["read_act"], mark("read_act", "co", 1))
            evict_group(5)
            evict_group(6)
            for i in range(3):
                act.wait_ge(sem["full"], value("full", "tk", i))
                b = bank_of("tk", i)
                nc.scalar.activation(KT[0:DH, 2 * i, :], b[0:DH, :], ACT.Copy)
                nc.scalar.activation(KT[DH:P, 2 * i + 1, :], b[DH:P, :], ACT.Copy).then_inc(
                    sem["read_act"], mark("read_act", "tk", i))
            for i in range(4):
                evict(QNT[:, i, :], "tqn", i)
            act.wait_ge(sem["full"], value("full", "tkc"))
            b = bank_of("tkc")
            nc.scalar.activation(KCT[0:DH, :], b[0:DH, 0:NCMP], ACT.Copy)
            nc.scalar.activation(KCT[DH:P, :], b[0:DH, NCMP:2 * NCMP], ACT.Copy).then_inc(
                sem["read_act"], mark("read_act", "tkc"))

            act.wait_ge(step, value("angles"))
            nc.scalar.activation(cs2[:], cs2[:], ACT.Sin).then_inc(sem["cos_sin"], mark("cos_sin"))

            def scale_ada(i):
                k = ("ada", 0, i)
                cb, row = divmod(i, 8)
                act.wait_ge(landed[ring(k)], loads(k))
                if row == 0:
                    dst = ACC[:, cb % 2, :]
                    if cb == 1:
                        act.wait_ge(step, value("setup"))
                    else:
                        act.wait_ge(sem["full"], value("full", "mod", 0, cb - 2))
                else:
                    dst = (ADA_T, ADA_T2)[i % 2][:]
                    if i >= 11:
                        act.wait_ge(sem["ada_sum"], value("ada_sum", i - 2 if row > 2 else i - row - 1))
                nc.scalar.activation(dst, raw(k)[:], ACT.Identity, scale=vec1[:, 2 * KD + row:2 * KD + row + 1]).then_inc(
                    sem["ada_scaled"], mark("ada_scaled", i))

            for u in range(len(UNITS1) + T_LAG):
                if u in O1_SPLITS:
                    split_through(("o1", O1_SPLITS.index(u)), 0)
                v = u - T_LAG
                if v >= 0 and evictor(v) == "read_act":
                    if v >= RING:
                        act.wait_ge(sem["full"], value("full", "o", 1, v - RING))
                    evict(PT1[:, v % RING, 0:(UNITS1[v][3] + 1) * P], "t", 1, v)
                if u < len(UNITS1):
                    n = (UNITS1[u][3] + 1) * P
                    act.wait_ge(sem["nmax"], value("nmax", 1, u))
                    if u >= RING:
                        act.wait_ge(sem["full"], value("full", "t", 1, u - RING))
                    act.wait_ge(sem["full"], value("full", "s", 1, u))
                    b = bank_of("s", 1, u)
                    nc.scalar.activation(PR[:, u % RING, 0:n], b[:, 0:n], ACT.Exp, bias=nmax[:, u % 8:u % 8 + 1],
                                         accum_out=rsum[:, u % 8:u % 8 + 1]).then_inc(
                        sem["read_act"], mark("read_act", "s", 1, u))
                qt = cmp_tile(u, CMP_EXP)
                if qt is not None:
                    act.wait_ge(sem["cmp_shift"], value("cmp_shift", qt))
                    nc.scalar.activation(PC[:, qt % 2], PC[:, qt % 2], ACT.Exp).then_inc(
                        sem["cmp_exp"], mark("cmp_exp", qt))
                qt = cmp_tile(u, CMP_MOVE)
                if qt is not None:
                    if qt >= 2:
                        act.wait_ge(sem["full"], value("full", "cpv", qt - 2))
                    evict(PTC[:, qt % 2, :], "ct", qt)
                if u in ATT_ADA:
                    scale_ada(8 + ATT_ADA.index(u))
            for i in range(KD):
                act.wait_ge(sem["full"], value("full", "tm", i))
                b = bank_of("tm", i)
                nc.scalar.activation(HH[:, i, :], b[:], ACT.Copy).then_inc(sem["mix_hi"], mark("mix_hi", i))
            for n in range(KD):
                split_through(("o1", n))
                act.wait_ge(sem["x_new"], value("x_new", "m0", n))
                square("m0", n, SQT)

            for layer in range(LAYERS):
                L = layer

                def vec(col):
                    return par[:, L, col:col + 1]

                split_through(("xl", L, 0), 0)
                norm_hi(f"m{L}", NTMP, mod[:, L, 0:KD])
                for q in range(4):
                    split_through(("xl", L, 2 * q))
                    for n in (2 * q, 2 * q + 1):
                        split_through(("xl", L, n))
                        act.wait_ge(sem["conv"], value("conv", L, n))
                        if n >= 2:
                            act.wait_ge(sem["full"], value("full", "li", L, n - 2))
                        nc.scalar.activation(XCH[:, n % 2, :], XC[:, n, :], ACT.Copy).then_inc(
                            sem["xc_hi"], mark("xc_hi", L, n))
                    split_through(("ga", L, q))
                    evict(SG[:, q, :], "ga", L, q, func=ACT.Sigmoid)
                    split_through(("lg", L, q))
                    for n in (2 * q, 2 * q + 1):
                        evict(LR[:, n, :], "lr", L, n, func=ACT.Sigmoid, bias=vec(PBA + n))
                        evict(LI[:, n, :], "li", L, n, func=ACT.Sigmoid, bias=vec(PBX + n))
                        act.wait_ge(sem["read_act"], value("read_act", "lr", L, n))
                        nc.scalar.activation(YA[:, n, :], LR[:, n, :], ACT.Tanh, scale=csc[:, L, n:n + 1]).then_inc(
                            sem["tanh"], mark("tanh", L, n))
                for n in range(KD):
                    act.wait_ge(sem["tanh"], value("tanh", L, n))
                    nc.scalar.activation(LR[:, n, :], LR[:, n, :], ACT.Exp, scale=csc[:, L, n:n + 1]).then_inc(
                        sem["lru_a"], mark("lru_a", L, n))
                for n in range(4, KD):
                    split_through(("ga", L, n))
                    evict(SG[:, n, :], "ga", L, n, func=ACT.Sigmoid)
                split_through(("kvq", L, 3))
                for tt in range(NT):
                    evict(KVR[:, tt, :], "kvq", L, tt)
                for n in range(KD):
                    act.wait_ge(sem["one_aa"], value("one_aa", L, n))
                    nc.scalar.activation(YA[:, n, :], YA[:, n, :], ACT.Sqrt, scale=-1.0).then_inc(
                        sem["mult"], mark("mult", L, n))
                for n in range(KD):
                    split_through(("gb", L, n))
                    act.wait_ge(sem["ya_gated"], value("ya_gated", L, n))
                    evict(SG[:, n, :], "gb", L, n, func=ACT.Sigmoid)
                for i in (2, 0, 1):
                    act.wait_ge(sem["full"], value("full", "tc2", L, i))
                    b = bank_of("tc2", L, i)
                    dst = CQH[:, i, :] if i < 2 else CKH[:]
                    nc.scalar.activation(dst, b[:], ACT.Identity, scale=vec(PQG + i)).then_inc(
                        sem["c_hi"], mark("c_hi", L, i))
                act.wait_ge(sem["full"], value("full", "tc2", L, 3))
                b = bank_of("tc2", L, 3)
                nc.scalar.activation(KPE[0:DH, 0, :], b[0:DH, :], ACT.Copy)
                nc.scalar.activation(KPE[DH:P, 1, :], b[0:DH, :], ACT.Copy).then_inc(
                    sem["read_act"], mark("read_act", "tc2", L, 3))
                split_through(("uv", L))
                for tt in range(NT):
                    for half in range(2):
                        evict(V2[:, tt, half * 512:(half + 1) * 512], "v", L, tt, half)
                for tt in range(NT):
                    evict(QRR[:, tt, :], "qr", L, tt, scale=float(QK) ** -0.5)
                split_through(("uqr", L))
                for h in range(2):
                    evict(QN[:, h, :], "qn", L, h, scale=float(QK) ** -0.5)
                for i in range(4):
                    evict(QRT[:, i, :], "tq", L, i)
                for u in range(len(UNITS2) + O_LAG):
                    v = u - T_LAG
                    if 0 <= v < len(UNITS2) and evictor(v) == "read_act":
                        h, qt = UNITS2[v]
                        if h >= 2:
                            act.wait_ge(sem["full"], value("full", "o", 2 + L, h - 2))
                        act.wait_ge(sem["full"], value("full", "t", 2 + L, v))
                        b = bank_of("t", 2 + L, v)
                        n = (qt + 1) * P
                        nc.scalar.activation(
                       PT2[:, h % 2, 0:qt + 1, qt * P:(qt + 1) * P],
                       b[:, 0:n].rearrange("p (k q) -> p k q", k=qt + 1), ACT.Copy).then_inc(
                            sem["read_act"], mark("read_act", "t", 2 + L, v))
                    if u < len(UNITS2):
                        h, qt = UNITS2[u]
                        n = (qt + 1) * P
                        act.wait_ge(sem["nmax"], value("nmax", 2 + L, u))
                        if u >= RING:
                            act.wait_ge(sem["full"], value("full", "t", 2 + L, u - RING))
                        act.wait_ge(sem["full"], value("full", "s", 2 + L, u))
                        b = bank_of("s", 2 + L, u)
                        nc.scalar.activation(P2[:, u % RING, 0:n], b[:, 0:n], ACT.Exp,
                                             bias=nmax[:, u % 8:u % 8 + 1],
                                             accum_out=rsum[:, u % 8:u % 8 + 1]).then_inc(
                            sem["read_act"], mark("read_act", "s", 2 + L, u))
                    if u >= 7 and (u - 7) % 4 == 0:
                        h = (u - 7) // 4
                        act.wait_ge(sem["y_full"], value("y_full", L, h))
                        nc.scalar.activation(YH[:, h, :], YT[:, h % 2, :], ACT.Copy).then_inc(
                            sem["y_hi"], mark("y_hi", L, h))
                    if u < len(UNITS2):
                        h, qt = UNITS2[u]
                        if qt == 1 and 1 <= h < HEADS - 1:
                            split_through(("hd", L, (h + 1) // 2))
                            act.wait_ge(sem["full"], value("full", "s", 2 + L, 4 * (h - 1) + 3))
                            evict(QN[:, (h + 1) % 2, :], "qn", L, h + 1, scale=float(QK) ** -0.5)
                for n in range(KD):
                    split_through(("o2", L, n))
                    act.wait_ge(sem["x_new"], value("x_new", f"f{L}", n))
                    square(f"f{L}", n, SQT)
                norm_hi(f"f{L}", NTMP, mod[:, L, 3 * KD:4 * KD])
                for half in range(2):
                    for f in range(half * FH, half * FH + FH):
                        split_through(("fg", L, f))
                        if f >= 2:
                            act.wait_ge(sem["hid"], value("hid", L, f - 2))
                        evict(SILU[:, f % 2, :], "fg", L, f, func=ACT.Silu)
                        split_through(("fu", L, f))
                        act.wait_ge(sem["hid"], value("hid", L, f))
                        nc.scalar.activation(HDH[:, f % FH, :], HF[:, f % 2, :], ACT.Copy).then_inc(
                            sem["hid_hi"], mark("hid_hi", L, f))
                    for n in range(KD):
                        split_through(fo_slot(L, half, n))
                        if half == 1:
                            tag = next_norm(L)
                            act.wait_ge(sem["x_new"], value("x_new", tag, n))
                            square(tag, n, SQT)
                        else:
                            act.wait_ge(sem["x_half"], value("x_half", L, n))

        @block.vector
        def _(dve):
            V = nc.vector
            ada_next = [0]
            ada_list = [k for k in STREAM if k[0] == "ada" and not in_attention(k)]

            def ada_through(key, behind=1):
                while ada_next[0] < len(ada_list) and SLOT[ada_list[ada_next[0]]] <= SLOT[key] + behind:
                    ada_one()

            def ada_one():
                k = ada_list[ada_next[0]]
                _, layer, i = k
                cb, r = divmod(i, 8)
                acc = ACC[:, cb % 2, :]
                c = vec1[:, 2 * KD + r:2 * KD + r + 1]
                dve.wait_ge(landed[ring(k)], loads(k))
                if r == 0:
                    if cb >= 2:
                        dve.wait_ge(sem["full"], value("full", "mod", layer, cb - 2))
                    elif layer:
                        dve.wait_ge(sem["full"], value("full", "mod", layer - 1, ADA // 8 - 2 + cb))
                    ins = V.tensor_scalar(acc, raw(k)[:], c, None, ALU.mult)
                else:
                    dve.wait_ge(sem["ada"], value("ada", layer, i - 1))
                    ins = V.scalar_tensor_tensor(out=acc, in0=raw(k)[:], scalar=c, in1=acc, op0=ALU.mult,
                                                 op1=ALU.add)
                ins.then_inc(sem["ada"], mark("ada", layer, i))
                ada_next[0] += 1

            def mods(key):
                for layer, cb in MODS.get(key, ()):
                    dve.wait_ge(sem["full"], value("full", "mod", layer, cb))
                    b = bank_of("mod", layer, cb)
                    V.tensor_tensor(mod[:, layer, 8 * cb:8 * cb + 8], b[:, 0:8],
                                    par[:, layer, PB_ADA + 8 * cb:PB_ADA + 8 * cb + 8], ALU.add).then_inc(
                        sem["read_dve"], mark("read_dve", "mod", layer, cb))
                    if cb in (1, 4):
                        dve.wait_ge(sem["read_dve"], value("read_dve", "mod", layer, cb))
                        V.tensor_scalar(sc1[:, layer, cb // 4, :], mod[:, layer, 8 * cb:8 * cb + 8], 1.0, None,
                                        ALU.add).then_inc(step, 1)
                        dve.wait_ge(step, own())

            def rsqrt(y, v, t):
                V.tensor_scalar(y.bitcast(I32), v.bitcast(I32), 1, None, ALU.arith_shift_right).then_inc(
                    step, 1)
                dve.wait_ge(step, own())
                V.tensor_scalar(y.bitcast(I32), y.bitcast(I32), -1.0, float(0x5F3759DF), ALU.mult, ALU.add).then_inc(
                    step, 1)
                dve.wait_ge(step, own())
                for _ in range(3):
                    V.tensor_tensor(t, y, y, ALU.mult).then_inc(step, 1)
                    dve.wait_ge(step, own())
                    V.scalar_tensor_tensor(out=t, in0=t, scalar=-0.5, in1=v, op0=ALU.mult, op1=ALU.mult).then_inc(
                        step, 1)
                    dve.wait_ge(step, own())
                    V.scalar_tensor_tensor(out=y, in0=t, scalar=1.5, in1=y, op0=ALU.add, op1=ALU.mult).then_inc(
                        step, 1)
                    dve.wait_ge(step, own())

            def norm(tag, tmp, gain, shift):
                dve.wait_ge(sem["full"], value("full", "ss", tag))
                b = bank_of("ss", tag)
                V.tensor_scalar(stat[:, 0, :], b[:, 0:NT], 1.0 / D, EPS, ALU.mult, ALU.add).then_inc(
                    sem["read_dve"], mark("read_dve", "ss", tag))
                dve.wait_ge(sem["read_dve"], value("read_dve", "ss", tag))
                rsqrt(stat[:, 1, :], stat[:, 0, :], stat[:, 2, :])
                note[("rstd", tag)] = count["step"]
                dve.wait_ge(sem["full"], value("full", "rb", tag))
                b = bank_of("rb", tag)
                for k in range(KD + 1):
                    if k < KD:
                        dst = tmp(k)
                        if k >= 2 and tag != "fin":
                            dve.wait_ge(sem["h_lo"], value("h_lo", tag, k - 2))
                        ins = V.scalar_tensor_tensor(out=dst, in0=X[:, k, :], scalar=gain[:, k:k + 1], in1=b[:],
                                                     op0=ALU.mult, op1=ALU.mult)
                        ins.then_inc(sem["normed"], mark("normed", tag, k))
                    if k and tag != "fin":
                        dve.wait_ge(sem["h_hi"], value("h_hi", tag, k - 1))
                        if shift is None:
                            ins = V.tensor_tensor(HL[:, k - 1, :], tmp(k - 1), HH[:, k - 1, :].bitcast(F32),
                                                  ALU.subtract)
                        else:
                            ins = V.scalar_tensor_tensor(out=HL[:, k - 1, :], in0=tmp(k - 1),
                                                         scalar=shift[:, k - 1:k],
                                                         in1=HH[:, k - 1, :].bitcast(F32), op0=ALU.add,
                                                         op1=ALU.subtract)
                        ins.then_inc(sem["h_lo"], mark("h_lo", tag, k - 1))

            def tables(tab, cs, row, scale, parts=P):
                nt = cs.shape[2]
                g = [spread(gains[0:parts, row, HALF * i:HALF * i + HALF], "p (o d) -> p o d", [parts, nt, HALF])
                     for i in range(2)]
                for out, src, s, gi in ((tab[:, 0, :, 0:HALF], 0, scale, 0), (tab[:, 0, :, HALF:DH], 0, scale, 1),
                                        (tab[:, 1, :, 0:HALF], 1, -scale, 1), (tab[:, 1, :, HALF:DH], 1, scale, 0)):
                    last = V.scalar_tensor_tensor(out=out, in0=cs[:, src], scalar=s, in1=g[gi], op0=ALU.mult,
                                                  op1=ALU.mult)
                last.then_inc(step, 1)
                dve.wait_ge(step, own())

            def rope(x, cos, sin, rstd, t0, t1, out=None):
                V.tensor_tensor(t0, x, cos, ALU.mult)
                V.tensor_tensor(t1[:, :, :, 0:HALF], x[:, :, :, HALF:DH], sin[:, :, :, 0:HALF], ALU.mult)
                V.tensor_tensor(t1[:, :, :, HALF:DH], x[:, :, :, 0:HALF], sin[:, :, :, HALF:DH], ALU.mult).then_inc(
                    step, 1)
                dve.wait_ge(step, own())
                out = x if out is None else out
                if rstd is None:
                    V.tensor_tensor(out, t0, t1, ALU.add).then_inc(step, 1)
                    dve.wait_ge(step, own())
                else:
                    V.tensor_tensor(t0, t0, t1, ALU.add).then_inc(step, 1)
                    dve.wait_ge(step, own())
                    V.tensor_tensor(out, t0, rstd, ALU.mult).then_inc(step, 1)
                    dve.wait_ge(step, own())

            def tmp4(i, x4, buf=None):
                _, A, B, _ = x4.shape
                return (TMP[:, i, :] if buf is None else buf)[0:x4.shape[0], 0:A * B * DH].rearrange(
                    "p (a b d) -> p a b d", a=A, b=B)

            def rope_tok(x4, tab, t0, A, B, rstd=None, bufs=(None, None)):
                shape = [P, A, B, DH]
                cos = spread(tab[:, 0, t0:t0 + A, :], "p a (o d) -> p a o d", shape)
                sin = spread(tab[:, 1, t0:t0 + A, :], "p a (o d) -> p a o d", shape)
                rope(x4, cos, sin, rstd, tmp4(0, x4, bufs[0]), tmp4(1, x4, bufs[1]))

            def head_rstd(x4, col, n):
                t0 = tmp4(0, x4)
                V.tensor_tensor(t0, x4, x4, ALU.mult).then_inc(step, 1)
                dve.wait_ge(step, own())
                _, A, B, _ = x4.shape
                V.tensor_reduce(kst[:, 0, col:col + n].rearrange("p (a b) -> p a b", a=A), t0, AX_X, ALU.add).then_inc(
                    step, 1)
                dve.wait_ge(step, own())

            def finish_rstd(n, width=DH):
                V.tensor_scalar(kst[:, 0, 0:n], kst[:, 0, 0:n], 1.0 / width, EPS, ALU.mult, ALU.add).then_inc(
                    step, 1)
                dve.wait_ge(step, own())
                rsqrt(kst[:, 1, 0:n], kst[:, 0, 0:n], kst[:, 2, 0:n])

            def rope2_tables(tab):
                dve.wait_ge(sem["cos_sin"], value("cos_sin"))
                V.tensor_copy(tab[:, 0, :, 0:HALF], cs2[:, 0])
                V.tensor_copy(tab[:, 0, :, HALF:DH], cs2[:, 0])
                V.tensor_scalar(tab[:, 1, :, 0:HALF], cs2[:, 1], -1.0, None, ALU.mult)
                V.tensor_copy(tab[:, 1, :, HALF:DH], cs2[:, 1]).then_inc(step, 1)
                dve.wait_ge(step, own())

            def out_head(L, h):
                dve.wait_ge(sem["full"], value("full", "o", 2 + L, h))
                b = bank_of("o", 2 + L, h)
                V.tensor_tensor(YT[:, h % 2, :], SG[:, h, :], b[:], ALU.mult).then_inc(
                    sem["yb"], mark("yb", L, h))
                dve.wait_ge(sem["yb"], value("yb", L, h))
                V.tensor_tensor(YT[:, h % 2, :], YT[:, h % 2, :], YA[:, h, :], ALU.add).then_inc(
                    sem["y_full"], mark("y_full", L, h))

            def out_head_lo(L, h):
                dve.wait_ge(sem["y_hi"], value("y_hi", L, h))
                V.tensor_tensor(YL[:, h, :], YT[:, h % 2, :], YH[:, h, :].bitcast(F32), ALU.subtract).then_inc(
                    sem["y_lo"], mark("y_lo", L, h))

            for k in range(1, KD):
                dve.wait_ge(sem["square"], value("square", "n1", k))
                if k > 1:
                    dve.wait_ge(sem["n1_added"], value("n1_added", "n1", k - 1))
                V.tensor_tensor(SQS[:], RELU[:, 0, :] if k == 1 else SQS[:], RELU[:, k % 2, :], ALU.add).then_inc(
                    sem["n1_added"], mark("n1_added", "n1", k))
            dve.wait_ge(sem["norm_consts"], value("norm_consts"))
            norm("n1", lambda k: TMP[:, k % 2, :], vec1[:, 0:KD], None)
            dve.wait_ge(sem["consts"], value("consts", "all"))
            V.tensor_copy(identb[:], ident[:])
            V.tensor_copy(causal[:], ACC[:, 0, 0:P])
            V.tensor_scalar(reset[:], ACC[:, 1, 0:S].bitcast(I32), 0.0, None, ALU.is_equal)
            V.tensor_scalar(keep[:], ACC[:, 1, 0:S].bitcast(I32), 0.0, None, ALU.not_equal).then_inc(step, 1)
            dve.wait_ge(step, own())
            note[("setup",)] = count["step"]

            dve.wait_ge(sem["lru_par"], value("lru_par", 1))
            V.tensor_scalar(lt[:, 2], lt[:, 1], 1.0, None, ALU.add).then_inc(sem["lru_w"], mark("lru_w"))
            dve.wait_ge(sem["lru_w"], value("lru_w"))
            V.tensor_scalar(lt[:, 4], lt[:, 2], -1.0, None, ALU.add).then_inc(step, 1)
            dve.wait_ge(step, own())
            V.tensor_scalar(lt[:, 5], lt[:, 4], 0.0, None, ALU.is_equal).then_inc(step, 1)
            dve.wait_ge(step, own())
            V.tensor_tensor(lt[:, 4], lt[:, 4], lt[:, 5], ALU.add).then_inc(step, 1)
            dve.wait_ge(step, own())
            V.reciprocal(lt[:, 4], lt[:, 4]).then_inc(step, 1)
            dve.wait_ge(step, own())
            dve.wait_ge(sem["lru_par"], value("lru_par", 2))
            V.tensor_tensor(lt[:, 3], lt[:, 3], lt[:, 5], ALU.add).then_inc(step, 1)
            dve.wait_ge(step, own())
            V.tensor_tensor(lt[:, 4], lt[:, 4], lt[:, 1], ALU.mult).then_inc(step, 1)
            dve.wait_ge(step, own())
            V.tensor_tensor(lt[:, 4], lt[:, 4], lt[:, 3], ALU.mult).then_inc(step, 1)
            dve.wait_ge(step, own())
            V.tensor_scalar(lt[:, 0], par[:, :, PA:PA + KD], -1.0, 0.0, ALU.mult, ALU.max).then_inc(step, 1)
            dve.wait_ge(step, own())
            V.tensor_tensor(lt[:, 4], lt[:, 4], lt[:, 0], ALU.add).then_inc(step, 1)
            dve.wait_ge(step, own())
            V.tensor_scalar(csc[:], lt[:, 4], -LRU_C, None, ALU.mult).then_inc(step, 1)
            dve.wait_ge(step, own())
            note[("csc",)] = count["step"]

            ada_through(("p1", 1, 1))
            tables(TAB, CS1, G_ONE, DH ** -0.5)
            for t in range(0, NT, 2):
                dve.wait_ge(sem["read_act"], value("read_act", "p1", 0, t + 1))
                rope_tok(MISC[:, t:t + 2, 0:256].rearrange("p a (b d) -> p a b d", d=DH), TAB, t, 2, 4)
            tables(TAB, CS1, G_ONE, 1.0)
            rope_tok(MISC[:, :, 256:384].rearrange("p a (b d) -> p a b d", d=DH), TAB, 0, NT, 2)
            note[("roped", 0)] = count["step"]

            ada_through(("p1", 1, 3))
            V.tensor_copy(posf[:], posi[:]).then_inc(step, 1)
            dve.wait_ge(step, own())
            ang = TMP[:, 0, 0:P].rearrange("p (t f) -> p t f", t=NT)
            turn = TMP[:, 0, P:2 * P].rearrange("p (t f) -> p t f", t=NT)
            red = TMP[:, 0, 2 * P:3 * P].rearrange("p (t f) -> p t f", t=NT)
            for t in range(NT):
                last = V.tensor_scalar(ang[:, t, :], freq[:], posf[:, t:t + 1], None, ALU.mult)
            last.then_inc(step, 1)
            dve.wait_ge(step, own())
            c1, c2, c3 = 6.28125, 0.00193500518798828125, 3.0176e-07
            c2 = float(np.float32(round((2 * math.pi - c1) * 2 ** 18) / 2 ** 18))
            c3 = float(np.float32(round((2 * math.pi - c1 - c2) * 2 ** 30) / 2 ** 30))
            c4 = 2 * math.pi - c1 - c2 - c3
            big = float(3 * 2 ** 22)
            for i, quarter in ((1, 0.0), (0, 0.25)):
                V.tensor_scalar(turn, ang, 1.0 / (2 * math.pi), quarter, ALU.mult, ALU.add).then_inc(step, 1)
                dve.wait_ge(step, own())
                V.tensor_scalar(turn, turn, big, None, ALU.add).then_inc(step, 1)
                dve.wait_ge(step, own())
                V.tensor_scalar(turn, turn, -big, None, ALU.add).then_inc(step, 1)
                dve.wait_ge(step, own())
                V.scalar_tensor_tensor(out=red, in0=turn, scalar=-c1, in1=ang, op0=ALU.mult, op1=ALU.add).then_inc(
                    step, 1)
                dve.wait_ge(step, own())
                for c in (c2, c3, c4):
                    V.scalar_tensor_tensor(out=red, in0=turn, scalar=-c, in1=red, op0=ALU.mult, op1=ALU.add).then_inc(
                        step, 1)
                    dve.wait_ge(step, own())
                if quarter:
                    V.tensor_scalar(red, red, math.pi / 2, None, ALU.add).then_inc(step, 1)
                    dve.wait_ge(step, own())
                V.tensor_scalar(cs2[:, i], red, 3.1415925, -3.1415925, ALU.min, ALU.max).then_inc(step, 1)
                dve.wait_ge(step, own())
            note[("angles",)] = count["step"]

            def rope_keys():
                for i, row in enumerate((G_KS, G_KW, G_KD)):
                    x4 = G[1][:, :, i * P:(i + 1) * P].rearrange("p a (b d) -> p a b d", d=DH)
                    if i == 0:
                        dve.wait_ge(sem["read_act"], value("read_act", "p1", 1, 3))
                    head_rstd(x4, 8 * i, 8)
                finish_rstd(24)
                for i, row in enumerate((G_KS, G_KW, G_KD)):
                    x4 = G[1][:, :, i * P:(i + 1) * P].rearrange("p a (b d) -> p a b d", d=DH)
                    tables(TAB, CS1, row, 1.0)
                    r = spread(kst[:, 1, 8 * i:8 * i + 8].rearrange("p (a b) -> p a b", a=NT),
                               "p a (b o) -> p a b o", [P, NT, 2, DH])
                    rope_tok(x4, TAB, 0, NT, 2, r)
                note[("roped", 1)] = count["step"]

            def rope_queries(g, row):
                tables(TAB, CS1, row, DH ** -0.5)
                x4 = [G[g][:, t:t + 1, :].rearrange("p a (b d) -> p a b d", d=DH) for t in range(NT)]
                for t in range(NT):
                    dve.wait_ge(sem["read_act"], value("read_act", "p1", g, t))
                    head_rstd(x4[t], 8 * t, 8)
                finish_rstd(32)
                for t in range(NT):
                    r = spread(kst[:, 1, 8 * t:8 * t + 8].rearrange("p (a b) -> p a b", a=1),
                               "p a (b o) -> p a b o", [P, 1, 8, DH])
                    rope_tok(x4[t], TAB, t, 1, 8, r)
                note[("roped", g)] = count["step"]

            def index_scores(qt):
                n = (qt + 1) * P
                dve.wait_ge(sem["full"], value("full", "idx", qt, 0))
                b = bank_of("idx", qt, 0)
                V.tensor_scalar(SCORE[:, 0:n], b[:, 0:n], 0.0, gate[:, qt, 24:25], ALU.max, ALU.mult).then_inc(
                    sem["read_dve"], mark("read_dve", "idx", qt, 0))
                dve.wait_ge(sem["read_dve"], value("read_dve", "idx", qt, 0))
                for h in range(1, 4):
                    dve.wait_ge(sem["read_act"], value("read_act", "idx", qt, h))
                    V.scalar_tensor_tensor(out=SCORE[:, 0:n], in0=RELU[:, h - 1, 0:n],
                                           scalar=gate[:, qt, 24 + h:25 + h], in1=SCORE[:, 0:n],
                                           op0=ALU.mult, op1=ALU.add).then_inc(
                        sem["iscore"], mark("iscore", qt, h))
                    dve.wait_ge(sem["iscore"], value("iscore", qt, h))
                V.tensor_tensor(SCORE[:, n - P:n], SCORE[:, n - P:n], causal[:], ALU.add).then_inc(step, 1)
                dve.wait_ge(step, own())
                V.tensor_scalar(SCORE[:, 0:n], SCORE[:, 0:n], 0.0, None, ALU.add).then_inc(step, 1)
                dve.wait_ge(step, own())

            def take_topk(qt):
                n = (qt + 1) * P
                for _ in range(TOPK // 8):
                    topk_round(n)
                topk_mask(qt)

            def topk_round(n):
                V.max(TKM[:], SCORE[:, 0:n]).then_inc(step, 1)
                dve.wait_ge(step, own())
                V.match_replace(SCORE[:, 0:n], TKM[:], SCORE[:, 0:n], TAKEN).then_inc(step, 1)
                dve.wait_ge(step, own())

            def topk_mask(qt):
                n = (qt + 1) * P
                V.tensor_scalar(MASKB[:, qt - 1, 0:n], SCORE[:, 0:n], TAKEN, NEG, ALU.not_equal, ALU.mult).then_inc(
                    sem["topk"], mark("topk", qt))
                dve.wait_ge(sem["topk"], value("topk", qt))

            ada_through(("p1", 4, 2))
            rope_keys()
            ada_through(("p1", 4, 3))
            index_scores(1)
            take_topk(1)
            mods(("p1", 2, 3))
            index_scores(2)
            rope_queries(2, G_Q)
            take_topk(2)
            index_scores(3)
            rope_queries(3, G_QD)
            dve.wait_ge(sem["read_act"], value("read_act", "co", 0))
            C = 2 * NCMP
            c4 = CK[0:C, 0:1, :].rearrange("p a (b d) -> p a b d", b=1)
            V.tensor_tensor(CK[0:C, 1, :], CK[0:C, 0, :], CK[0:C, 0, :], ALU.mult).then_inc(step, 1)
            dve.wait_ge(step, own())
            V.tensor_reduce(kst[0:C, 0, 0:1], CK[0:C, 1, :], AX_X, ALU.add).then_inc(step, 1)
            dve.wait_ge(step, own())
            V.tensor_scalar(kst[0:C, 0, 0:1], kst[0:C, 0, 0:1], 1.0 / DH, EPS, ALU.mult, ALU.add).then_inc(
                step, 1)
            dve.wait_ge(step, own())
            rsqrt(kst[0:C, 1, 0:1], kst[0:C, 0, 0:1], kst[0:C, 2, 0:1])
            tables(TAB[0:C, :, 0:1], cscmp[0:C].rearrange("p c (o f) -> p c o f", o=1), G_KC, 1.0, parts=C)
            rope(c4, TAB[0:C, 0:1, 0:1, :], TAB[0:C, 1:2, 0:1, :], None,
                 CK[0:C, 1:2, :].rearrange("p a (b d) -> p a b d", b=1),
                 CK[0:C, 2:3, :].rearrange("p a (b d) -> p a b d", b=1))
            V.tensor_scalar(CK[0:C, 0, :], CK[0:C, 0, :], kst[0:C, 1, 0:1], None, ALU.mult).then_inc(step, 1)
            dve.wait_ge(step, own())
            note[("cmp_key",)] = count["step"]
            for i in range(4):
                dve.wait_ge(sem["full"], value("full", "tqd", i))
                b = bank_of("tqd", i)
                V.tensor_copy(QDT[:, i, :], b[:]).then_inc(sem["read_dve"], mark("read_dve", "tqd", i))

            nU = len(UNITS1)
            for u in range(nU + O_LAG):
                if u < nU:
                    n = (UNITS1[u][3] + 1) * P
                    dve.wait_ge(sem["full"], value("full", "s", 1, u))
                    b = bank_of("s", 1, u)
                    V.tensor_reduce(nmax[:, u % 8:u % 8 + 1], b[:, 0:n], AX_X, ALU.max, negate=True).then_inc(
                        sem["nmax"], mark("nmax", 1, u))
                v = u - T_LAG
                if 0 <= v < nU and evictor(v) == "read_dve":
                    n = (UNITS1[v][3] + 1) * P
                    dve.wait_ge(sem["full"], value("full", "t", 1, v))
                    b = bank_of("t", 1, v)
                    if v >= RING:
                        dve.wait_ge(sem["full"], value("full", "o", 1, v - RING))
                    V.tensor_copy(PT1[:, v % RING, 0:n], b[:, 0:n]).then_inc(
                        sem["read_dve"], mark("read_dve", "t", 1, v))
                v = u - O_LAG
                if v >= 0 and v % 2:
                    br, j, _, qt = UNITS1[v]
                    cc = coef[:, (v - 1) % 8:v % 8 + 1]
                    dve.wait_ge(sem["read_act"], value("read_act", "s", 1, v))
                    V.reciprocal(cc, rsum[:, (v - 1) % 8:v % 8 + 1]).then_inc(step, 1)
                    dve.wait_ge(step, own())
                    if br < 2:
                        c = 3 * j + 1 + br
                        V.tensor_tensor(cc, cc, gate[:, qt, c:c + 13:12], ALU.mult).then_inc(step, 1)
                        dve.wait_ge(step, own())
                    for g in range(2):
                        unit = v - 1 + g
                        cc = coef[:, unit % 8:unit % 8 + 1]
                        dve.wait_ge(sem["full"], value("full", "o", 1, unit))
                        b = bank_of("o", 1, unit)
                        head = 4 * g + j
                        if br == 1:
                            dst = MIX[:, qt, head * DH:(head + 1) * DH]
                            V.scalar_tensor_tensor(out=dst, in0=b[:, 0:DH], scalar=cc, in1=dst, op0=ALU.mult,
                                                   op1=ALU.add).then_inc(
                                sem["read_dve"], mark("read_dve", "o", 1, unit))
                        else:
                            first = (8 + head if br else head) * DH
                            dst = MIX[:, qt, first:first + DH]
                            V.tensor_scalar(dst, b[:, 0:DH], cc, None, ALU.mult).then_inc(
                                sem["read_dve"], mark("read_dve", "o", 1, unit))
                mods(("att", u))
                if u in TOPK_UNITS:
                    topk_round(S)
                    if u == TOPK_UNITS[-1]:
                        topk_mask(3)
                qt = cmp_tile(u, CMP_MASK)
                if qt is not None:
                    pc = PC[:, qt % 2]
                    if qt >= 2:
                        dve.wait_ge(sem["full"], value("full", "ct", qt - 2))
                    for g in range(2):
                        dve.wait_ge(sem["full"], value("full", "cs", qt, g))
                        b = bank_of("cs", qt, g)
                        V.tensor_tensor(pc[:, 4 * g:4 * g + 4], b[:, 0:P].rearrange("p (h c) -> p h c", c=NCMP),
                                        spread(cmask[:, qt, :], "p (o c) -> p o c", [P, 4, NCMP]), ALU.add).then_inc(
                            sem["read_dve"], mark("read_dve", "cs", qt, g))
                    dve.wait_ge(sem["read_dve"], value("read_dve", "cs", qt, 1))
                    V.tensor_reduce(CST[:, 0, :], pc, AX_X, ALU.max).then_inc(step, 1)
                    dve.wait_ge(step, own())
                    V.tensor_tensor(pc, pc, spread(CST[:, 0, :], "p (h o) -> p h o", [P, 8, NCMP]),
                                    ALU.subtract).then_inc(sem["cmp_shift"], mark("cmp_shift", qt))
                qt = cmp_tile(u, CMP_NORM)
                if qt is not None:
                    pc = PC[:, qt % 2]
                    dve.wait_ge(sem["cmp_exp"], value("cmp_exp", qt))
                    V.tensor_reduce(CST[:, 1, :], pc, AX_X, ALU.add).then_inc(step, 1)
                    dve.wait_ge(step, own())
                    V.reciprocal(CST[:, 2, :], CST[:, 1, :]).then_inc(step, 1)
                    dve.wait_ge(step, own())
                    V.scalar_tensor_tensor(
                        out=CST[:, 3, :], in0=CST[:, 2, :], scalar=cvalid[:, qt:qt + 1],
                        in1=gate[:, qt, 0:24].rearrange("p (h b) -> p h b", b=3)[:, :, 0], op0=ALU.mult,
                        op1=ALU.mult).then_inc(step, 1)
                    dve.wait_ge(step, own())
                    V.tensor_tensor(pc, pc, spread(CST[:, 3, :], "p (h o) -> p h o", [P, 8, NCMP]),
                                    ALU.mult).then_inc(sem["cmp_p"], mark("cmp_p", qt))
                qt = cmp_tile(u, CMP_ADD)
                if qt is not None:
                    dve.wait_ge(sem["full"], value("full", "cpv", qt))
                    b = bank_of("cpv", qt)
                    dve.wait_ge(sem["read_dve"], max(1, count["read_dve"]))
                    V.tensor_tensor(MIX[:, qt, 0:512], MIX[:, qt, 0:512], b[:], ALU.add).then_inc(
                        sem["read_dve"], mark("read_dve", "cpv", qt))
            for i in range(KD):
                dve.wait_ge(sem["full"], value("full", "tm", i))
                b = bank_of("tm", i)
                dve.wait_ge(sem["mix_hi"], value("mix_hi", i))
                V.tensor_tensor(HL[:, i, :], b[:], HH[:, i, :].bitcast(F32), ALU.subtract).then_inc(
                    sem["read_dve"], mark("read_dve", "tm", i))
            for n in range(KD):
                ada_through(("o1", n), 6)
                dve.wait_ge(sem["full"], value("full", "o1", n))
                b = bank_of("o1", n)
                V.tensor_tensor(X[:, n, :], X[:, n, :], b[:], ALU.add).then_inc(
                    sem["x_new"], mark("x_new", "m0", n))
                mods(("o1", n)) if n < KD - 1 else None
            ada_through(("xl", 0, 0))
            mods(("o1", KD - 1))

            for layer in range(LAYERS):
                L = layer

                def vec(col):
                    return par[:, L, col:col + 1]

                norm(f"m{L}", lambda k: NTMP[:, k % 2, :], sc1[:, L, 0, :], mod[:, L, 0:KD])
                for n in range(KD):
                    dve.wait_ge(sem["full"], value("full", "xl", L, n))
                    b = bank_of("xl", L, n)
                    xc = XC[:, n, :]
                    V.tensor_scalar(xc, b[:], vec(PCONV_W + 4 * n + 3), vec(PCONV_B + n), ALU.mult, ALU.add).then_inc(
                        step, 1)
                    dve.wait_ge(step, own())
                    for d in range(1, 4):
                        ins = V.scalar_tensor_tensor(out=xc[:, d:S], in0=b[:, 0:S - d],
                                                     scalar=vec(PCONV_W + 4 * n + 3 - d), in1=xc[:, d:S],
                                                     op0=ALU.mult, op1=ALU.add)
                        if d < 3:
                            ins.then_inc(step, 1)
                            dve.wait_ge(step, own())
                    ins.then_inc(sem["conv"], mark("conv", L, n))
                    note[("conv", L, n)] = count["conv"]
                    dve.wait_ge(sem["xc_hi"], value("xc_hi", L, n))
                    V.tensor_tensor(XCL[:, n % 2, :], xc, XCH[:, n % 2, :].bitcast(F32), ALU.subtract).then_inc(
                        sem["xc_lo"], mark("xc_lo", L, n))
                for n in range(KD):
                    dve.wait_ge(sem["lru_a"], value("lru_a", L, n))
                    V.tensor_tensor(YT[:, n % 2, :], LR[:, n, :], LR[:, n, :], ALU.mult).then_inc(step, 1)
                    dve.wait_ge(step, own())
                    V.scalar_tensor_tensor(out=YA[:, n, :], in0=YT[:, n % 2, :], scalar=1.0, in1=YA[:, n, :],
                                           op0=ALU.add, op1=ALU.mult).then_inc(
                        sem["one_aa"], mark("one_aa", L, n))
                dve.wait_ge(sem["read_act"], value("read_act", "kvq", L, NT - 1))
                for t in range(NT):
                    sq = YT[:, 0, 0:384]
                    V.tensor_tensor(sq, KVR[:, t, 0:384], KVR[:, t, 0:384], ALU.mult).then_inc(step, 1)
                    dve.wait_ge(step, own())
                    V.tensor_reduce(kst[:, 0, t:t + 1], sq[:, 0:Q_RANK], AX_X, ALU.add)
                    V.tensor_reduce(kst[:, 0, NT + t:NT + t + 1], sq[:, Q_RANK:384], AX_X, ALU.add).then_inc(
                        step, 1)
                    dve.wait_ge(step, own())
                V.tensor_scalar(kst[:, 0, 0:NT], kst[:, 0, 0:NT], 1.0 / Q_RANK, EPS, ALU.mult, ALU.add)
                V.tensor_scalar(kst[:, 0, NT:2 * NT], kst[:, 0, NT:2 * NT], 1.0 / KV_RANK, EPS, ALU.mult,
                                ALU.add).then_inc(step, 1)
                dve.wait_ge(step, own())
                rsqrt(kst[:, 1, 0:2 * NT], kst[:, 0, 0:2 * NT], kst[:, 2, 0:2 * NT])
                for t in range(NT):
                    V.tensor_scalar(KVR[:, t, 0:Q_RANK], KVR[:, t, 0:Q_RANK], kst[:, 1, t:t + 1], None, ALU.mult)
                    ins = V.tensor_scalar(KVR[:, t, Q_RANK:384], KVR[:, t, Q_RANK:384],
                                          kst[:, 1, NT + t:NT + t + 1], None, ALU.mult)
                ins.then_inc(step, 1)
                dve.wait_ge(step, own())
                rope2_tables(TAB2K)
                rope_tok(KVR[:, :, 384:448].rearrange("p a (b d) -> p a b d", b=1), TAB2K, 0, NT, 1,
                         bufs=(YT[:, 0, :], YT[:, 1, :]))
                note[("latents", L)] = count["step"]
                for n in range(KD):
                    if n == 0:
                        dve.wait_ge(sem["read_act"], value("read_act", "li", L, KD - 1))
                    V.tensor_tensor(LR[:, n, :], LR[:, n, :], keep[:], ALU.mult)
                    V.tensor_tensor(XC[:, n, :], XC[:, n, :], LI[:, n, :], ALU.mult).then_inc(step, 1)
                    dve.wait_ge(step, own())
                    dve.wait_ge(sem["mult"], value("mult", L, n))
                    V.tensor_tensor(YA[:, n, :], YA[:, n, :], reset[:], ALU.max).then_inc(step, 1)
                    dve.wait_ge(step, own())
                    V.tensor_tensor(XC[:, n, :], XC[:, n, :], YA[:, n, :], ALU.mult).then_inc(step, 1)
                    dve.wait_ge(step, own())
                    V.tensor_tensor_scan(YA[:, n, :], LR[:, n, :], XC[:, n, :], 0.0, ALU.mult, ALU.add).then_inc(
                        step, 1)
                    dve.wait_ge(step, own())
                    if n >= 4:
                        dve.wait_ge(sem["read_act"], value("read_act", "ga", L, n))
                    V.tensor_tensor(YA[:, n, :], YA[:, n, :], SG[:, n, :], ALU.mult).then_inc(
                        sem["ya_gated"], mark("ya_gated", L, n))
                for i in (2, 0, 1):
                    dve.wait_ge(sem["full"], value("full", "tc2", L, i))
                    b = bank_of("tc2", L, i)
                    dve.wait_ge(sem["c_hi"], value("c_hi", L, i))
                    h_, l_ = (CQH[:, i, :], CQL[:, i, :]) if i < 2 else (CKH[:], CKL[:])
                    V.scalar_tensor_tensor(out=l_, in0=b[:], scalar=vec(PQG + i), in1=h_.bitcast(F32),
                                           op0=ALU.mult, op1=ALU.subtract).then_inc(
                        sem["read_dve"], mark("read_dve", "tc2", L, i))
                rope2_tables(TAB2)
                for t in range(NT):
                    dve.wait_ge(sem["read_act"], value("read_act", "qr", L, t))
                    rope_tok(QRR[:, t:t + 1, :].rearrange("p a (b d) -> p a b d", d=DH), TAB2, t, 1, 8,
                             bufs=(YT[:, 0, :], YT[:, 1, :]))
                note[("q_roped", L)] = count["step"]
                for h in range(2):
                    dve.wait_ge(sem["full"], value("full", "kn", L, h))
                    b = bank_of("kn", L, h)
                    V.tensor_copy(KN[:, h, :], b[:]).then_inc(sem["read_dve"], mark("read_dve", "kn", L, h))
                nU = len(UNITS2)
                for u in range(nU + O_LAG):
                    if u < nU:
                        n = (UNITS2[u][1] + 1) * P
                        dve.wait_ge(sem["full"], value("full", "s", 2 + L, u))
                        b = bank_of("s", 2 + L, u)
                        V.tensor_reduce(nmax[:, u % 8:u % 8 + 1], b[:, 0:n], AX_X, ALU.max, negate=True).then_inc(
                            sem["nmax"], mark("nmax", 2 + L, u))
                    v = u - 1
                    if 0 <= v < nU:
                        n = (UNITS2[v][1] + 1) * P
                        cc = coef[:, v % 8:v % 8 + 1]
                        dve.wait_ge(sem["read_act"], value("read_act", "s", 2 + L, v))
                        V.reciprocal(cc, rsum[:, v % 8:v % 8 + 1]).then_inc(step, 1)
                        dve.wait_ge(step, own())
                        V.tensor_scalar(P2[:, v % RING, 0:n], P2[:, v % RING, 0:n], cc, None, ALU.mult).then_inc(
                            sem["p_norm"], mark("p_norm", 2 + L, v))
                    v = u - T_LAG
                    if 0 <= v < nU and evictor(v) == "read_dve":
                        h, qt = UNITS2[v]
                        n = (qt + 1) * P
                        if h >= 2:
                            dve.wait_ge(sem["full"], value("full", "o", 2 + L, h - 2))
                        dve.wait_ge(sem["full"], value("full", "t", 2 + L, v))
                        b = bank_of("t", 2 + L, v)
                        V.tensor_copy(PT2[:, h % 2, 0:qt + 1, qt * P:(qt + 1) * P],
                                      b[:, 0:n].rearrange("p (k q) -> p k q", k=qt + 1)).then_inc(
                            sem["read_dve"], mark("read_dve", "t", 2 + L, v))
                    if u >= 7 and (u - 7) % 4 == 0:
                        out_head(L, (u - 7) // 4)
                    if u >= 8 and (u - 8) % 4 == 0:
                        out_head_lo(L, (u - 8) // 4)
                    if u < nU:
                        h, qt = UNITS2[u]
                        if qt == 1 and 1 <= h < HEADS - 1:
                            dve.wait_ge(sem["full"], value("full", "s", 2 + L, 4 * (h - 1) + 3))
                            dve.wait_ge(sem["full"], value("full", "kn", L, h + 1))
                            b = bank_of("kn", L, h + 1)
                            V.tensor_copy(KN[:, (h + 1) % 2, :], b[:]).then_inc(
                                sem["read_dve"], mark("read_dve", "kn", L, h + 1))
                out_head_lo(L, HEADS - 1)
                for n in range(KD):
                    if n == 6:
                        ada_through(("fu", L, 0))
                    dve.wait_ge(sem["full"], value("full", "o2", L, n))
                    b = bank_of("o2", L, n)
                    V.scalar_tensor_tensor(out=X[:, n, :], in0=b[:], scalar=mod[:, L, 2 * KD + n:2 * KD + n + 1],
                                           in1=X[:, n, :], op0=ALU.mult, op1=ALU.add).then_inc(
                        sem["x_new"], mark("x_new", f"f{L}", n))
                norm(f"f{L}", lambda k: NTMP[:, k % 2, :], sc1[:, L, 1, :], mod[:, L, 3 * KD:4 * KD])
                for half in range(2):
                    for f in range(half * FH, half * FH + FH):
                        ada_through(("fu", L, f), 3)
                        dve.wait_ge(sem["read_act"], value("read_act", "fg", L, f))
                        dve.wait_ge(sem["full"], value("full", "fu", L, f))
                        b = bank_of("fu", L, f)
                        V.tensor_tensor(HF[:, f % 2, :], SILU[:, f % 2, :], b[:], ALU.mult).then_inc(
                            sem["hid"], mark("hid", L, f))
                        dve.wait_ge(sem["hid_hi"], value("hid_hi", L, f))
                        V.tensor_tensor(HDL[:, f % FH, :], HF[:, f % 2, :], HDH[:, f % FH, :].bitcast(F32),
                                        ALU.subtract).then_inc(sem["hid_lo"], mark("hid_lo", L, f))
                        if L == 0:
                            mods(("fu", L, f))
                    for n in range(KD):
                        ada_through(fo_slot(L, half, n))
                        dve.wait_ge(sem["full"], value("full", "fo", L, half, n))
                        b = bank_of("fo", L, half, n)
                        ins = V.scalar_tensor_tensor(out=X[:, n, :], in0=b[:],
                                                     scalar=mod[:, L, 5 * KD + n:5 * KD + n + 1],
                                                     in1=X[:, n, :], op0=ALU.mult, op1=ALU.add)
                        if half:
                            ins.then_inc(sem["x_new"], mark("x_new", next_norm(L), n))
                        else:
                            ins.then_inc(sem["x_half"], mark("x_half", L, n))
                        if L == 0 and (n == KD - 1 or fo_slot(L, half, n + 1) != fo_slot(L, half, n)):
                            mods(fo_slot(L, half, n))
            norm("fin", lambda k: YA[:, k, :], vec1[:, KD:2 * KD], None)

        @block.tensor
        def _(pe):
            jobs, used_before = [], set()

            def claim(*key):
                j = len(jobs)
                jobs.append(key)
                note[("bank",) + key] = j % 8
                if j >= 8:
                    reader = last_reader(jobs[j - 8])
                    pe.wait_ge(sem[reader[0]], value(*reader))
                return bank[j % 8]

            def last_reader(key):
                kind = key[0]
                if kind in ("xl",):
                    return ("conv",) + key[1:]
                if kind == "o1":
                    return ("x_new", "m0", key[1])
                if kind == "o2":
                    return ("x_new", f"f{key[1]}", key[2])
                if kind == "fo":
                    return ("x_new", next_norm(key[1]), key[3]) if key[2] else ("x_half", key[1], key[3])
                if kind == "fu":
                    return ("hid",) + key[1:]
                if kind == "rb":
                    return ("normed", key[1], KD - 1)
                if kind == "o" and key[1] >= 2:
                    return ("yb", key[1] - 2, key[2])
                return ("read_dve",) + key if ("read_dve",) + key in known else ("read_act",) + key

            def full(ins, *key):
                return ins.then_inc(sem["full"], mark("full", *key))

            def used(key, family="full"):
                note[("used",) + key] = (family, count[family])

            def mm3(out, A, B, first, last):
                nc.tensor.matmul(out, A[0], B[0], start=first, stop=False)
                nc.tensor.matmul(out, A[0], B[1], start=False, stop=False)
                return nc.tensor.matmul(out, A[1], B[0], start=False, stop=last)

            def wpair(key, c0, n):
                return hi(key)[:, c0:c0 + n], lo(key)[:, c0:c0 + n]

            def dense_pair(keys, tag):
                b = [claim(*key) for key in keys]
                for key in keys:
                    pe.wait_ge(sem["passed"], value("passed", *key))
                for k in range(KD):
                    pe.wait_ge(sem["h_hi"], value("h_hi", tag, k))
                    for i, key in enumerate(keys):
                        w_hi, w_lo = wpair(key, k * P, P)
                        nc.tensor.matmul(b[i][:], w_hi, HH[:, k, :], start=(k == 0), stop=False)
                        nc.tensor.matmul(b[i][:], w_lo, HH[:, k, :], start=False, stop=False)
                    if first_use("h", tag, k):
                        pe.wait_ge(sem["h_lo"], value("h_lo", tag, k))
                    for i, key in enumerate(keys):
                        w_hi, _ = wpair(key, k * P, P)
                        last = nc.tensor.matmul(b[i][:], w_hi, HL[:, k, :], start=False, stop=(k == KD - 1))
                        if k == KD - 1:
                            full(last, *key)
                            used(key)

            def dense(key, chunks, x):
                b = claim(*key)
                for i, (slot, col) in enumerate(chunks):
                    if i == 0 or slot != chunks[i - 1][0]:
                        pe.wait_ge(sem["passed"], value("passed", *slot))
                    last = mm3(b[:], wpair(slot, col, P), x(i), i == 0, i == len(chunks) - 1)
                full(last, *key)
                for slot in dict.fromkeys(s for s, _ in chunks):
                    used(slot)

            def first_use(*key):
                fresh = key not in used_before
                used_before.add(key)
                return fresh

            def h_pair(tag):
                def x(k):
                    if first_use("h", tag, k):
                        pe.wait_ge(sem["h_lo"], value("h_lo", tag, k))
                    return HH[:, k, :], HL[:, k, :]
                return x

            def tokens(kind, slots, width, tag):
                b = [claim(*kind, tt) for tt in range(NT)]
                for s, slot in enumerate(slots):
                    pe.wait_ge(sem["passed"], value("passed", *slot))
                    for tt in range(NT):
                        for c in range(2):
                            k = 2 * s + c
                            if first_use("h", tag, k):
                                pe.wait_ge(sem["h_lo"], value("h_lo", tag, k))
                            last = mm3(b[tt][:, 0:width],
                                       (HH[:, k, tt * P:(tt + 1) * P], HL[:, k, tt * P:(tt + 1) * P]),
                                       wpair(slot, 512 * c, width), k == 0, k == KD - 1)
                        if s == 3:
                            full(last, *kind, tt)
                    if s < 3:
                        last.then_inc(sem["w_used"], mark("w_used", *slot))
                        used(slot, "w_used")
                    else:
                        used(slot)

            def turn(key, srcs, rows=P):
                b = claim(*key)
                for tt, src in enumerate(srcs):
                    k = src.shape[0]
                    last = nc.tensor.transpose(b[0:rows, tt * k:(tt + 1) * k], src, ident[0:k, 0:k])
                full(last, *key)

            def norm(tag, total):
                adder = "n1_added" if tag == "n1" else "sq_added"
                pe.wait_ge(sem[adder], value(adder, tag, KD - 1))
                if tag == "n1":
                    pe.wait_ge(sem["norm_consts"], value("norm_consts"))
                b = claim("ss", tag)
                for tt in range(NT):
                    last = nc.tensor.matmul(b[:, tt:tt + 1], total[:, tt * P:(tt + 1) * P], ones[:, 0:1],
                                            start=True, stop=True)
                full(last, "ss", tag)
                b = claim("rb", tag)
                pe.wait_ge(step, value("rstd", tag))
                for tt in range(NT):
                    last = nc.tensor.matmul(b[:, tt * P:(tt + 1) * P],
                                            stat[:, 1, tt:tt + 1].broadcast_to([P, P]), ident[:], start=True,
                                            stop=True)
                full(last, "rb", tag)

            def mods(key):
                for layer, cb in MODS.get(key, ()):
                    if in_attention(("ada", layer, 8 * cb + 7)):
                        pe.wait_ge(sem["ada_sum"], value("ada_sum", 8 * cb + 7))
                    else:
                        pe.wait_ge(sem["ada"], value("ada", layer, 8 * cb + 7))
                    b = claim("mod", layer, cb)
                    for c in range(8):
                        last = nc.tensor.matmul(b[:, c:c + 1], ACC[:, cb % 2, c * P:(c + 1) * P], ones[:, 0:1],
                                                start=True, stop=True)
                    full(last, "mod", layer, cb)

            def project(g):
                tokens(("p1", g), [("p1", g, s) for s in range(4)], 412 if g == 0 else 512, "n1")
                mods(("p1", g, 3))

            def index(qt):
                n = (qt + 1) * P
                for h in range(4):
                    pe.wait_ge(sem["read_act"], value("read_act", "ti", 2))
                    b = claim("idx", qt, h)
                    r = slice(DH * (h % 2), DH * (h % 2) + DH)
                    full(nc.tensor.matmul(b[:, 0:n], QIT[r, h // 2, qt * P:(qt + 1) * P], KIT[r, 0:n],
                                          start=True, stop=True), "idx", qt, h)

            def hidden(kv):
                pe.wait_ge(sem["ca"], value("ca", kv, 15))
                pe.wait_ge(sem["consts"], value("consts", "all"))
                b = claim("hid", kv)
                for i in range(16):
                    slot = ("cw", kv, i // 4)
                    pe.wait_ge(landed[ring(slot)], loads(slot))
                    last = nc.tensor.matmul(b[0:2 * NCMP, 0:CMP_HID], CA[:, i, :],
                                            raw(slot)[:, (i % 4) * CMP_HID:(i % 4 + 1) * CMP_HID],
                                            start=(i == 0), stop=False)
                    if i % 4 == 3:
                        last.then_inc(sem["w_used"], mark("w_used", *slot))
                        used(slot, "w_used")
                full(nc.tensor.matmul(b[0:2 * NCMP, 0:CMP_HID], ones[0:1, 0:2 * NCMP], cb1[0:1, kv, :],
                                      start=False, stop=True), "hid", kv)

            norm("n1", SQS)
            project(0)
            project(1)
            pe.wait_ge(step, value("roped", 0))
            for i in range(3):
                turn(("ti", i), [MISC[:, tt, i * P:(i + 1) * P] for tt in range(NT)])
            project(4)
            index(1)
            pe.wait_ge(sem["read_act"], value("read_act", "p1", 1, 3))
            turn(("tc", 0), [G[1][:, tt, 384:512] for tt in range(NT)])
            project(2)
            index(2)
            hidden(0)
            pe.wait_ge(sem["read_act"], value("read_act", "p1", 4, 3))
            turn(("tc", 1), [G[4][:, tt, 384:512] for tt in range(NT)])
            project(3)
            hidden(1)
            index(3)
            for kv in range(2):
                pe.wait_ge(sem["read_act"], value("read_act", "hid", kv))
                b = claim("ht", kv)
                for c in range(2):
                    last = nc.tensor.transpose(b[:, 64 * c:64 * c + 64], HID[0:64, kv, c * P:(c + 1) * P],
                                               ident[0:64, 0:64])
                full(last, "ht", kv)
            for kv in range(2):
                pe.wait_ge(sem["read_act"], value("read_act", "ht", kv))
                b = claim("co", kv)
                for c in range(2):
                    last = nc.tensor.matmul(b[0:64, 0:DH], HIDT[:, kv, c, :], cw2[:, kv, c, :], start=(c == 0),
                                            stop=(c == 1))
                full(last, "co", kv)
            project(5)
            project(6)
            pe.wait_ge(step, value("roped", 1))
            for i in range(3):
                turn(("tk", i), [G[1][:, tt, i * P:(i + 1) * P] for tt in range(NT)])
            pe.wait_ge(step, value("roped", 2))
            for i in range(4):
                turn(("tqn", i), [G[2][:, tt, i * P:(i + 1) * P] for tt in range(NT)])
            pe.wait_ge(step, value("cmp_key"))
            turn(("tkc",), [CK[0:2 * NCMP, 0, :]], rows=DH)
            pe.wait_ge(step, value("roped", 3))
            for i in range(4):
                turn(("tqd", i), [G[3][:, tt, i * P:(i + 1) * P] for tt in range(NT)])

            nU = len(UNITS1)
            pe.wait_ge(sem["read_dve"], value("read_dve", "tqd", 3))
            pe.wait_ge(step, value("setup"))
            pe.wait_ge(sem["topk"], value("topk", 2))
            pe.wait_ge(sem["pool_set"], value("pool_set", 4))
            pe.wait_ge(sem["read_act"], value("read_act", "tkc"))
            for u in range(nU + O_LAG):
                mods(("att", u))
                qt = cmp_tile(u, 0)
                if qt is not None:
                    for g in range(2):
                        b = claim("cs", qt, g)
                        for j in range(4):
                            last = nc.tensor.matmul(b[:, j * NCMP:(j + 1) * NCMP],
                                                    QNT[DH * g:DH * g + DH, j, qt * P:(qt + 1) * P],
                                                    KCT[DH * g:DH * g + DH, :], start=True, stop=True)
                        full(last, "cs", qt, g)
                qt = cmp_tile(u, CMP_TURN)
                if qt is not None:
                    pe.wait_ge(sem["cmp_p"], value("cmp_p", qt))
                    b = claim("ct", qt)
                    for g in range(2):
                        last = nc.tensor.transpose(
                            b[:, g * P:(g + 1) * P],
                            PC[:, qt % 2, 4 * g:4 * g + 4, :].rearrange("p h c -> p (h c)"), ident[:])
                    full(last, "ct", qt)
                qt = cmp_tile(u, CMP_PV)
                if qt is not None:
                    pe.wait_ge(sem["read_act"], value("read_act", "ct", qt))
                    b = claim("cpv", qt)
                    for g in range(2):
                        last = nc.tensor.matmul(b[:, g * 256:(g + 1) * 256], PTC[:, qt % 2, g * P:(g + 1) * P],
                                                VBLK[:, g, :], start=True, stop=True)
                    full(last, "cpv", qt)
                if u < nU:
                    br, j, g, qt = UNITS1[u]
                    n = (qt + 1) * P
                    b = claim("s", 1, u)
                    nc.tensor.matmul(b[:, 0:n], (QNT if br < 2 else QDT)[:, j, qt * P:(qt + 1) * P],
                                     KT[:, 2 * br + g, 0:n], start=True, stop=False)
                    if br == 2 and qt:
                        if qt == 3:
                            pe.wait_ge(sem["topk"], value("topk", 3))
                        last = nc.tensor.matmul(b[:, 0:n], identb[:], MASKB[:, qt - 1, 0:n], start=False,
                                                stop=True)
                    else:
                        last = nc.tensor.matmul(b[:, n - P:n], identb[:], causal[:], start=False, stop=True)
                    full(last, "s", 1, u)
                v = u - T_LAG
                if 0 <= v < nU:
                    pe.wait_ge(sem["read_act"], value("read_act", "s", 1, v))
                    b = claim("t", 1, v)
                    for kb in range(UNITS1[v][3] + 1):
                        last = nc.tensor.transpose(b[:, kb * P:(kb + 1) * P], PR[:, v % RING, kb * P:(kb + 1) * P],
                                                   ident[:])
                    full(last, "t", 1, v)
                v = u - O_LAG
                if v >= 0:
                    br, j, g, qt = UNITS1[v]
                    pe.wait_ge(sem[evictor(v)], value(evictor(v), "t", 1, v))
                    b = claim("o", 1, v)
                    for kb in range(qt + 1):
                        c = br * P + g * DH
                        last = nc.tensor.matmul(b[:, 0:DH], PT1[:, v % RING, kb * P:(kb + 1) * P],
                                                G[4][:, kb, c:c + DH], start=(kb == 0), stop=(kb == qt))
                    full(last, "o", 1, v)
            pe.wait_ge(sem["gmix"], value("gmix", NT - 1))
            for i in range(KD):
                turn(("tm", i), [MIX[:, tt, i * P:(i + 1) * P] for tt in range(NT)])

            def mix_pair(k):
                if first_use("mix", k):
                    pe.wait_ge(sem["read_dve"], value("read_dve", "tm", k))
                return HH[:, k, :], HL[:, k, :]

            for n in range(KD):
                dense(("o1", n), [(("o1", n), P * k) for k in range(KD)], mix_pair)
                mods(("o1", n))

            for layer in range(LAYERS):
                L = layer
                tag = f"m{L}"
                norm(tag, SQ2)
                h = h_pair(tag)

                def square_tile(kind, n):
                    dense((kind, L, n), [((kind, L, n), P * k) for k in range(KD)], h)

                for q in range(4):
                    if q == 0:
                        dense_pair((("xl", L, 0), ("xl", L, 1)), tag)
                    else:
                        square_tile("xl", 2 * q)
                        square_tile("xl", 2 * q + 1)
                    square_tile("ga", q)
                    slot = ("lg", L, q)
                    pe.wait_ge(sem["passed"], value("passed", *slot))
                    for i in range(4):
                        n, which = 2 * q + i // 2, ("lr", "li")[i % 2]
                        pe.wait_ge(sem["xc_lo"], value("xc_lo", L, n))
                        b = claim(which, L, n)
                        full(mm3(b[:], wpair(slot, P * i, P), (XCH[:, n % 2, :], XCL[:, n % 2, :]), True, True),
                             which, L, n)
                    used(slot)
                for n in range(4, KD):
                    square_tile("ga", n)
                tokens(("kvq", L), [("kvq", L, s) for s in range(4)], 448, tag)
                for n in range(KD):
                    square_tile("gb", n)
                pe.wait_ge(step, value("latents", L))
                for i in (2, 0, 1):
                    turn(("tc2", L, i), [KVR[:, tt, i * P:(i + 1) * P] for tt in range(NT)])
                turn(("tc2", L, 3), [KVR[:, tt, 384:448] for tt in range(NT)], rows=DH)
                slot = ("uv", L)
                pe.wait_ge(sem["passed"], value("passed", *slot))
                pe.wait_ge(sem["read_dve"], value("read_dve", "tc2", L, 2))
                for tt in range(NT):
                    for half in range(2):
                        b = claim("v", L, tt, half)
                        t = slice(tt * P, (tt + 1) * P)
                        full(mm3(b[:], (CKH[:, t], CKL[:, t]), wpair(slot, 512 * half, 512), True, True),
                             "v", L, tt, half)
                used(slot)
                slot = ("uqr", L)
                pe.wait_ge(sem["passed"], value("passed", *slot))
                pe.wait_ge(sem["read_dve"], value("read_dve", "tc2", L, 1))
                for tt in range(NT):
                    b = claim("qr", L, tt)
                    t = slice(tt * P, (tt + 1) * P)
                    for k in range(2):
                        last = mm3(b[:], (CQH[:, k, t], CQL[:, k, t]), wpair(slot, 512 * k, 512), k == 0, k == 1)
                    full(last, "qr", L, tt)
                used(slot)

                def head_qk(hd):
                    slot = ("hd", L, hd // 2)
                    c = 3 * P * (hd % 2)
                    pe.wait_ge(sem["passed"], value("passed", *slot))
                    b = claim("qn", L, hd)
                    for k in range(2):
                        last = mm3(b[:], wpair(slot, c + P * k, P), (CQH[:, k, :], CQL[:, k, :]), k == 0, k == 1)
                    full(last, "qn", L, hd)
                    b = claim("kn", L, hd)
                    full(mm3(b[:], wpair(slot, c + 2 * P, P), (CKH[:], CKL[:]), True, True), "kn", L, hd)
                    used(slot)

                head_qk(0)
                head_qk(1)
                pe.wait_ge(step, value("q_roped", L))
                for i in range(4):
                    turn(("tq", L, i), [QRR[:, tt, i * P:(i + 1) * P] for tt in range(NT)])
                nU = len(UNITS2)
                for u in range(nU + O_LAG):
                    if u < nU:
                        hd, qt = UNITS2[u]
                        n = (qt + 1) * P
                        if u == 0:
                            pe.wait_ge(sem["pool_set"], value("pool_set", "kpe", L))
                            pe.wait_ge(sem["read_act"], value("read_act", "tq", L, 3))
                            pe.wait_ge(sem["read_act"], value("read_act", "tc2", L, 3))
                        pe.wait_ge(sem["read_act"], value("read_act", "qn", L, hd))
                        pe.wait_ge(sem["read_dve"], value("read_dve", "kn", L, hd))
                        b = claim("s", 2 + L, u)
                        nc.tensor.matmul(b[:, 0:n], QN[:, hd % 2, qt * P:(qt + 1) * P], KN[:, hd % 2, 0:n],
                                         start=True, stop=False)
                        nc.tensor.matmul(b[:, 0:n], QRT[:, hd // 2, qt * P:(qt + 1) * P], KPE[:, hd % 2, 0:n],
                                         start=False, stop=False)
                        full(nc.tensor.matmul(b[:, n - P:n], identb[:], causal[:], start=False, stop=True),
                             "s", 2 + L, u)
                    v = u - T_LAG
                    if 0 <= v < nU:
                        pe.wait_ge(sem["p_norm"], value("p_norm", 2 + L, v))
                        b = claim("t", 2 + L, v)
                        for kb in range(UNITS2[v][1] + 1):
                            last = nc.tensor.transpose(b[:, kb * P:(kb + 1) * P],
                                                       P2[:, v % RING, kb * P:(kb + 1) * P], ident[:])
                        full(last, "t", 2 + L, v)
                    if u >= 7 and (u - 7) % 4 == 0:
                        hd = (u - 7) // 4
                        pe.wait_ge(sem["read_act"], value("read_act", "t", 2 + L, 4 * hd + 2))
                        pe.wait_ge(sem["read_dve"], value("read_dve", "t", 2 + L, 4 * hd + 3))
                        b = claim("o", 2 + L, hd)
                        for kb in range(NT):
                            last = nc.tensor.matmul(b[:, kb * P:S], V2[:, kb, hd * P:(hd + 1) * P],
                                                    PT2[:, hd % 2, kb, kb * P:S], start=(kb == 0),
                                                    stop=(kb == NT - 1))
                        full(last, "o", 2 + L, hd)
                    if u < nU:
                        hd, qt = UNITS2[u]
                        if qt == 1 and 1 <= hd < HEADS - 1:
                            head_qk(hd + 1)

                def y_pair(k):
                    if first_use("y", L, k):
                        pe.wait_ge(sem["y_lo"], value("y_lo", L, k))
                    return YH[:, k, :], YL[:, k, :]

                for n in range(KD):
                    dense(("o2", L, n), [(("o2", L, n), P * k) for k in range(KD)], y_pair)
                tag = f"f{L}"
                norm(tag, SQ2)
                h = h_pair(tag)
                for half in range(2):
                    for f in range(half * FH, half * FH + FH):
                        if f == 0:
                            dense_pair((("fg", L, 0), ("fu", L, 0)), tag)
                        else:
                            square_tile("fg", f)
                            square_tile("fu", f)
                        if L == 0:
                            mods(("fu", L, f))

                    def hid_pair(j):
                        if first_use("hid", L, half, j):
                            pe.wait_ge(sem["hid_lo"], value("hid_lo", L, half * FH + j))
                        return HDH[:, j, :], HDL[:, j, :]

                    for n in range(KD):
                        chunks = [(("fo", L, half, (n * FH + j) // 8), P * ((n * FH + j) % 8)) for j in range(FH)]
                        dense(("fo", L, half, n), chunks, hid_pair)
                        if L == 0 and (n == KD - 1 or fo_slot(L, half, n + 1) != fo_slot(L, half, n)):
                            mods(fo_slot(L, half, n))
            norm("fin", SQ2)

    return note


def lay_out(v):
    A = {k: np.asarray(x) for k, x in v.items()}
    f = np.float32

    def tiles(w):
        k, n = w.shape
        return w.reshape(k // P, P, n // P, P).transpose(2, 1, 0, 3)

    def rows(w):
        return w.reshape(4, 2, P, 512).transpose(0, 2, 1, 3)

    slots = {}
    w = A["w_in"][0]
    c = dict(qn=0, kc=512, vc=640, ks=768, vs=896, kw=1024, vw=1152, gl=1280, zn=1304, qd=1816, kd=2328,
             vd=2456, qi=2584, ki=2840, wi=2904, zd=2908)
    r = {k: np.arange(o, o + 128) for k, o in c.items()}
    span = lambda k, n: np.arange(c[k], c[k] + n)
    heads = np.concatenate([np.arange(DH) + DH * (4 * g + j) for j in range(4) for g in range(2)])
    groups = {
        0: np.concatenate([span("qi", 256), span("ki", 64), span("ki", 64), span("gl", 24), span("wi", 4),
                           span("qi", 100)]),
        1: np.concatenate([r["ks"], r["kw"], r["kd"], r["kc"]]),
        2: c["qn"] + heads,
        3: c["qd"] + heads,
        4: np.concatenate([r["vs"], r["vw"], r["vd"], r["vc"]]),
        5: span("zn", 512),
        6: span("zd", 512),
    }
    for g, cols in groups.items():
        for s, x in enumerate(rows(w[:, cols])):
            slots[("p1", g, s)] = x
    for kv, name in enumerate(("cmp_k_w1", "cmp_v_w1")):
        for s, x in enumerate(A[name][0].reshape(4, 4, P, CMP_HID).transpose(0, 2, 1, 3)):
            slots[("cw", kv, s)] = x
    for n, x in enumerate(tiles(A["w_out"][0])):
        slots[("o1", n)] = x
    for L in range(LAYERS):
        w = A["w_in_2"][L]
        for kind, o in (("xl", 0), ("ga", 1472), ("gb", 2496)):
            for n, x in enumerate(tiles(w[:, o:o + D])):
                slots[(kind, L, n)] = x
        for s, x in enumerate(rows(np.concatenate([w[:, 1024:1472], w[:, 1024:1088]], 1))):
            slots[("kvq", L, s)] = x
        lw = np.stack([A["lru_wa_2"][L], A["lru_wx_2"][L]], 1)
        for q in range(4):
            x = lw[2 * q:2 * q + 2].transpose(2, 0, 1, 3).reshape(P, 512)
            slots[("lg", L, q)] = np.concatenate([x, x], 1)
        uq, ukv = A["w_uq_2"][L], A["w_ukv_2"][L]
        slots[("uv", L)] = ukv[:, :, P:].reshape(P, D)
        slots[("uqr", L)] = uq[:, :, P:].reshape(2, P, 512).transpose(1, 0, 2)
        for n in range(4):
            parts = []
            for h in (2 * n, 2 * n + 1):
                parts += [uq[0:P, h, 0:P], uq[P:2 * P, h, 0:P], ukv[:, h, 0:P]]
            slots[("hd", L, n)] = np.concatenate(parts + parts[0:2], 1)
        for n, x in enumerate(tiles(A["w_out_2"][L])):
            slots[("o2", L, n)] = x
        ff = tiles(A["w_ffn_in_2"][L])
        for i in range(FT):
            slots[("fg", L, i)], slots[("fu", L, i)] = ff[i], ff[FT + i]
        fo = A["w_ffn_out_2"][L].reshape(2, FH, P, KD, P).transpose(0, 2, 3, 1, 4).reshape(2, P, FH, 1024)
        for half in range(2):
            for s in range(FH):
                slots[("fo", L, half, s)] = fo[half, :, s]
        ada = A["w_ada_2"][L].reshape(KD, P, 6, 1024)
        for cb in range(6):
            for k in range(KD):
                slots[("ada", L, 8 * cb + k)] = ada[k, :, cb]
    stream = np.stack([slots[k].reshape(P, 1024) for k in STREAM])

    def col(x):
        return x.reshape(-1, P).T

    par = np.stack([np.concatenate([
        col(A["b_ada_2"][L]), A["conv_w_2"][L].reshape(4, KD, P).transpose(2, 1, 0).reshape(P, 32),
        col(A["conv_b_2"][L]), col(A["lru_ba_2"][L].reshape(-1)), col(A["lru_bx_2"][L].reshape(-1)),
        col(A["lru_a_param_2"][L]), col(A["q_norm_g_2"][L]), col(A["kv_norm_g_2"][L])], 1)
        for L in range(LAYERS)], 1)
    vec1 = np.concatenate([col(A["norm_gain"][0]), col(A["final_norm_g_2"]), col(A["c_2"][0])], 1)
    gains = np.stack([A["nsa_q_gain"][0], A["nsa_kc_gain"][0], A["nsa_ks_gain"][0], A["nsa_kw_gain"][0],
                      A["dsa_q_gain"][0], A["dsa_k_gain"][0], np.ones(DH, f)])
    pe2 = np.stack([A[n][0].reshape(16, P).T for n in ("cmp_pe_k", "cmp_pe_v")], 1)
    cw2 = np.stack([A[n][0].reshape(2, P, DH).transpose(1, 0, 2) for n in ("cmp_k_w2", "cmp_v_w2")], 1)
    cb1 = np.stack([A["cmp_k_b1"][0], A["cmp_v_b1"][0]])[None]

    freq = (f(THETA) ** (-np.arange(HALF, dtype=f) / f(HALF))).astype(f)
    ang = np.arange(S, dtype=f)[:, None] * freq
    cs1 = np.stack([np.cos(ang), np.sin(ang)]).astype(f).reshape(2, NT, P, HALF).transpose(2, 0, 1, 3)
    cpos = (np.arange(NCMP) * CMP_STRIDE + CMP_BLOCK - 1).astype(f)
    cang = np.tile(cpos, 2)[:, None] * freq
    cscmp = np.stack([np.cos(cang), np.sin(cang)], 1).astype(f)
    tok = np.arange(S).reshape(NT, P)
    sees = cpos[None, None, :] <= tok[:, :, None]
    cmask = np.where(sees, 0.0, NEG).astype(f).transpose(1, 0, 2)
    i = np.arange(P)
    return {
        "xt": A["x"][0].T.reshape(KD, P, S).transpose(1, 0, 2), "stream": stream, "ones": np.ones((P, P), f),
        "ident": np.eye(P, dtype=f), "causal": np.where(i[None, :] <= i[:, None], 0.0, NEG).astype(f),
        "vec1": vec1, "par": par, "freq": freq[None], "pos": A["positions_2"],
        "pos_tok": A["positions_2"].reshape(NT, P).T, "cs1": cs1, "gains": gains, "pe2": pe2, "cw2": cw2,
        "cb1": cb1, "cscmp": cscmp, "cmask": cmask, "cvalid": sees.any(2).astype(f).T,
    }


def kernel(**inputs):
    import concourse.bacc as bacc
    from concourse.bass_utils import run_bass_kernel_spmd

    arrays = {k: np.ascontiguousarray(x) for k, x in lay_out(inputs).items()}
    known = {}
    for _ in range(2):
        nc = bacc.Bacc("TRN2", target_bir_lowering=False, num_devices=1)
        args = {k: nc.dram_tensor(f"in_{k}", x.shape, mybir.dt.from_np(x.dtype), kind="ExternalInput").ap()
                for k, x in arrays.items()}
        args["out"] = nc.dram_tensor("out_t", (P, KD, S), F32, kind="ExternalOutput").ap()
        known = program(nc, args, known)
    r = run_bass_kernel_spmd(nc, [{f"in_{k}": x for k, x in arrays.items()}], core_ids=[0])
    out = np.asarray(r.results[0]["out_t"])
    return np.ascontiguousarray(out.transpose(1, 0, 2).reshape(D, S).T)[None]
```
